# Optimizing a Trainium2 kernel written in Bass

```python
import math
import jax
import jax.numpy as jnp
from jax import lax
import numpy as np

D_MODEL = 1024
BATCH = 1
SEQ = 128
DEPTH = 2
DEC_BATCH = 1
DEC_SEQ = 256
PAST_LEN = 128

GRID_W = 64
A_HEADS = 4
A_DH = 64
A_DV = 128
B_HEADS = 8
B_DH = 64
NA_ROWS = 8
NA_COLS = 16
C_HEADS = 4
C_DK = 64
C_DV = 128
RET_CHUNK = 128
N_BRANCH = 3
N_EXPERTS = 16
EXPERT_FF = 1024
EC_FACTOR = 2
ROPE_BASE = 10000.0
EPS = 1e-6
Q_BLOCK = 128
NEG_INF = -1e30

A_QK = A_HEADS * 2 * A_DH
A_V = A_HEADS * A_DV
B_W = B_HEADS * B_DH
C_QK = C_HEADS * C_DK
C_V = C_HEADS * C_DV
D_IN = 2 * A_QK + A_V + 3 * B_W + 2 * C_QK + 2 * C_V + N_BRANCH * D_MODEL

kernel_name = 'hybrid_diffusion_trunk_step'

def _rmsnorm(x, g):
    x32 = x.astype(jnp.float32)
    y = x32 * lax.rsqrt(jnp.mean(x32 * x32, axis=-1, keepdims=True) + EPS)
    return y.astype(x.dtype) * g

def _modulation(cvec, w_mod, b_mod):
    m = jnp.einsum('bd,de->be', jax.nn.silu(cvec), w_mod) + b_mod
    return [t[:, None, :] for t in jnp.split(m, 6, axis=-1)]

def _split_projection(h, w_in):
    b, n, _ = h.shape
    sizes = [A_QK, A_QK, A_V, B_W, B_W, B_W, C_QK, C_QK, C_V, C_V]
    offsets = [int(o) for o in np.cumsum(sizes)]
    z = jnp.einsum('bnd,de->bne', h, w_in)
    aq, ak, av, bq, bk, bv, cq, ck, cv, cg, gates = jnp.split(z, offsets, axis=-1)
    return (aq.reshape(b, n, A_HEADS, 2, A_DH), ak.reshape(b, n, A_HEADS, 2, A_DH),
            av.reshape(b, n, A_HEADS, A_DV),
            bq.reshape(b, n, B_HEADS, B_DH), bk.reshape(b, n, B_HEADS, B_DH),
            bv.reshape(b, n, B_HEADS, B_DH),
            cq.reshape(b, n, C_HEADS, C_DK), ck.reshape(b, n, C_HEADS, C_DK) * (C_DK ** -0.5),
            cv.reshape(b, n, C_HEADS, C_DV), cg, gates.reshape(b, n, N_BRANCH, D_MODEL))

def _axial_rope(x, n):
    half = A_DH // 2
    quarter = half // 2
    freqs = ROPE_BASE ** (-jnp.arange(quarter, dtype=jnp.float32) * 2.0 / half)
    t = jnp.arange(n)
    row = (t // GRID_W).astype(jnp.float32)[:, None] * freqs
    col = (t % GRID_W).astype(jnp.float32)[:, None] * freqs
    ang = jnp.concatenate([row, row, col, col], axis=-1)
    shape = (1, n) + (1,) * (x.ndim - 3) + (A_DH,)
    cos = jnp.cos(ang).reshape(shape)
    sin = jnp.sin(ang).reshape(shape)
    x32 = x.astype(jnp.float32)
    a1, a2, b1, b2 = jnp.split(x32, 4, axis=-1)
    rot = jnp.concatenate([-a2, a1, -b2, b1], axis=-1)
    return (x32 * cos + rot * sin).astype(x.dtype)

def _sweep_query_blocks(q, fn):
    b, n = q.shape[:2]
    nb = n // Q_BLOCK
    qb = jnp.moveaxis(q.reshape((b, nb, Q_BLOCK) + q.shape[2:]), 1, 0)
    out = jnp.moveaxis(lax.map(fn, qb), 0, 1)
    return out.reshape((b, n) + out.shape[3:])

def _diff_attention(q, k, v, lam):
    scale = A_DH ** -0.5

    def block(qb):
        s = jnp.einsum('bqhid,bkhid->bhiqk', qb, k).astype(jnp.float32) * scale
        p = jax.nn.softmax(s, axis=-1)
        a = p[:, :, 0] - lam * p[:, :, 1]
        return jnp.einsum('bhqk,bkhe->bqhe', a.astype(v.dtype), v)
    return _sweep_query_blocks(q, block)

def _diff_lambda(lam, lam_init):
    lam = lam.astype(jnp.float32)
    return jnp.exp(jnp.sum(lam[0] * lam[1])) - jnp.exp(jnp.sum(lam[2] * lam[3])) + lam_init

def _diff_output(o, gain, lam_init):
    b, n = o.shape[:2]
    o32 = o.astype(jnp.float32)
    on = o32 * lax.rsqrt(jnp.mean(o32 * o32, axis=-1, keepdims=True) + EPS)
    return (on.reshape(b, n, A_V).astype(o.dtype) * gain) * (1.0 - lam_init)

def _softmax_attention(q, k, v):
    scale = q.shape[-1] ** -0.5

    def block(qb):
        s = jnp.einsum('bqhd,bkhd->bhqk', qb, k).astype(jnp.float32) * scale
        p = jax.nn.softmax(s, axis=-1)
        return jnp.einsum('bhqk,bkhd->bqhd', p.astype(v.dtype), v)
    return _sweep_query_blocks(q, block)

def _neighbourhood_attention(q, k, v, ck, cv, rpb):
    b, n, h, d = q.shape
    rows = n // GRID_W
    kr = min(NA_ROWS, rows)
    kc = NA_COLS
    band = 2 * kc
    ncb = GRID_W // kc
    scale = d ** -0.5
    q_row = jnp.arange(rows)
    key_rows = jnp.clip(q_row - kr // 2, 0, rows - kr)[:, None] + jnp.arange(kr)
    q_col = jnp.arange(ncb)[:, None] * kc + jnp.arange(kc)
    band_start = jnp.clip(jnp.arange(ncb) * kc - kc // 2, 0, GRID_W - band)
    key_cols = band_start[:, None] + jnp.arange(band)
    kidx = (key_rows[:, None, :, None] * GRID_W + key_cols[None, :, None, :]).reshape(rows, ncb, kr * band)
    kg = k[:, kidx]
    vg = v[:, kidx]
    qg = q.reshape(b, rows, ncb, kc, h, d)
    s_win = jnp.einsum('brcqhd,brckhd->bhrcqk', qg, kg).astype(jnp.float32) * scale
    win_start = jnp.clip(q_col - kc // 2, 0, GRID_W - kc)
    col_ok = ((key_cols[:, None, :] >= win_start[..., None])
              & (key_cols[:, None, :] < win_start[..., None] + kc))
    col_ok = jnp.broadcast_to(col_ok[:, :, None, :], (ncb, kc, kr, band)).reshape(ncb, kc, kr * band)
    dr = key_rows - q_row[:, None] + (NA_ROWS - 1)
    dc = jnp.clip(key_cols[:, None, :] - q_col[..., None] + (NA_COLS - 1), 0, 2 * NA_COLS - 2)
    bias = rpb[:, dr[:, None, None, :, None], dc[None, :, :, None, :]].reshape(h, rows, ncb, kc, kr * band)
    s_win = jnp.where(col_ok, s_win + bias[None].astype(jnp.float32), NEG_INF)
    s_ctx = jnp.einsum('brcqhd,blhd->bhrcql', qg, ck).astype(jnp.float32) * scale
    nwin = kr * band
    p = jax.nn.softmax(jnp.concatenate([s_win, s_ctx], axis=-1), axis=-1).astype(v.dtype)
    o = (jnp.einsum('bhrcqk,brckhd->brcqhd', p[..., :nwin], vg)
         + jnp.einsum('bhrcql,blhd->brcqhd', p[..., nwin:], cv))
    return o.reshape(b, n, h, d)

def _retention_scan(q, k, v, log_gamma, s0):
    b, n, h, dk = q.shape
    dv = v.shape[-1]
    t = RET_CHUNK
    nc = n // t
    f32 = jnp.float32

    def chunks(x):
        return jnp.moveaxis(x.astype(f32).reshape((b, nc, t) + x.shape[2:]), 1, 0)
    pos = jnp.arange(t, dtype=f32)
    diff = pos[:, None] - pos[None, :]
    d_in = jnp.where((diff >= 0)[None],
                     jnp.exp(log_gamma[:, None, None] * jnp.maximum(diff, 0.0)[None]), 0.0)
    d_cross = jnp.exp(log_gamma[None, :] * (pos[:, None] + 1.0))[None, :, :, None]
    d_upd = jnp.exp(log_gamma[None, :] * (t - 1.0 - pos[:, None]))[None, :, :, None]
    g_chunk = jnp.exp(log_gamma * t)[None, :, None, None]

    def step(s, inp):
        qb, kb, vb = inp
        att = jnp.einsum('bihd,bjhd->bhij', qb, kb) * d_in[None]
        o = (jnp.einsum('bhij,bjhe->bihe', att, vb)
             + jnp.einsum('bihd,bhde->bihe', qb, s) * d_cross)
        s_new = g_chunk * s + jnp.einsum('bjhd,bjhe->bhde', kb * d_upd, vb)
        return s_new, o
    s_fin, o = lax.scan(step, s0.astype(f32), (chunks(q), chunks(k), chunks(v)))
    return jnp.moveaxis(o, 0, 1).reshape(b, n, h, dv), s_fin

def _bidirectional_retention(q, k, v, log_gamma, s0_fwd, s0_bwd):
    o_f, s_f = _retention_scan(q, k, v, log_gamma[0], s0_fwd)
    o_b, s_b = _retention_scan(jnp.flip(q, 1), jnp.flip(k, 1), jnp.flip(v, 1), log_gamma[1], s0_bwd)
    return o_f + jnp.flip(o_b, 1), s_f, s_b

def _retention_output(o, g, gain):
    b, n = o.shape[:2]
    mu = jnp.mean(o, axis=-1, keepdims=True)
    var = jnp.mean(jnp.square(o - mu), axis=-1, keepdims=True)
    on = ((o - mu) * lax.rsqrt(var + EPS)).reshape(b, n, C_V).astype(g.dtype) * gain
    return jax.nn.silu(g) * on

def _merge(gates, a_o, b_o, c_o, w_pa, w_pb, w_pc, w_o):
    b, n = a_o.shape[:2]
    br = jnp.stack([jnp.einsum('bne,ed->bnd', a_o.reshape(b, n, A_V), w_pa),
                    jnp.einsum('bne,ed->bnd', b_o.reshape(b, n, B_W), w_pb),
                    jnp.einsum('bne,ed->bnd', c_o, w_pc)], axis=2)
    merged = jnp.sum(jax.nn.sigmoid(gates) * br, axis=2)
    return jnp.einsum('bnd,de->bne', merged, w_o)

def _expert_choice_ffn(h, w_router, w_gate, w_up, w_down):
    b, n, d = h.shape
    cap = EC_FACTOR * n // N_EXPERTS
    aff = jax.nn.softmax(jnp.einsum('bnd,de->bne', h, w_router).astype(jnp.float32), axis=-1)
    g, idx = lax.top_k(jnp.swapaxes(aff, 1, 2), cap)
    xg = jax.vmap(lambda hb, ib: hb[ib])(h, idx)
    hid = jax.nn.silu(jnp.einsum('becd,edf->becf', xg, w_gate)) * jnp.einsum('becd,edf->becf', xg, w_up)
    out = jnp.einsum('becf,efd->becd', hid, w_down) * g[..., None].astype(h.dtype)
    return jax.vmap(lambda ob, ib: jnp.zeros((n, d), ob.dtype).at[ib.reshape(-1)].add(ob.reshape(-1, d)))(out, idx)

def setup_inputs(seed: int = 0) -> dict:
    key = jax.random.key(seed)
    ks = iter(jax.random.split(key, 40))
    f32 = jnp.float32

    def nrm(shape, scale):
        return jax.random.normal(next(ks), shape, f32) * scale
    gam = 1.0 - 2.0 ** (-5.0 - np.arange(C_HEADS))
    decay_logit = np.log(gam / (1.0 - gam)).astype(np.float32)
    return {
        'x_prompt': nrm((BATCH, SEQ, D_MODEL), 1.0),
        'x_sample': nrm((DEC_BATCH, DEC_SEQ, D_MODEL), 1.0),
        'cache_a_k': nrm((DEC_BATCH, DEPTH, PAST_LEN, A_HEADS, 2, A_DH), 1.0),
        'cache_a_v': nrm((DEC_BATCH, DEPTH, PAST_LEN, A_HEADS, A_DV), 1.0),
        'cache_b_k': nrm((DEC_BATCH, DEPTH, PAST_LEN, B_HEADS, B_DH), 1.0),
        'cache_b_v': nrm((DEC_BATCH, DEPTH, PAST_LEN, B_HEADS, B_DH), 1.0),
        'state_c_fwd': nrm((DEC_BATCH, DEPTH, C_HEADS, C_DK, C_DV), 0.5),
        'state_c_bwd': nrm((DEC_BATCH, DEPTH, C_HEADS, C_DK, C_DV), 0.5),
        'c': nrm((DEC_BATCH, D_MODEL), 1.0),
        'c_ctx': nrm((D_MODEL,), 1.0),
        'w_mod': nrm((DEPTH, D_MODEL, 6 * D_MODEL), 0.5 * D_MODEL ** -0.5),
        'b_mod': nrm((DEPTH, 6 * D_MODEL), 0.02),
        'norm_mix': 1.0 + nrm((DEPTH, D_MODEL), 0.02),
        'norm_ffn': 1.0 + nrm((DEPTH, D_MODEL), 0.02),
        'w_in': nrm((DEPTH, D_MODEL, D_IN), D_MODEL ** -0.5),
        'diff_lambda': nrm((DEPTH, 4, A_DH), 0.1),
        'diff_norm': 1.0 + nrm((DEPTH, A_V), 0.02),
        'na_rpb': nrm((DEPTH, B_HEADS, 2 * NA_ROWS - 1, 2 * NA_COLS - 1), 0.1),
        'ret_decay': jnp.asarray(decay_logit)[None, None, :] + nrm((DEPTH, 2, C_HEADS), 0.1),
        'ret_norm': 1.0 + nrm((DEPTH, C_V), 0.02),
        'w_proj_a': nrm((DEPTH, A_V, D_MODEL), A_V ** -0.5),
        'w_proj_b': nrm((DEPTH, B_W, D_MODEL), B_W ** -0.5),
        'w_proj_c': nrm((DEPTH, C_V, D_MODEL), C_V ** -0.5),
        'w_out': nrm((DEPTH, D_MODEL, D_MODEL), D_MODEL ** -0.5),
        'w_router': nrm((DEPTH, D_MODEL, N_EXPERTS), D_MODEL ** -0.5),
        'w_exp_gate': nrm((DEPTH, N_EXPERTS, D_MODEL, EXPERT_FF), D_MODEL ** -0.5),
        'w_exp_up': nrm((DEPTH, N_EXPERTS, D_MODEL, EXPERT_FF), D_MODEL ** -0.5),
        'w_exp_down': nrm((DEPTH, N_EXPERTS, EXPERT_FF, D_MODEL), EXPERT_FF ** -0.5),
        'norm_final': 1.0 + nrm((D_MODEL,), 0.02),
    }

def reference(x_prompt, x_sample, cache_a_k, cache_a_v, cache_b_k, cache_b_v, state_c_fwd, state_c_bwd,
              c, c_ctx, w_mod, b_mod, norm_mix, norm_ffn, w_in, diff_lambda, diff_norm, na_rpb,
              ret_decay, ret_norm, w_proj_a, w_proj_b, w_proj_c, w_out, w_router, w_exp_gate,
              w_exp_up, w_exp_down, norm_final):
    xc = x_prompt
    xl = x_sample
    n_lat = xl.shape[1]
    new_ak, new_av, new_bk, new_bv, new_sf, new_sb = [], [], [], [], [], []
    for l in range(DEPTH):
        lam_init = 0.8 - 0.6 * math.exp(-0.3 * l)
        log_gamma = jax.nn.log_sigmoid(ret_decay[l].astype(jnp.float32))
        lam = _diff_lambda(diff_lambda[l], lam_init)
        mc = _modulation(c_ctx[None], w_mod[l], b_mod[l])
        ml = _modulation(c, w_mod[l], b_mod[l])

        h = _rmsnorm(xc, norm_mix[l]) * (1.0 + mc[1]) + mc[0]
        aq, ak, av, bq, bk, bv, cq, ck, cv, cg, gates = _split_projection(h, w_in[l])
        a_o = _diff_output(_diff_attention(aq, ak, av, lam), diff_norm[l], lam_init)
        b_o = _softmax_attention(bq, bk, bv)
        zero_state = jnp.zeros((xc.shape[0], C_HEADS, C_DK, C_DV), jnp.float32)
        c_raw, s_f, s_b = _bidirectional_retention(cq, ck, cv, log_gamma, zero_state, zero_state)
        c_o = _retention_output(c_raw, cg, ret_norm[l])
        xc = xc + mc[2] * _merge(gates, a_o, b_o, c_o, w_proj_a[l], w_proj_b[l], w_proj_c[l], w_out[l])
        h = _rmsnorm(xc, norm_ffn[l]) * (1.0 + mc[4]) + mc[3]
        xc = xc + mc[5] * _expert_choice_ffn(h, w_router[l], w_exp_gate[l], w_exp_up[l], w_exp_down[l])
        new_ak.append(ak)
        new_av.append(av)
        new_bk.append(bk)
        new_bv.append(bv)
        new_sf.append(s_f.astype(xc.dtype))
        new_sb.append(s_b.astype(xc.dtype))

        h = _rmsnorm(xl, norm_mix[l]) * (1.0 + ml[1]) + ml[0]
        aq, ak, av, bq, bk, bv, cq, ck, cv, cg, gates = _split_projection(h, w_in[l])
        aq = _axial_rope(aq, n_lat)
        ak = _axial_rope(ak, n_lat)
        k_all = jnp.concatenate([ak, cache_a_k[:, l].astype(ak.dtype)], axis=1)
        v_all = jnp.concatenate([av, cache_a_v[:, l].astype(av.dtype)], axis=1)
        a_o = _diff_output(_diff_attention(aq, k_all, v_all, lam), diff_norm[l], lam_init)
        b_o = _neighbourhood_attention(bq, bk, bv, cache_b_k[:, l].astype(bq.dtype),
                                       cache_b_v[:, l].astype(bv.dtype), na_rpb[l])
        c_raw, _, _ = _bidirectional_retention(cq, ck, cv, log_gamma, state_c_fwd[:, l], state_c_bwd[:, l])
        c_o = _retention_output(c_raw, cg, ret_norm[l])
        xl = xl + ml[2] * _merge(gates, a_o, b_o, c_o, w_proj_a[l], w_proj_b[l], w_proj_c[l], w_out[l])
        h = _rmsnorm(xl, norm_ffn[l]) * (1.0 + ml[4]) + ml[3]
        xl = xl + ml[5] * _expert_choice_ffn(h, w_router[l], w_exp_gate[l], w_exp_up[l], w_exp_down[l])

    y_prompt = _rmsnorm(xc, norm_final)
    y_sample = _rmsnorm(xl, norm_final)
    return (y_prompt, y_sample, jnp.stack(new_ak, axis=1), jnp.stack(new_av, axis=1),
            jnp.stack(new_bk, axis=1), jnp.stack(new_bv, axis=1),
            jnp.stack(new_sf, axis=1), jnp.stack(new_sb, axis=1))


_drawn_inputs = setup_inputs


def setup_inputs(seed=0):
    import zlib

    import numpy as np

    out = dict(_drawn_inputs(seed))
    spreads = {}
    factors = {'cache_b_k': 2.729,
     'state_c_fwd': 2.684,
     'state_c_bwd': 2.687,
     'norm_ffn': 6.174,
     'diff_lambda': 8.0,
     'diff_norm': 8.0,
     'na_rpb': 8.0,
     'ret_norm': 8.0,
     'norm_final': 2.74}
    for name, (base, spread) in spreads.items():
        noise = np.random.default_rng([zlib.crc32(name.encode()), seed]).standard_normal(out[name].shape)
        drawn = base * np.exp(spread * noise) if base else spread * noise
        out[name] = jnp.asarray(drawn.astype(out[name].dtype))
    for name, factor in factors.items():
        out[name] = (out[name] * factor).astype(out[name].dtype)
    return out
```

```python
import math
from contextlib import ExitStack

import numpy as np

import concourse.bass as bass
from concourse import mybir

F32 = mybir.dt.float32
ALU = mybir.AluOpType
ACT = mybir.ActivationFunctionType
AX_X = mybir.AxisListType.X

P = 128
D = 1024
KD = D // P
NBLK = 3
T = NBLK * P
CTX = slice(0, P)
LAT = slice(P, T)
DEPTH = 2
GRID_W = 64
HEADS_A = 4
HEADS_B = 8
HEADS_C = 4
RPB_ROWS, RPB_COLS = 15, 31
NE = 16
CAP_CTX = 2 * P // NE
CAP_LAT = 2 * (T - P) // NE
SLOTS = CAP_CTX + CAP_LAT
EPS = 1e-6
SCALE = 64 ** -0.5
NEG = -1e30

SLAB = 512
RING = 4
DENSE_SLABS = 32
EXPERT_SLABS = 6

CONST_AT = {}
_at = 0
for _name, _width in (("ident", P), ("rot", P), ("ones", P), ("cos", 2 * P), ("sin", 2 * P),
                      ("below", P), ("above", P), ("is_below", P), ("is_above", P),
                      ("since", P), ("until", P), ("k_until", 1), ("k_since", 1), ("eps", 1), ("one", 1),
                      ("slot", SLOTS), ("window", GRID_W)):
    CONST_AT[_name] = (_at, _at + _width)
    _at += _width
CONST_COLS = _at


def shape_constants():
    t = np.zeros((P, CONST_COLS), np.float32)

    def put(name, value):
        a, b = CONST_AT[name]
        t[:, a:b] = value

    p = np.arange(P)[:, None].astype(np.float32)
    i = np.arange(P)[None, :].astype(np.float32)
    put("ident", np.eye(P))
    rot = np.zeros((P, P), np.float32)
    for m in range(P):
        if m % 32 < 16:
            rot[m + 16, m] = -1.0
        else:
            rot[m - 16, m] = 1.0
    put("rot", rot)
    put("ones", 1.0)
    quarter = 16
    freqs = (np.float32(10000.0) ** (-np.arange(quarter, dtype=np.float32) * np.float32(2.0) / np.float32(32))).astype(np.float32)
    tok = np.arange(2 * P)
    row = (tok // GRID_W).astype(np.float32)[:, None] * freqs
    col = (tok % GRID_W).astype(np.float32)[:, None] * freqs
    ang = np.concatenate([row, row, col, col], axis=-1).T
    ang = np.concatenate([ang, ang], axis=0)
    put("cos", np.cos(ang))
    put("sin", np.sin(ang))
    put("below", np.maximum(i - p, 0))
    put("above", np.maximum(p - i, 0))
    put("is_below", (i >= p).astype(np.float32))
    put("is_above", (p >= i).astype(np.float32))
    put("since", i + 1)
    put("until", P - i)
    put("k_until", P - 1 - p)
    put("k_since", p)
    put("eps", EPS)
    put("one", 1.0)
    put("slot", np.arange(1, SLOTS + 1)[None, :])
    qc = np.arange(P)[:, None] % GRID_W
    kc = GRID_W - 1 - np.arange(GRID_W)[None, :]
    start = np.clip(qc - 8, 0, GRID_W - 16)
    put("window", np.where((kc >= start) & (kc < start + 16), 0.0, NEG))
    layer = np.zeros((DEPTH, P, 2), np.float32)
    for l in range(DEPTH):
        lam_init = 0.8 - 0.6 * math.exp(-0.3 * l)
        layer[l, :, 0] = lam_init
        layer[l, :, 1] = 1.0 - lam_init
    return t, layer


def build(nc, x_rows, cvec, cache_a_k, cache_a_v, cache_b_k, cache_b_v, state_f, state_b, w_mod, b_mod,
          norm_mix, norm_ffn, w_in, diff_lambda, diff_norm, rpb_rev, ret_decay, ret_norm, w_pa, w_pb, w_pc,
          w_out, w_router, w_gate, w_up, w_down, norm_final, const_in, layer_in,
          y_out, new_ak, new_av, new_bk, new_bv, new_sf, new_sb):
    ctx = ExitStack()
    sems = []

    def sb(name, shape):
        return ctx.enter_context(nc.sbuf_tensor(name, shape, F32))

    def sem(name):
        s = ctx.enter_context(nc.semaphore(name))
        sems.append(s)
        return s

    with ctx:
        ring = sb("ring", [P, RING, KD, SLAB])
        xT = sb("xT", [P, KD, T])
        hT = sb("hT", [P, KD, T])
        const = sb("const", [P, CONST_COLS])
        dense = sb("dense", [P, 13824])
        silu_c = sb("silu_c", [P, KD, 2])
        modT = sb("modT", [P, 48, 2])
        scale_mix = sb("scale_mix", [P, KD, 2])
        scale_ffn = sb("scale_ffn", [P, KD, 2])
        vec_rows = sb("vec_rows", [72, P])
        vecT = sb("vecT", [P, 72])
        square = sb("square", [P, 2, T])
        rs = sb("rs", [P, T])
        tmp = sb("tmp", [P, 2, T])
        merged = sb("merged", [P, KD, T])
        bias0 = sb("bias0", [P, HEADS_B * 4, GRID_W])
        probs = sb("probs", [P, 2, 2, T])
        probsT = sb("probsT", [P, 2, 2, T])
        akcT = sb("akcT", [P, 4, P])
        bkcT = sb("bkcT", [P, 4, P])
        small = sb("small", [P, 2, 8])
        lam_rows = sb("lam_rows", [P, 4, 64])
        lamb = sb("lamb", [P, 8])
        layer_c = sb("layer_c", [P, 2])
        gain_a = sb("gain_a", [P, 4])
        decay = sb("decay", [P, 8])
        decay_t = sb("decay_t", [P, 4, 8])
        in_decay = sb("in_decay", [P, 4, P])
        bwd_decay = sb("bwd_decay", [P, 4, P])
        q_decay = sb("q_decay", [P, 2, 2, P])
        k_decay = sb("k_decay", [P, 2, 4])
        chunk_decay = sb("chunk_decay", [P, 2, 2])
        state0 = sb("state0", [P, 2, 2, P])
        state1 = sb("state1", [P, 2, 2, P])
        ctx_state = sb("ctx_state", [P, 2, 2, P])
        w_r = sb("w_r", [P, KD, NE])
        keys_out = bwd_decay[:].rearrange("p h t -> p (h t)")

        def c_(name):
            a, b = CONST_AT[name]
            return const[:, a:b]

        ident = c_("ident")
        ones = c_("ones")

        zT = dense[:, 0:24 * T].rearrange("p (c t) -> p c t", t=T)
        AQ, AK, BQ, BK, CQ, CK, CG = 0, 4, 8, 12, 16, 18, 20
        v_rows = dense[:, 24 * T:24 * T + 9 * SLAB].rearrange("p (m b e) -> p m b e", m=3, b=NBLK)
        assert 24 * T + 9 * SLAB == 13824
        av_c = merged[:].rearrange("p k t -> p (k t)")[:, 0:SLAB]
        bv_c = merged[:].rearrange("p k t -> p (k t)")[:, SLAB:2 * SLAB]
        akc_rows = probs[:].rearrange("p a b t -> p (a b t)")[:, 0:SLAB]
        bkc_rows = probs[:].rearrange("p a b t -> p (a b t)")[:, SLAB:2 * SLAB]
        bias1 = merged[:].rearrange("p k t -> p (k t)")[:, 2 * SLAB:6 * SLAB].rearrange("p (r c) -> p r c", c=GRID_W)
        bias = [bias0, bias1]
        q_dec = probs[:].rearrange("p a b t -> p (a b t)")[:, 0:1024].rearrange("p (d c t) -> p d c t", d=2, c=2)
        k_dec = probsT[:].rearrange("p a b t -> p (a b t)")[:, 0:1024].rearrange("p (n e) -> p n e", n=4)
        att = tmp
        gate_e = [x[:].rearrange("p a b t -> p (a b t)")[:, 1024:1024 + T] for x in (probs, probsT)]
        a_free = v_rows[:, 0].rearrange("p b e -> p (b e)")
        c_raw = a_free[:, 0:2 * T].rearrange("p (u t) -> p u t", u=2)
        c_rs = a_free[:, 2 * T:4 * T].rearrange("p (u t) -> p u t", u=2)
        cg_sig = v_rows[:, 1].rearrange("p b e -> p (b e)")[:, 0:4 * T]
        h_rows = dense[:, 0:3072].rearrange("p (b d) -> p b d", b=NBLK)
        acc = dense[:, 3072:6144].rearrange("p (k t) -> p k t", k=KD)
        at = 6144

        def carve(n):
            nonlocal at
            at += n
            return dense[:, at - n:at]

        pick = carve(2 * NBLK * SLOTS).rearrange("p (u b s) -> p u b s", u=2, b=NBLK)
        pick_g = carve(2 * NBLK * SLOTS).rearrange("p (u b s) -> p u b s", u=2, b=NBLK)
        pick_gT = carve(T)
        xgT = carve(KD * SLOTS).rearrange("p (k s) -> p k s", k=KD)
        act = carve(KD * SLOTS).rearrange("p (k s) -> p k s", k=KD)
        hid = carve(KD * SLOTS).rearrange("p (k s) -> p k s", k=KD)
        outT = carve(KD * SLOTS).rearrange("p (k s) -> p k s", k=KD)
        out_rows = carve(D)
        aff = carve(NBLK * NE).rearrange("p (b e) -> p b e", b=NBLK)
        slot_of = carve(NBLK * NE).rearrange("p (b e) -> p b e", b=NBLK)
        affT = carve(T)
        left = carve(T)
        chosen = carve(T)
        place = carve(T)
        best = carve(8)
        assert at <= 13824

        psum = ctx.enter_context(nc.psum_tensor("psum", [P, 8, SLAB], F32))
        Z = [0, 1]
        S = [2, 3]
        TR = [4, 7]
        O = [5, 6]

        slab_in = [sem(f"slab_in{i}") for i in range(RING)]
        rows_in = sem("rows_in")
        small_in = sem("small_in")
        cache_in = sem("cache_in")
        state_in = sem("state_in")
        bias_in = sem("bias_in")
        stored = sem("stored")
        act_link = sem("act_link")
        dve_link = sem("dve_link")
        pool_link = sem("pool_link")
        x_tr = sem("x_tr")
        x_ev = sem("x_ev")
        c_ready = sem("c_ready")
        vec_tr = sem("vec_tr")
        vec_ready = sem("vec_ready")
        lam_sum = sem("lam_sum")
        lam_exp = sem("lam_exp")
        lam_ready = sem("lam_ready")
        abs_ready = sem("abs_ready")
        ln_ready = sem("ln_ready")
        decay_ready = sem("decay_ready")
        decay_exp = sem("decay_exp")
        in_decay_ready = sem("in_decay_ready")
        chunk_ready = sem("chunk_ready")
        sq_ready = sem("sq_ready")
        sq_used = sem("sq_used")
        rs_ready = sem("rs_ready")
        mod1_ready = sem("mod1_ready")
        norm_mul = sem("norm_mul")
        h_ready = sem("h_ready")
        z_full = sem("z_full")
        z_read = sem("z_read")
        rot_full = sem("rot_full")
        rope_done = sem("rope_done")
        kc_tr = sem("kc_tr")
        kc_ev = sem("kc_ev")
        ko_tr = sem("ko_tr")
        ko_ev = sem("ko_ev")
        ko_st = sem("ko_st")
        bias_ready = sem("bias_ready")
        s_full = sem("s_full")
        s_max = sem("s_max")
        s_exp = sem("s_exp")
        p_ready = sem("p_ready")
        pT_full = sem("pT_full")
        pT_act = sem("pT_act")
        pT_dve = sem("pT_dve")
        o_full = sem("o_full")
        o_read = sem("o_read")
        nsum = sem("nsum")
        nrs = sem("nrs")
        a_done = sem("a_done")
        kr_tr = sem("kr_tr")
        kr_ev = sem("kr_ev")
        qd_ready = sem("qd_ready")
        st_full = sem("st_full")
        st_ev = sem("st_ev")
        st1_ready = sem("st1_ready")
        att_full = sem("att_full")
        att_ready = sem("att_ready")
        co_full = sem("co_full")
        co_read = sem("co_read")
        cmean_full = sem("cmean_full")
        ccen = sem("ccen")
        csq = sem("csq")
        cvar_full = sem("cvar_full")
        crs = sem("crs")
        cgate = sem("cgate")
        c_done = sem("c_done")
        gate_full = sem("gate_full")
        gate_exp = sem("gate_exp")
        br_full = sem("br_full")
        br_read = sem("br_read")
        mod2_ready = sem("mod2_ready")
        w_full = sem("w_full")
        w_read = sem("w_read")
        lg_full = sem("lg_full")
        lg_max = sem("lg_max")
        lg_exp = sem("lg_exp")
        aff_ready = sem("aff_ready")
        affT_full = sem("affT_full")
        slots_ready = sem("slots_ready")
        slots_tr = sem("slots_tr")
        slots_ev = sem("slots_ev")
        hr_tr = sem("hr_tr")
        hr_ev = sem("hr_ev")
        v_stored = sem("v_stored")
        acc_zero = sem("acc_zero")
        a_sq = sem("a_sq")
        crs_read = sem("crs_read")
        cg_exp = sem("cg_exp")
        pick_ready = sem("pick_ready")
        g_full = sem("g_full")
        g_read = sem("g_read")
        pgT_full = sem("pgT_full")
        pgT_read = sem("pgT_read")
        gate_h = sem("gate_h")
        up_h = sem("up_h")
        silu_ready = sem("silu_ready")
        hid_ready = sem("hid_ready")
        down_full = sem("down_full")
        down_read = sem("down_read")
        or_tr = sem("or_tr")
        or_read = sem("or_read")
        sc_full = sem("sc_full")
        sc_read = sem("sc_read")
        e_link = sem("e_link")

        V, A_, G, M = nc.vector, nc.scalar, nc.gpsimd, nc.tensor

        def chain(eng, s):
            n = 0

            def then(ins):
                nonlocal n
                n += 1
                ins.then_inc(s, 1)
                eng.wait_ge(s, n)
            return then

        def clear_all():
            with nc.Block() as block:
                @block.sync
                def _(sp):
                    for s in sems:
                        sp.sem_clear(s)

        def transpose(out, in_):
            n = in_.shape[0]
            return M.matmul(out, in_, ident[0:n, 0:n], start=True, stop=True, is_transpose=True)

        x_in = hT[:].rearrange("p k t -> p (k t)").rearrange("p (b d) -> p b d", b=NBLK)
        with nc.Block() as block:
            @block.sync
            def _(sp):
                sp.dma_start(const[:], const_in).then_inc(rows_in, 16)
                sp.dma_start(x_in, x_rows.rearrange("(b p) d -> p b d", p=P)).then_inc(rows_in, 16)
                sp.dma_start(vec_rows[0:2 * KD, :], cvec.rearrange("g (k p) -> (g k) p", p=P)).then_inc(rows_in, 16)

            @block.tensor
            def _(pe):
                pe.wait_ge(rows_in, 48)
                for k in range(KD):
                    if k >= 4:
                        pe.wait_ge(x_ev, k - 3)
                    for b in range(NBLK):
                        last = transpose(psum[:, k % 4, b * P:(b + 1) * P], x_in[:, b, k * P:(k + 1) * P])
                    last.then_inc(x_tr, 1)
                transpose(psum[:, 4, 0:2 * KD], vec_rows[0:2 * KD, :]).then_inc(vec_tr, 1)

            @block.vector
            def _(dve):
                for k in range(KD):
                    dve.wait_ge(x_tr, k + 1)
                    V.tensor_copy(xT[:, k, :], psum[:, k % 4, 0:T]).then_inc(x_ev, 1)

            @block.scalar
            def _(sc):
                sc.wait_ge(vec_tr, 1)
                A_.activation(silu_c[:].rearrange("p k g -> p g k"),
                              psum[:, 4, 0:2 * KD].rearrange("p (g k) -> p g k", g=2), ACT.Silu).then_inc(c_ready, 1)
        clear_all()

        with nc.Fori(0, DEPTH) as layer:
            with nc.Block() as block:
                def f_of_z(g):
                    return 4 + g if g < 25 else (30 + 2 * (g - 25) if g < 29 else 37 + g - 29)

                def f_of_mod(j):
                    return j if j < 4 else 41 + j - 4

                FILLERS = 49
                Z_GROUPS = ([(0, j, "T") for j in range(4)] + [(1, j, "T") for j in range(4)]
                            + [(2, j, "rows") for j in range(NBLK)]
                            + [(3, j, "T") for j in range(4)] + [(4, j, "T") for j in range(4)]
                            + [(5, j, "rows") for j in range(NBLK)]
                            + [(6, j, "T") for j in range(4)] + [(7, j, "rows") for j in range(NBLK)]
                            + [(8, j, "T") for j in range(4)])
                UNITS = 12
                A_STEPS = UNITS + 2

                def slab_source(n):
                    def cols(w, j):
                        return w[layer].rearrange("(k p) n -> p k n", p=P)[:, :, j * SLAB:(j + 1) * SLAB]
                    if n < 4:
                        return cols(w_mod, n)
                    if n < 13:
                        return cols(w_in, n - 4)
                    if n < 21:
                        return cols(w_mod, n - 9)
                    if n < 30:
                        branch, which = divmod(n - 21, 3)
                        if which == 1:
                            return [w_pa, w_pb, w_pc][branch][layer].rearrange("(k p) n -> p k n", p=P)
                        return cols(w_in, 9 + 2 * branch + which // 2)
                    return cols(w_out, n - 30)

                def slab_into(n):
                    if 21 <= n < 30 and (n - 21) % 3 == 1:
                        return ring[:, n % RING].rearrange("p k n -> p (k n)").rearrange("p (k n) -> p k n", k=4)
                    return ring[:, n % RING]

                def wait_slab_free(eng, n):
                    if n < 4:
                        eng.wait_ge(z_full, f_of_mod(n) + 1)
                    elif n < 13:
                        last_group = max(g for g, (slab, _, _) in enumerate(Z_GROUPS) if slab == n - 4)
                        eng.wait_ge(z_full, f_of_z(last_group) + 1)
                    elif n < 21:
                        eng.wait_ge(z_full, f_of_mod(n - 9) + 1)
                    elif n < 30:
                        branch, which = divmod(n - 21, 3)
                        if which == 1:
                            eng.wait_ge(br_full, KD * (branch + 1))
                        else:
                            eng.wait_ge(gate_full, KD * branch + (4 if which == 0 else 8))
                    else:
                        eng.wait_ge(w_full, 4 * (n - 29))

                @block.sync
                def _(sp):
                    for n in range(DENSE_SLABS):
                        if n >= RING:
                            wait_slab_free(sp, n - RING)
                        sp.dma_start(slab_into(n), slab_source(n)).then_inc(slab_in[n % RING], 16)

                    def load(pair, j):
                        e, s = divmod(j, EXPERT_SLABS)
                        w = (w_gate, w_up, w_down)[s // 2]
                        sp.dma_start(ring[:, j % RING],
                                     w[layer, pair * 2 + e].rearrange("(k p) n -> p k n", p=P)[:, :, (s % 2) * SLAB:(s % 2 + 1) * SLAB]
                                     ).then_inc(slab_in[j % RING], 16)

                    def wait_free(pair, j):
                        e, s = divmod(j, EXPERT_SLABS)
                        sp.wait_ge((gate_h, up_h, down_full)[s // 2], pair * 4 + (2 * e + s % 2 + 1))

                    for j in range(RING):
                        wait_slab_free(sp, DENSE_SLABS - RING + j)
                        load(0, j)
                    with sp.Fori(0, NE // 2 - 1) as pair:
                        for j in range(RING, 2 * EXPERT_SLABS + RING):
                            wait_free(pair, j - RING)
                            if j < 2 * EXPERT_SLABS:
                                load(pair, j)
                            else:
                                load(pair + 1, j - 2 * EXPERT_SLABS)
                    for j in range(RING, 2 * EXPERT_SLABS):
                        wait_free(NE // 2 - 1, j - RING)
                        load(NE // 2 - 1, j)

                @block.gpsimd
                def _(pool):
                    link = chain(pool, pool_link)
                    pool.wait_ge(decay_exp, 1)
                    four = [P, 4, P]
                    link(G.tensor_tensor(in_decay[:], in_decay[:], c_("is_below").unsqueeze(1).to_broadcast(four), ALU.mult))
                    link(G.tensor_tensor(bwd_decay[:], bwd_decay[:], c_("is_above").unsqueeze(1).to_broadcast(four), ALU.mult))
                    G.tensor_tensor(in_decay[:], in_decay[:], bwd_decay[:], ALU.add).then_inc(in_decay_ready, 1)
                    pool.wait_ge(bias_in, 64)
                    for b in bias:
                        v = b if b is bias1 else b[:]
                        G.tensor_tensor(v, v, c_("window").unsqueeze(1).to_broadcast([P, 32, GRID_W]), ALU.add).then_inc(bias_ready, 1)
                    pool.wait_ge(w_full, KD)
                    G.memset(acc, 0.0).then_inc(acc_zero, 1)

                @block.tensor
                def _(pe):
                    def slab_here(n):
                        pe.wait_ge(slab_in[n % RING], 16 * (n // RING + 1))

                    def bank_free(f):
                        if f >= 2:
                            pe.wait_ge(z_read, f - 1)
                        return Z[f % 2]

                    def norm_sum(bank, first):
                        for k in range(KD):
                            pe.wait_ge(sq_ready, first + k + 1)
                            M.matmul(psum[:, bank, 0:T], ones, square[:, k % 2, :], start=k == 0, stop=k == KD - 1).then_inc(sq_used, 1)

                    def mod_slab(j):
                        n = j if j < 4 else j + 9
                        f = f_of_mod(j)
                        slab_here(n)
                        bank = bank_free(f)
                        for q in range(4):
                            for k in range(KD):
                                last = M.matmul(psum[:, bank, 2 * q:2 * q + 2], ring[:, n % RING, k, q * P:(q + 1) * P],
                                                silu_c[:, k, :], start=k == 0, stop=k == KD - 1)
                        last.then_inc(z_full, 1)

                    def z_group(g):
                        slab, j, kind = Z_GROUPS[g]
                        n = 4 + slab
                        f = f_of_z(g)
                        if j == 0:
                            slab_here(n)
                        bank = bank_free(f)
                        cols = slice(j * P, (j + 1) * P)
                        for k in range(KD):
                            if kind == "T":
                                last = M.matmul(psum[:, bank, 0:T], ring[:, n % RING, k, cols], hT[:, k, :], start=k == 0, stop=k == KD - 1)
                            else:
                                last = M.matmul(psum[:, bank, :], hT[:, k, cols], ring[:, n % RING, k, :], start=k == 0, stop=k == KD - 1)
                        last.then_inc(z_full, 1)

                    norm_sum(S[0], 0)
                    pe.wait_ge(small_in, 16 * 9)
                    transpose(psum[:, TR[1], 0:72], vec_rows[:, :]).then_inc(vec_tr, 1)
                    pe.wait_ge(cache_in, 64)
                    for rows, bank in ((akc_rows, O[0]), (bkc_rows, O[1])):
                        for c in range(4):
                            last = transpose(psum[:, bank, c * P:(c + 1) * P], rows[:, c * P:(c + 1) * P])
                        last.then_inc(kc_tr, 1)
                    for j in range(4):
                        mod_slab(j)
                    pe.wait_ge(h_ready, KD)
                    for g in range(11):
                        z_group(g)

                    for c in range(8):
                        pe.wait_ge(z_read, f_of_z(c) + 1)
                        if c >= 2:
                            pe.wait_ge(rope_done, c - 1)
                        M.matmul(psum[:, S[c % 2], 0:2 * P], c_("rot"), zT[:, AQ + c, LAT], start=True, stop=True).then_inc(rot_full, 1)

                    def keys_in_rows(first, bank):
                        for c in range(4):
                            last = transpose(psum[:, bank, c * P:(c + 1) * P], zT[:, first + c, CTX])
                        last.then_inc(ko_tr, 1)

                    keys_in_rows(AK, TR[0])
                    pe.wait_ge(rope_done, 8)
                    pe.wait_ge(kc_ev, 2)

                    def scores(n):
                        mixer, u = divmod(n, UNITS)
                        c, b = divmod(u, NBLK)
                        q0, k0 = ((AQ, AK), (BQ, BK))[mixer]
                        kcT = (akcT, bkcT)[mixer]
                        if n >= 1:
                            pe.wait_ge(s_exp, n)
                        for i in range(2):
                            part = slice(64 * i, 64 * i + 64)
                            q = zT[part, q0 + c, b * P:(b + 1) * P]
                            if b == 0:
                                last = M.matmul(psum[:, S[i], 0:P], q, zT[part, k0 + c, CTX], start=True, stop=True)
                            else:
                                M.matmul(psum[:, S[i], 0:2 * P], q, zT[part, k0 + c, LAT], start=True, stop=True)
                                last = M.matmul(psum[:, S[i], 2 * P:T], q, kcT[part, c, :], start=True, stop=True)
                        last.then_inc(s_full, 1)

                    def probs_transposed(n):
                        mixer, u = divmod(n, UNITS)
                        tiles = 1 if u % NBLK == 0 else 3
                        pe.wait_ge(p_ready, n + 1)
                        if n == 0:
                            pe.wait_ge(ko_ev, 1)
                        else:
                            pe.wait_ge(pT_act, n)
                        if n > UNITS:
                            pe.wait_ge(pT_dve, n - UNITS)
                        for i in range(1 + mixer):
                            for m in range(tiles):
                                last = transpose(psum[:, TR[i], m * P:(m + 1) * P], probs[:, n % 2, i, m * P:(m + 1) * P])
                        last.then_inc(pT_full, 1)

                    def values(n):
                        mixer, u = divmod(n, UNITS)
                        c, b = divmod(u, NBLK)
                        head = 4 * mixer + c
                        pe.wait_ge(pT_act, n + 1)
                        if mixer:
                            pe.wait_ge(pT_dve, n + 1 - UNITS)
                        if b == 0 and head >= 2:
                            pe.wait_ge(o_read, head - 1)
                        elif n == 0:
                            pe.wait_ge(kc_ev, 2)
                        cached = (av_c, bv_c)[mixer]
                        tiles = [(v_rows[:, mixer, 0], 0)] if b == 0 else [
                            (v_rows[:, mixer, 1], 0), (v_rows[:, mixer, 2], 1), (cached, 2)]
                        out = psum[:, O[head % 2], b * P:(b + 1) * P]
                        for v, m in tiles:
                            keys = slice(m * P, (m + 1) * P)
                            if mixer == 0:
                                last = M.matmul(out, v[:, c * P:(c + 1) * P], probsT[:, n % 2, 0, keys], start=m == 0, stop=m == len(tiles) - 1)
                            else:
                                for i in range(2):
                                    last = M.matmul(out[64 * i:64 * i + 64], v[:, (2 * c + i) * 64:(2 * c + i + 1) * 64],
                                                    probsT[:, n % 2, i, keys], start=m == 0, stop=m == len(tiles) - 1)
                        last.then_inc(o_full, 1)

                    for t in range(A_STEPS):
                        if t < UNITS:
                            scores(t)
                        if 1 <= t <= UNITS:
                            probs_transposed(t - 1)
                        if t >= 2:
                            values(t - 2)
                        z_group(11 + t)
                    for t in range(A_STEPS):
                        if t < UNITS:
                            scores(UNITS + t)
                        if 1 <= t <= UNITS:
                            probs_transposed(UNITS + t - 1)
                        if t >= 2:
                            values(UNITS + t - 2)
                        if t < 4:
                            f = 29 + 2 * t
                            pe.wait_ge(a_sq, t + 1)
                            M.matmul(psum[:, bank_free(f), 0:T], ones, square[:, t % 2, :], start=True, stop=True).then_inc(z_full, 1)
                        if t < 8:
                            z_group(25 + t)
                        else:
                            mod_slab(t - 4)
                    mod_slab(10)
                    mod_slab(11)

                    pe.wait_ge(pT_act, 2 * UNITS)
                    keys_in_rows(BK, TR[0])
                    for b in range(NBLK):
                        for c in range(2):
                            last = transpose(psum[:, S[b // 2], (b % 2) * 2 * P + c * P:(b % 2) * 2 * P + (c + 1) * P],
                                             zT[:, CK + c, b * P:(b + 1) * P])
                    last.then_inc(kr_tr, 1)
                    pe.wait_ge(ko_ev, 2)
                    pe.wait_ge(pT_dve, UNITS)
                    pe.wait_ge(kr_ev, 4)
                    for kind, b in ((0, 0), (1, 0), (2, 1), (3, 2)):
                        for h in range(HEADS_C):
                            c, i = divmod(h, 2)
                            last = M.matmul(psum[64 * i:64 * i + 64, TR[kind // 2], (kind % 2) * 2 * P + c * P:(kind % 2) * 2 * P + (c + 1) * P],
                                            k_dec[:, kind, h * 64:(h + 1) * 64], v_rows[:, 2, b, h * P:(h + 1) * P], start=True, stop=True)
                        if kind % 2:
                            last.then_inc(st_full, 1)

                    def c_att(h):
                        c, i = divmod(h, 2)
                        part = slice(64 * i, 64 * i + 64)
                        if h >= 2:
                            pe.wait_ge(att_ready, h - 1)
                        for b in range(NBLK):
                            blk = slice(b * P, (b + 1) * P)
                            last = M.matmul(psum[:, S[h % 2], blk], zT[part, CK + c, blk], zT[part, CQ + c, blk], start=True, stop=True)
                        last.then_inc(att_full, 1)

                    def c_out(h):
                        c, i = divmod(h, 2)
                        part = slice(64 * i, 64 * i + 64)
                        pe.wait_ge(att_ready, h + 1)
                        if h == 0:
                            pe.wait_ge(st1_ready, 4)
                            pe.wait_ge(qd_ready, 4)
                            pe.wait_ge(o_read, 8)
                        if h >= 2:
                            pe.wait_ge(co_read, h - 1)
                        for b in range(NBLK):
                            out = psum[:, O[h % 2], b * P:(b + 1) * P]
                            last = M.matmul(out, v_rows[:, 2, b, h * P:(h + 1) * P], att[:, h % 2, b * P:(b + 1) * P], start=True, stop=b == 0)
                            if b:
                                for d in range(2):
                                    state = state0 if (b == 1) == (d == 0) else state1
                                    last = M.matmul(out, state[part, d, c, :], q_dec[part, d, c, (b - 1) * P:b * P], start=False, stop=d == 1)
                        last.then_inc(co_full, 1)

                    def c_mean(h):
                        if h == 0:
                            pe.wait_ge(st_ev, 1)
                        pe.wait_ge(co_read, h + 1)
                        if h >= 1:
                            pe.wait_ge(ccen, h)
                        M.matmul(psum[:, TR[0], 0:T], ones, c_raw[:, h % 2, :], start=True, stop=True).then_inc(cmean_full, 1)

                    def c_var(h):
                        pe.wait_ge(csq, h + 1)
                        if h >= 1:
                            pe.wait_ge(crs, h)
                        M.matmul(psum[:, TR[1], 0:T], ones, square[:, h % 2, :], start=True, stop=True).then_inc(cvar_full, 1)

                    for m in range(3 * KD):
                        branch, j = divmod(m, KD)
                        if m < HEADS_C:
                            c_att(m)
                        if 1 <= m <= HEADS_C:
                            c_out(m - 1)
                        if 2 <= m <= HEADS_C + 1:
                            c_mean(m - 2)
                        if 3 <= m <= HEADS_C + 2:
                            c_var(m - 3)
                        n_gate = 21 + 3 * branch + (0 if j < 4 else 2)
                        n_proj = 22 + 3 * branch
                        if j % 4 == 0:
                            slab_here(n_gate)
                        if m == 0:
                            pe.wait_ge(z_read, FILLERS)
                        else:
                            pe.wait_ge(gate_exp, m)
                        bank = Z[1]
                        for k in range(KD):
                            last = M.matmul(psum[:, bank, 0:T], ring[:, n_gate % RING, k, (j % 4) * P:(j % 4 + 1) * P], hT[:, k, :],
                                            start=k == 0, stop=k == KD - 1)
                        last.then_inc(gate_full, 1)
                        if j == 0:
                            slab_here(n_proj)
                            if branch == 0:
                                pe.wait_ge(a_done, 4)
                            if branch == 2:
                                pe.wait_ge(c_done, 4)
                        if m >= 1:
                            pe.wait_ge(br_read, m)
                        w = slab_into(n_proj)
                        source = (AQ, BQ, CG)[branch]
                        for k in range(4):
                            last = M.matmul(psum[:, Z[0], 0:T], w[:, k, j * P:(j + 1) * P], zT[:, source + k, :], start=k == 0, stop=k == 3)
                        last.then_inc(br_full, 1)

                    for j in range(KD):
                        if j % 4 == 0:
                            slab_here(30 + j // 4)
                        if j == 0:
                            pe.wait_ge(br_read, 3 * KD)
                        if j >= 2:
                            pe.wait_ge(w_read, j - 1)
                        for k in range(KD):
                            last = M.matmul(psum[:, S[j % 2], 0:T], ring[:, (30 + j // 4) % RING, k, (j % 4) * P:(j % 4 + 1) * P], merged[:, k, :],
                                            start=k == 0, stop=k == KD - 1)
                        last.then_inc(w_full, 1)

                    norm_sum(TR[0], KD)
                    pe.wait_ge(h_ready, 2 * KD)
                    for b in range(NBLK):
                        for k in range(KD):
                            last = M.matmul(psum[:, TR[1], b * NE:(b + 1) * NE], hT[:, k, b * P:(b + 1) * P], w_r[:, k, :], start=k == 0, stop=k == KD - 1)
                    last.then_inc(lg_full, 1)
                    for n in range(2 * NBLK):
                        if n >= 2:
                            pe.wait_ge(hr_ev, n - 1)
                        for q in range(4):
                            last = transpose(psum[:, O[n % 2], q * P:(q + 1) * P], hT[:, (n % 2) * 4 + q, (n // 2) * P:(n // 2 + 1) * P])
                        last.then_inc(hr_tr, 1)
                    pe.wait_ge(aff_ready, 1)
                    for b in range(NBLK):
                        last = transpose(psum[0:NE, S[0], b * P:(b + 1) * P], aff[:, b, :])
                    last.then_inc(affT_full, 1)
                    pe.wait_ge(slots_ready, 1)
                    for b in range(NBLK):
                        last = transpose(psum[:, S[1], b * NE:(b + 1) * NE], place[0:NE, b * P:(b + 1) * P])
                    last.then_inc(slots_tr, 1)
                    pe.wait_ge(hr_ev, 2 * NBLK)

                    with pe.Fori(0, NE // 2) as pair:
                        for e in range(2):
                            def nth(per_expert, x):
                                return pair * (2 * per_expert) + (e * per_expert + x)

                            def expert_slab(s):
                                j = e * EXPERT_SLABS + s
                                pe.wait_ge(slab_in[j % RING], pair * (16 * 3) + 16 * (DENSE_SLABS // RING + j // RING + 1))
                                return ring[:, j % RING]

                            pe.wait_ge(pick_ready, nth(1, 1))
                            for k in range(KD):
                                for b in range(NBLK):
                                    last = M.matmul(psum[:, O[0], k * SLOTS:(k + 1) * SLOTS], h_rows[:, b, k * P:(k + 1) * P], pick[:, e, b, :],
                                                    start=b == 0, stop=b == NBLK - 1)
                            last.then_inc(g_full, 1)
                            for b in range(NBLK):
                                last = transpose(psum[0:SLOTS, O[1], b * P:(b + 1) * P], pick_g[:, e, b, :])
                            last.then_inc(pgT_full, 1)
                            pe.wait_ge(g_read, nth(1, 1))
                            for s in range(4):
                                w = expert_slab(s)
                                for q in range(4):
                                    cols = slice((4 * (s % 2) + q) * SLOTS, (4 * (s % 2) + q + 1) * SLOTS)
                                    for k in range(KD):
                                        last = M.matmul(psum[:, S[s // 2], cols], w[:, k, q * P:(q + 1) * P], xgT[:, k, :], start=k == 0, stop=k == KD - 1)
                                last.then_inc((gate_h, up_h)[s // 2], 1)
                            pe.wait_ge(hid_ready, nth(1, 1))
                            for s in range(4, 6):
                                w = expert_slab(s)
                                for q in range(4):
                                    cols = slice((4 * (s % 2) + q) * SLOTS, (4 * (s % 2) + q + 1) * SLOTS)
                                    for k in range(KD):
                                        last = M.matmul(psum[:, TR[0], cols], w[:, k, q * P:(q + 1) * P], hid[:, k, :], start=k == 0, stop=k == KD - 1)
                                last.then_inc(down_full, 1)
                            pe.wait_ge(down_read, nth(1, 1))
                            for k in range(KD):
                                dst = psum[0:SLOTS, Z[k // 4], (k % 4) * P:(k % 4 + 1) * P]
                                if k == 0:
                                    M.matmul(dst, outT[:, k, :], ident, start=True, stop=True)
                                else:
                                    last = transpose(dst, outT[:, k, :])
                                if k % 4 == 3:
                                    last.then_inc(or_tr, 1)
                            pe.wait_ge(or_read, nth(2, 2))
                            pe.wait_ge(pgT_read, nth(1, 1))
                            for k in range(KD):
                                if k >= 2:
                                    pe.wait_ge(sc_read, nth(8, k - 1))
                                M.matmul(psum[:, (TR[1], O[0])[k % 2], 0:T], out_rows[0:SLOTS, k * P:(k + 1) * P], pick_gT[0:SLOTS, :],
                                         start=True, stop=True).then_inc(sc_full, 1)

                @block.scalar
                def _(sc):
                    for dst, src in ((vec_rows[0:48, :], b_mod[layer].rearrange("(k p) -> k p", p=P)),
                                     (vec_rows[48:56, :], norm_mix[layer].rearrange("(k p) -> k p", p=P)),
                                     (vec_rows[56:64, :], norm_ffn[layer].rearrange("(k p) -> k p", p=P)),
                                     (vec_rows[64:68, :], diff_norm[layer].rearrange("(k p) -> k p", p=P)),
                                     (vec_rows[68:72, :], ret_norm[layer].rearrange("(k p) -> k p", p=P)),
                                     (lam_rows[:].rearrange("p a d -> p (a d)"),
                                      bass.AP(diff_lambda.tensor, diff_lambda.offset + layer * 256, [[0, P], [1, 256]])),
                                     (decay[:], bass.AP(ret_decay.tensor, ret_decay.offset + layer * 8, [[0, P], [1, 8]])),
                                     (layer_c[:], layer_in[layer]),
                                     (w_r[:], w_router[layer].rearrange("(k p) e -> p k e", p=P))):
                        sc.dma_start(dst, src).then_inc(small_in, 16)
                    for dst, src in ((akc_rows, cache_a_k), (av_c, cache_a_v), (bkc_rows, cache_b_k), (bv_c, cache_b_v)):
                        sc.dma_start(dst, src[layer]).then_inc(cache_in, 16)
                    for d, src in enumerate((state_f, state_b)):
                        sc.dma_start(state0[:, d], src[layer].rearrange("(c i) k e -> (i k) c e", c=2)).then_inc(state_in, 16)
                    for b in range(2):
                        for half in range(2):
                            q_row = 2 * b + half
                            skew = bass.AP(rpb_rev.tensor,
                                           rpb_rev.offset + layer * (HEADS_B * RPB_ROWS * RPB_COLS) + ((7 - q_row) * HEADS_B * RPB_COLS + 15 - (GRID_W - 1)),
                                           [[1, GRID_W], [RPB_COLS, 4 * HEADS_B], [1, GRID_W]])
                            dst = (bias[b] if b else bias[b][:])[GRID_W * half:GRID_W * (half + 1)]
                            sc.dma_start(dst, skew).then_inc(bias_in, 16)

                    link = chain(sc, act_link)

                    def squares(first):
                        for k in range(KD):
                            if first + k >= 2:
                                sc.wait_ge(sq_used, first + k - 1)
                            if first:
                                sc.wait_ge(w_read, k + 1)
                            A_.activation(square[:, k % 2, :], xT[:, k, :], ACT.Square).then_inc(sq_ready, 1)

                    def inverse_rms(bank, n):
                        sc.wait_ge(sq_used, n)
                        link(A_.activation(rs[:], psum[:, bank, 0:T], ACT.Ln, scale=1.0 / D, bias=c_("eps")))
                        A_.activation(rs[:], rs[:], ACT.Exp, scale=-0.5).then_inc(rs_ready, 1)

                    def modulate(first, scale, shift):
                        for k in range(KD):
                            sc.wait_ge(norm_mul, first + k + 1)
                            for g, cols in enumerate((CTX, LAT)):
                                last = A_.activation(hT[:, k, cols], tmp[:, k % 2, cols], ACT.Identity,
                                                     bias=modT[:, shift + k, g:g + 1], scale=scale[:, k, g:g + 1])
                            last.then_inc(h_ready, 1)

                    A_.preload_act_table_set("natural_log_exp_and_others")
                    squares(0)
                    inverse_rms(S[0], KD)
                    sc.wait_ge(lam_sum, 1)
                    A_.activation(lamb[:, 2:4], lamb[:, 0:2], ACT.Exp).then_inc(lam_exp, 1)
                    sc.wait_ge(abs_ready, 1)
                    link(A_.activation(decay_t[:, 1], decay_t[:, 0], ACT.Exp, scale=-1.0))
                    A_.activation(decay_t[:, 2], decay_t[:, 1], ACT.Ln, bias=c_("one")).then_inc(ln_ready, 1)
                    sc.wait_ge(decay_ready, 1)
                    for h in range(HEADS_C):
                        A_.activation(in_decay[:, h], c_("below"), ACT.Exp, scale=decay[:, h:h + 1])
                        last = A_.activation(bwd_decay[:, h], c_("above"), ACT.Exp, scale=decay[:, 4 + h:5 + h])
                    last.then_inc(decay_exp, 1)
                    for d, (row, col) in enumerate((("since", "k_until"), ("until", "k_since"))):
                        for c in range(2):
                            for i in range(2):
                                part = slice(64 * i, 64 * i + 64)
                                h = 4 * d + 2 * c + i
                                A_.activation(q_decay[part, d, c, :], c_(row)[part], ACT.Exp, scale=decay[part, h:h + 1])
                        A_.activation(k_decay[:, d, :], decay[:, 4 * d:4 * d + 4], ACT.Exp, scale=c_(col))
                    for i in range(2):
                        part = slice(64 * i, 64 * i + 64)
                        last = A_.activation(chunk_decay[part], decay[part].rearrange("p (d c i) -> p d c i", d=2, c=2)[:, :, :, i],
                                             ACT.Exp, scale=float(P))
                    last.then_inc(chunk_ready, 1)
                    for n, (dst, bank) in enumerate(((akcT, O[0]), (bkcT, O[1]))):
                        sc.wait_ge(kc_tr, n + 1)
                        A_.activation(dst[:].rearrange("p c t -> p (c t)"), psum[:, bank, :], ACT.Copy).then_inc(kc_ev, 1)

                    def read_mod(j):
                        f = f_of_mod(j)
                        sc.wait_ge(z_full, f + 1)
                        A_.activation(modT[:, 4 * j:4 * j + 4, :].rearrange("p k g -> p (k g)"), psum[:, Z[f % 2], 0:8], ACT.Copy).then_inc(z_read, 1)

                    def read_z(g):
                        slab, j, kind = Z_GROUPS[g]
                        f = f_of_z(g)
                        sc.wait_ge(z_full, f + 1)
                        if kind == "rows":
                            mixer = {2: 0, 5: 1, 7: 2}[slab]
                            A_.activation(v_rows[:, mixer, j, :], psum[:, Z[f % 2], :], ACT.Copy).then_inc(z_read, 1)
                        else:
                            chunk = {0: AQ, 1: AK, 3: BQ, 4: BK, 6: CQ, 8: CG}[slab] + j
                            s = SCALE if chunk in (CK, CK + 1) else 1.0
                            A_.activation(zT[:, chunk, :], psum[:, Z[f % 2], 0:T], ACT.Copy, scale=s).then_inc(z_read, 1)

                    for j in range(4):
                        read_mod(j)
                    sc.wait_ge(mod1_ready, 1)
                    modulate(0, scale_mix, 0)
                    for g in range(11):
                        read_z(g)
                    sc.wait_ge(z_read, f_of_z(10) + 1)
                    sc.dma_start(new_av[layer], v_rows[:, 0, 0, :]).then_inc(v_stored, 16)
                    sc.wait_ge(ko_tr, 1)
                    sc.wait_ge(in_decay_ready, 1)
                    A_.activation(keys_out, psum[:, TR[0], :], ACT.Copy).then_inc(ko_ev, 1)
                    sc.wait_ge(ko_ev, 1)
                    sc.dma_start(new_ak[layer], keys_out).then_inc(ko_st, 16)

                    def exps(n):
                        mixer, u = divmod(n, UNITS)
                        b = u % NBLK
                        keys = P if b == 0 else T
                        own = mixer == 0 or b == 0
                        sc.wait_ge(s_max, n + 1)
                        if own and n >= 2:
                            sc.wait_ge(pT_full, n - 1)
                        for i in range(2):
                            dst = probs[:, n % 2, i, 0:keys]
                            last = A_.activation(dst, psum[:, S[i], 0:keys] if own else dst, ACT.Exp,
                                                 bias=small[:, n % 2, i:i + 1], scale=SCALE if own else 1.0,
                                                 accum_out=small[:, n % 2, 2 + i:3 + i])
                        last.then_inc(s_exp, 1)

                    def read_pT(n):
                        keys = P if n % NBLK == 0 else T
                        sc.wait_ge(pT_full, n + 1)
                        if n >= 2:
                            sc.wait_ge(o_full, n - 1)
                        A_.activation(probsT[:, n % 2, 0, 0:keys], psum[:, TR[0], 0:keys], ACT.Copy).then_inc(pT_act, 1)

                    def read_o(n):
                        mixer, u = divmod(n, UNITS)
                        if u % NBLK == NBLK - 1:
                            c = u // NBLK
                            sc.wait_ge(o_full, n + 1)
                            A_.activation(zT[:, (AQ, BQ)[mixer] + c, :], psum[:, O[c % 2], 0:T], ACT.Copy).then_inc(o_read, 1)

                    for t in range(A_STEPS):
                        if t < UNITS:
                            exps(t)
                        if 1 <= t <= UNITS:
                            read_pT(t - 1)
                        if t >= 2:
                            read_o(t - 2)
                        read_z(11 + t)
                        if 11 + t == 21:
                            sc.wait_ge(z_read, f_of_z(21) + 1)
                            sc.dma_start(new_bv[layer], v_rows[:, 1, 0, :]).then_inc(v_stored, 16)
                    for t in range(A_STEPS):
                        if t < 4:
                            sc.wait_ge(o_read, t + 1)
                            A_.activation(square[:, t % 2, :], zT[:, AQ + t, :], ACT.Square).then_inc(a_sq, 1)
                        if t < UNITS:
                            exps(UNITS + t)
                        if 1 <= t <= UNITS:
                            read_pT(UNITS + t - 1)
                        if t >= 2:
                            read_o(UNITS + t - 2)
                        if t < 4:
                            f = 29 + 2 * t
                            sc.wait_ge(z_full, f + 1)
                            if t >= 2:
                                sc.wait_ge(a_done, t - 1)
                            A_.activation(tmp[:, t % 2, :], psum[:, Z[f % 2], 0:T], ACT.Ln, scale=1.0 / P, bias=c_("eps")).then_inc(z_read, 1)
                            sc.wait_ge(z_read, f + 1)
                            A_.activation(tmp[:, t % 2, :], tmp[:, t % 2, :], ACT.Exp, scale=-0.5).then_inc(nrs, 1)
                        if t < 8:
                            read_z(25 + t)
                        else:
                            read_mod(t - 4)
                    read_mod(10)
                    read_mod(11)

                    sc.wait_ge(ko_tr, 2)
                    sc.wait_ge(ko_st, 16)
                    A_.activation(keys_out, psum[:, TR[0], :], ACT.Copy).then_inc(ko_ev, 1)
                    sc.wait_ge(ko_ev, 2)
                    sc.dma_start(new_bk[layer], keys_out).then_inc(ko_st, 16)
                    sc.wait_ge(v_stored, 32)
                    sc.wait_ge(o_full, 2 * UNITS)
                    sc.wait_ge(z_read, f_of_z(32) + 1)
                    A_.activation(cg_sig, zT[:, CG:CG + 4, :].rearrange("p c t -> p (c t)"), ACT.Exp, scale=-1.0).then_inc(cg_exp, 1)
                    sc.wait_ge(st_full, 1)
                    A_.activation(ctx_state[:].rearrange("p d c e -> p (d c e)"), psum[:, TR[0], :], ACT.Copy).then_inc(st_ev, 1)
                    sc.wait_ge(st_ev, 1)
                    for d, out in enumerate((new_sf, new_sb)):
                        sc.dma_start(out[layer].rearrange("(c i) k e -> (i k) c e", c=2), ctx_state[:, d]).then_inc(stored, 16)

                    for m in range(3 * KD):
                        if 2 <= m <= HEADS_C + 1:
                            h = m - 2
                            sc.wait_ge(ccen, h + 1)
                            A_.activation(square[:, h % 2, :], c_raw[:, h % 2, :], ACT.Square).then_inc(csq, 1)
                        if 3 <= m <= HEADS_C + 2:
                            h = m - 3
                            sc.wait_ge(cvar_full, h + 1)
                            if h >= 2:
                                sc.wait_ge(c_done, h - 1)
                            A_.activation(c_rs[:, h % 2, :], psum[:, TR[1], 0:T], ACT.Ln, scale=1.0 / P, bias=c_("eps")).then_inc(crs, 1)
                            sc.wait_ge(crs, h + 1)
                            A_.activation(c_rs[:, h % 2, :], c_rs[:, h % 2, :], ACT.Exp, scale=-0.5).then_inc(crs_read, 1)
                        if 1 <= m <= HEADS_C:
                            h = m - 1
                            sc.wait_ge(co_full, h + 1)
                            if h >= 2:
                                sc.wait_ge(c_done, h - 1)
                            A_.activation(c_raw[:, h % 2, :], psum[:, O[h % 2], 0:T], ACT.Copy).then_inc(co_read, 1)
                        sc.wait_ge(gate_full, m + 1)
                        if m >= 2:
                            sc.wait_ge(br_read, m - 1)
                        A_.activation(gate_e[m % 2], psum[:, Z[1], 0:T], ACT.Exp, scale=-1.0).then_inc(gate_exp, 1)

                    squares(KD)
                    inverse_rms(TR[0], 2 * KD)
                    modulate(KD, scale_ffn, 24)
                    sc.wait_ge(lg_max, 1)
                    A_.activation(aff, aff, ACT.Exp).then_inc(lg_exp, 1)
                    for n in range(2 * NBLK):
                        sc.wait_ge(hr_tr, n + 1)
                        A_.activation(h_rows[:, n // 2, (n % 2) * 512:(n % 2 + 1) * 512], psum[:, O[n % 2], :], ACT.Copy).then_inc(hr_ev, 1)

                    sc.wait_ge(ko_st, 32)
                    sc.wait_ge(stored, 32)
                    A_.preload_act_table(ACT.Silu)
                    with sc.Fori(0, NE // 2) as pair:
                        for e in range(2):
                            def nth(per_expert, x):
                                return pair * (2 * per_expert) + (e * per_expert + x)

                            def flat(x):
                                return x.rearrange("p k s -> p (k s)")

                            sc.wait_ge(g_full, nth(1, 1))
                            A_.activation(flat(xgT), psum[:, O[0], 0:KD * SLOTS], ACT.Copy).then_inc(g_read, 1)
                            sc.wait_ge(gate_h, nth(2, 2))
                            A_.activation(flat(act), psum[:, S[0], 0:KD * SLOTS], ACT.Silu).then_inc(silu_ready, 1)
                            sc.wait_ge(down_full, nth(2, 2))
                            A_.activation(flat(outT), psum[:, TR[0], 0:KD * SLOTS], ACT.Copy).then_inc(down_read, 1)
                            for half in range(2):
                                sc.wait_ge(or_tr, nth(2, half + 1))
                                A_.activation(out_rows[0:SLOTS, half * 512:(half + 1) * 512], psum[0:SLOTS, Z[half], :], ACT.Copy).then_inc(or_read, 1)

                @block.vector
                def _(dve):
                    then = chain(dve, dve_link)

                    dve.wait_ge(vec_tr, 1)
                    V.tensor_copy(vecT[:], psum[:, TR[1], 0:72]).then_inc(vec_ready, 1)
                    dve.wait_ge(vec_ready, 1)
                    dve.wait_ge(small_in, 16 * 9)
                    pairs = lam_rows[:].rearrange("p (a i) d -> p a i d", i=2)
                    prod = gate_e[0][:, 0:P].rearrange("p (a d) -> p a d", a=2)
                    then(V.tensor_tensor(prod, pairs[:, :, 0, :], pairs[:, :, 1, :], ALU.mult))
                    V.reduce_sum(lamb[:, 0:2], prod, axis=AX_X).then_inc(lam_sum, 1)
                    then(V.tensor_scalar(decay_t[:, 3], decay[:], -1.0, None, ALU.mult))
                    V.tensor_tensor(decay_t[:, 0], decay[:], decay_t[:, 3], ALU.max).then_inc(abs_ready, 1)
                    dve.wait_ge(lam_exp, 1)
                    then(V.tensor_tensor(lamb[:, 4:5], lamb[:, 3:4], lamb[:, 2:3], ALU.subtract))
                    then(V.tensor_tensor(lamb[:, 5:6], lamb[:, 4:5], layer_c[:, 0:1], ALU.subtract))
                    then(V.tensor_scalar(gain_a[:], vecT[:, 64:68], layer_c[:, 1:2], None, ALU.mult))
                    dve.wait_ge(ln_ready, 1)
                    then(V.tensor_scalar(decay_t[:, 3], decay[:], 0.0, None, ALU.min))
                    V.tensor_tensor(decay[:], decay_t[:, 3], decay_t[:, 2], ALU.subtract).then_inc(decay_ready, 1)
                    dve.wait_ge(decay_ready, 1)

                    def normed(first):
                        dve.wait_ge(rs_ready, 1 + first // KD)
                        for k in range(KD):
                            if k >= 2:
                                dve.wait_ge(h_ready, first + k - 1)
                            V.tensor_tensor(tmp[:, k % 2, :], xT[:, k, :], rs[:], ALU.mult).then_inc(norm_mul, 1)

                    dve.wait_ge(z_read, 4)
                    then(V.tensor_tensor(modT[:, 0:16, :], modT[:, 0:16, :], vecT[:, 0:16].unsqueeze(2).to_broadcast([P, 16, 2]), ALU.add))
                    V.scalar_tensor_tensor(out=scale_mix[:], in0=modT[:, 8:16, :], scalar=1.0,
                                           in1=vecT[:, 48:56].unsqueeze(2).to_broadcast([P, KD, 2]), op0=ALU.add, op1=ALU.mult).then_inc(mod1_ready, 1)
                    normed(0)

                    for c in range(8):
                        dve.wait_ge(rot_full, c + 1)
                        if c >= 2:
                            dve.wait_ge(rope_done, c - 1)
                        else:
                            dve.wait_ge(h_ready, KD)
                        then(V.tensor_tensor(tmp[:, c % 2, 0:2 * P], psum[:, S[c % 2], 0:2 * P], c_("sin"), ALU.mult))
                        then(V.tensor_tensor(zT[:, AQ + c, LAT], zT[:, AQ + c, LAT], c_("cos"), ALU.mult))
                        V.tensor_tensor(zT[:, AQ + c, LAT], zT[:, AQ + c, LAT], tmp[:, c % 2, 0:2 * P], ALU.add).then_inc(rope_done, 1)

                    def row_max(n):
                        mixer, u = divmod(n, UNITS)
                        c, b = divmod(u, NBLK)
                        keys = P if b == 0 else T
                        dve.wait_ge(s_full, n + 1)
                        if mixer == 0 or b == 0:
                            for i in range(2):
                                then(V.reduce_max(small[:, n % 2, 4 + i:5 + i], psum[:, S[i], 0:keys], axis=AX_X))
                            V.tensor_scalar(small[:, n % 2, 0:2], small[:, n % 2, 4:6], -SCALE, None, ALU.mult).then_inc(s_max, 1)
                        else:
                            dve.wait_ge(pT_full, n - 1)
                            if n < UNITS + 3:
                                dve.wait_ge(bias_ready, 2)
                            for i in range(2):
                                h = 2 * c + i
                                own = probs[:, n % 2, i, 0:2 * P].rearrange("p (r c) -> p r c", r=4)
                                V.scalar_tensor_tensor(out=own, in0=psum[:, S[i], 0:2 * P].rearrange("p (r c) -> p r c", r=4), scalar=SCALE,
                                                       in1=bias[b - 1][:, h::HEADS_B, ::-1], op0=ALU.mult, op1=ALU.add)
                                then(V.tensor_scalar(probs[:, n % 2, i, 2 * P:T], psum[:, S[i], 2 * P:T], SCALE, None, ALU.mult))
                            then(V.reduce_max(small[:, n % 2, 4:6], probs[:, n % 2, :, :], axis=AX_X))
                            V.tensor_scalar(small[:, n % 2, 0:2], small[:, n % 2, 4:6], -1.0, None, ALU.mult).then_inc(s_max, 1)

                    def normalise(n):
                        mixer, u = divmod(n, UNITS)
                        keys = P if u % NBLK == 0 else T
                        dve.wait_ge(s_exp, n + 1)
                        then(V.reciprocal(small[:, n % 2, 4:6], small[:, n % 2, 2:4]))
                        p0, p1 = probs[:, n % 2, 0, 0:keys], probs[:, n % 2, 1, 0:keys]
                        if mixer == 0:
                            then(V.tensor_tensor(small[:, n % 2, 6:7], small[:, n % 2, 5:6], lamb[:, 5:6], ALU.mult))
                            then(V.tensor_scalar(p1, p1, small[:, n % 2, 6:7], None, ALU.mult))
                            V.scalar_tensor_tensor(out=p0, in0=p0, scalar=small[:, n % 2, 4:5], in1=p1, op0=ALU.mult, op1=ALU.add).then_inc(p_ready, 1)
                        else:
                            V.tensor_scalar(p0, p0, small[:, n % 2, 4:5], None, ALU.mult)
                            V.tensor_scalar(p1, p1, small[:, n % 2, 5:6], None, ALU.mult).then_inc(p_ready, 1)

                    for n in range(UNITS):
                        row_max(n)
                        normalise(n)
                    for t in range(A_STEPS):
                        if t < UNITS:
                            row_max(UNITS + t)
                            normalise(UNITS + t)
                        if 1 <= t <= UNITS:
                            n = UNITS + t - 1
                            keys = P if n % NBLK == 0 else T
                            dve.wait_ge(pT_full, n + 1)
                            dve.wait_ge(o_full, n - 1)
                            V.tensor_copy(probsT[:, n % 2, 1, 0:keys], psum[:, TR[1], 0:keys]).then_inc(pT_dve, 1)
                        if t < 4:
                            dve.wait_ge(nrs, t + 1)
                            V.scalar_tensor_tensor(out=zT[:, AQ + t, :], in0=zT[:, AQ + t, :], scalar=gain_a[:, t:t + 1],
                                                   in1=tmp[:, t % 2, :], op0=ALU.mult, op1=ALU.mult).then_inc(a_done, 1)

                    dve.wait_ge(o_full, 2 * UNITS)
                    dve.wait_ge(kr_tr, 1)
                    dve.wait_ge(chunk_ready, 1)
                    heads = [P, 4, 64]
                    for kind, (b, d) in enumerate(((0, 0), (0, 1), (1, 0), (2, 1))):
                        rows = psum[:, S[b // 2], (b % 2) * 2 * P:(b % 2 + 1) * 2 * P].rearrange("p (h e) -> p h e", h=4)
                        V.tensor_tensor(k_dec[:, kind, :].rearrange("p (h e) -> p h e", h=4), rows,
                                        k_decay[:, d, :].unsqueeze(2).to_broadcast(heads), ALU.mult).then_inc(kr_ev, 1)
                    for d in range(2):
                        for c in range(2):
                            V.tensor_tensor(q_dec[:, d, c, :].rearrange("p (b t) -> p b t", b=2),
                                            zT[:, CQ + c, LAT].rearrange("p (b t) -> p b t", b=2),
                                            q_decay[:, d, c, :].unsqueeze(1).to_broadcast([P, 2, P]), ALU.mult).then_inc(qd_ready, 1)
                    dve.wait_ge(st_full, 2)
                    dve.wait_ge(state_in, 32)
                    for d in range(2):
                        for c in range(2):
                            V.scalar_tensor_tensor(out=state1[:, d, c, :], in0=state0[:, d, c, :], scalar=chunk_decay[:, d, c:c + 1],
                                                   in1=psum[:, TR[1], d * 2 * P + c * P:d * 2 * P + (c + 1) * P],
                                                   op0=ALU.mult, op1=ALU.add).then_inc(st1_ready, 1)
                    dve.wait_ge(z_read, FILLERS)
                    then(V.tensor_tensor(modT[:, 16:48, :], modT[:, 16:48, :], vecT[:, 16:48].unsqueeze(2).to_broadcast([P, 32, 2]), ALU.add))
                    V.scalar_tensor_tensor(out=scale_ffn[:], in0=modT[:, 32:40, :], scalar=1.0,
                                           in1=vecT[:, 56:64].unsqueeze(2).to_broadcast([P, KD, 2]), op0=ALU.add, op1=ALU.mult).then_inc(mod2_ready, 1)
                    dve.wait_ge(mod2_ready, 1)
                    dve.wait_ge(in_decay_ready, 1)

                    for m in range(3 * KD):
                        branch, j = divmod(m, KD)
                        if m < HEADS_C:
                            dve.wait_ge(att_full, m + 1)
                            if m >= 2:
                                dve.wait_ge(co_full, m - 1)
                            blocks = [P, NBLK, P]
                            V.tensor_tensor(att[:, m % 2, :].rearrange("p (b t) -> p b t", b=NBLK),
                                            psum[:, S[m % 2], 0:T].rearrange("p (b t) -> p b t", b=NBLK),
                                            in_decay[:, m, :].unsqueeze(1).to_broadcast(blocks), ALU.mult).then_inc(att_ready, 1)
                        if m == 0:
                            cg = zT[:, CG:CG + 4, :].rearrange("p c t -> p (c t)")
                            dve.wait_ge(cg_exp, 1)
                            then(V.tensor_scalar(cg_sig, cg_sig, 1.0, None, ALU.add))
                            then(V.reciprocal(cg_sig, cg_sig))
                            then(V.tensor_tensor(cg, cg, cg_sig, ALU.mult))
                        if 2 <= m <= HEADS_C + 1:
                            h = m - 2
                            dve.wait_ge(cmean_full, h + 1)
                            V.scalar_tensor_tensor(out=c_raw[:, h % 2, :], in0=psum[:, TR[0], 0:T], scalar=-1.0 / P, in1=c_raw[:, h % 2, :],
                                                   op0=ALU.mult, op1=ALU.add).then_inc(ccen, 1)
                        if 3 <= m <= HEADS_C + 2:
                            h = m - 3
                            dve.wait_ge(crs_read, h + 1)
                            then(V.tensor_tensor(c_rs[:, h % 2, :], c_rs[:, h % 2, :], c_raw[:, h % 2, :], ALU.mult))
                            V.scalar_tensor_tensor(out=zT[:, CG + h, :], in0=c_rs[:, h % 2, :], scalar=vecT[:, 68 + h:69 + h],
                                                   in1=zT[:, CG + h, :], op0=ALU.mult, op1=ALU.mult).then_inc(c_done, 1)
                        g = gate_e[m % 2]
                        dve.wait_ge(gate_exp, m + 1)
                        then(V.tensor_scalar(g, g, 1.0, None, ALU.add))
                        then(V.reciprocal(g, g))
                        dve.wait_ge(br_full, m + 1)
                        if branch == 0:
                            V.tensor_tensor(merged[:, j, :], g, psum[:, Z[0], 0:T], ALU.mult).then_inc(br_read, 1)
                        else:
                            then(V.tensor_tensor(g, g, psum[:, Z[0], 0:T], ALU.mult))
                            V.tensor_tensor(merged[:, j, :], merged[:, j, :], g, ALU.add).then_inc(br_read, 1)

                    for j in range(KD):
                        dve.wait_ge(w_full, j + 1)
                        for g, cols in enumerate((CTX, LAT)):
                            last = V.scalar_tensor_tensor(out=xT[:, j, cols], in0=psum[:, S[j % 2], cols], scalar=modT[:, 16 + j, g:g + 1],
                                                          in1=xT[:, j, cols], op0=ALU.mult, op1=ALU.add)
                        last.then_inc(w_read, 1)
                    dve.wait_ge(w_read, KD)
                    normed(KD)

                    dve.wait_ge(lg_full, 1)
                    logits = psum[:, TR[1], 0:NBLK * NE].rearrange("p (b e) -> p b e", b=NBLK)
                    per_block = small[:].rearrange("p a b -> p (a b)")
                    wide = [P, NBLK, NE]
                    then(V.reduce_max(per_block[:, 0:3], logits, axis=AX_X))
                    V.tensor_tensor(aff, logits, per_block[:, 0:3].unsqueeze(2).to_broadcast(wide), ALU.subtract).then_inc(lg_max, 1)
                    dve.wait_ge(lg_exp, 1)
                    then(V.reduce_sum(per_block[:, 4:7], aff, axis=AX_X))
                    then(V.reciprocal(per_block[:, 8:11], per_block[:, 4:7]))
                    V.tensor_tensor(aff, aff, per_block[:, 8:11].unsqueeze(2).to_broadcast(wide), ALU.mult).then_inc(aff_ready, 1)
                    dve.wait_ge(affT_full, 1)
                    rows = slice(0, NE)
                    then(V.tensor_copy(left[rows], psum[rows, S[0], 0:T]))
                    for cols, cap, first in ((CTX, CAP_CTX, 0), (LAT, CAP_LAT, CAP_CTX)):
                        for _ in range(cap // 8):
                            then(V.max(best[rows], left[rows, cols]))
                            then(V.match_replace(left[rows, cols], best[rows], left[rows, cols], -1.0))
                        then(V.tensor_scalar(chosen[rows, cols], left[rows, cols], 0.0, None, ALU.is_lt))
                        then(V.tensor_tensor_scan(place[rows, cols], chosen[rows, cols], chosen[rows, cols], float(first), ALU.add, ALU.max))
                        last = V.tensor_tensor(place[rows, cols], place[rows, cols], chosen[rows, cols], ALU.mult)
                        if cols is CTX:
                            then(last)
                        else:
                            last.then_inc(slots_ready, 1)
                    dve.wait_ge(slots_tr, 1)
                    V.tensor_copy(slot_of, psum[:, S[1], 0:NBLK * NE].rearrange("p (b e) -> p b e", b=NBLK)).then_inc(slots_ev, 1)
                    dve.wait_ge(slots_ev, 1)
                    dve.wait_ge(acc_zero, 1)

                    with dve.Fori(0, NE // 2) as pair:
                        for e in range(2):
                            def nth(per_expert, x):
                                return pair * (2 * per_expert) + (e * per_expert + x)

                            def flat(x):
                                return x.rearrange("p k s -> p (k s)")

                            expert = bass.ds(pair * 2 + e, 1)
                            for b in range(NBLK):
                                V.tensor_scalar(pick[:, e, b, :], c_("slot"), slot_of[:, b, expert], None, ALU.is_equal)
                                last = V.tensor_scalar(pick_g[:, e, b, :], c_("slot"), slot_of[:, b, expert], aff[:, b, expert], ALU.is_equal, ALU.mult)
                            last.then_inc(pick_ready, 1)
                            dve.wait_ge(pgT_full, nth(1, 1))
                            V.tensor_copy(pick_gT[0:SLOTS, :], psum[0:SLOTS, O[1], 0:T]).then_inc(pgT_read, 1)
                            dve.wait_ge(silu_ready, nth(1, 1))
                            dve.wait_ge(up_h, nth(2, 2))
                            V.tensor_tensor(flat(hid), flat(act), psum[:, S[1], 0:KD * SLOTS], ALU.mult).then_inc(hid_ready, 1)
                            for k in range(KD):
                                dve.wait_ge(sc_full, nth(8, k + 1))
                                V.tensor_tensor(acc[:, k, :], acc[:, k, :], psum[:, (TR[1], O[0])[k % 2], 0:T], ALU.add).then_inc(sc_read, 1)

                    dve.wait_ge(sc_read, NE * KD)
                    for k in range(KD):
                        for g, cols in enumerate((CTX, LAT)):
                            V.scalar_tensor_tensor(out=xT[:, k, cols], in0=acc[:, k, cols], scalar=modT[:, 40 + k, g:g + 1],
                                                   in1=xT[:, k, cols], op0=ALU.mult, op1=ALU.add)
            clear_all()

        y_rows = hT[:].rearrange("p k t -> p (k t)").rearrange("p (b d) -> p b d", b=NBLK)
        with nc.Block() as block:
            @block.sync
            def _(sp):
                sp.dma_start(vec_rows[0:KD, :], norm_final.rearrange("(k p) -> k p", p=P)).then_inc(small_in, 16)
                for b in range(NBLK):
                    sp.wait_ge(hr_ev, 2 * (b + 1))
                    sp.dma_start(y_out[b * P:(b + 1) * P, :], y_rows[:, b, :]).then_inc(stored, 16)
                sp.wait_ge(stored, 48)

            @block.scalar
            def _(sc):
                for k in range(KD):
                    if k >= 2:
                        sc.wait_ge(sq_used, k - 1)
                    A_.activation(square[:, k % 2, :], xT[:, k, :], ACT.Square).then_inc(sq_ready, 1)
                sc.wait_ge(nsum, 1)
                link = chain(sc, act_link)
                link(A_.activation(rs[:], psum[:, S[0], 0:T], ACT.Ln, scale=1.0 / D, bias=c_("eps")))
                A_.activation(rs[:], rs[:], ACT.Exp, scale=-0.5).then_inc(rs_ready, 1)

            @block.vector
            def _(dve):
                dve.wait_ge(vec_tr, 1)
                V.tensor_copy(vecT[:, 0:KD], psum[:, TR[1], 0:KD]).then_inc(vec_ready, 1)
                dve.wait_ge(vec_ready, 1)
                dve.wait_ge(rs_ready, 1)
                for k in range(KD):
                    V.scalar_tensor_tensor(out=xT[:, k, :], in0=xT[:, k, :], scalar=vecT[:, k:k + 1], in1=rs[:],
                                           op0=ALU.mult, op1=ALU.mult).then_inc(h_ready, 1)
                for n in range(2 * NBLK):
                    dve.wait_ge(hr_tr, n + 1)
                    V.tensor_copy(y_rows[:, n // 2, (n % 2) * 512:(n % 2) * 512 + 512], psum[:, n % 2, :]).then_inc(hr_ev, 1)

            @block.tensor
            def _(pe):
                pe.wait_ge(small_in, 16)
                transpose(psum[:, TR[1], 0:KD], vec_rows[0:KD, :]).then_inc(vec_tr, 1)
                for k in range(KD):
                    pe.wait_ge(sq_ready, k + 1)
                    last = M.matmul(psum[:, S[0], 0:T], ones, square[:, k % 2, :], start=k == 0, stop=k == KD - 1)
                    last.then_inc(sq_used if k < KD - 1 else nsum, 1)
                pe.wait_ge(h_ready, KD)
                for n in range(2 * NBLK):
                    if n >= 2:
                        pe.wait_ge(hr_ev, n - 1)
                    for j in range(4):
                        k = (n % 2) * 4 + j
                        last = transpose(psum[:, n % 2, j * P:(j + 1) * P], xT[:, k, (n // 2) * P:(n // 2 + 1) * P])
                    last.then_inc(hr_tr, 1)


_OUTS = [("y_prompt", (1, P, D)), ("y_sample", (1, T - P, D)), ("new_a_k", (1, DEPTH, P, HEADS_A, 2, 64)),
         ("new_a_v", (1, DEPTH, P, HEADS_A, 128)), ("new_b_k", (1, DEPTH, P, HEADS_B, 64)),
         ("new_b_v", (1, DEPTH, P, HEADS_B, 64)), ("new_c_fwd", (1, DEPTH, HEADS_C, 64, 128)),
         ("new_c_bwd", (1, DEPTH, HEADS_C, 64, 128))]


def kernel(**inputs):
    import numpy as _np
    import concourse.bacc as _bacc
    from concourse import mybir as _mybir
    from concourse.bass_utils import run_bass_kernel_spmd as _run

    a = {k: _np.asarray(v) for k, v in inputs.items()}
    table, per_layer = shape_constants()
    feeds = [
        ("x", _np.concatenate([a["x_prompt"][0], a["x_sample"][0]], axis=0)),
        ("cvec", _np.stack([a["c_ctx"], a["c"][0]])),
        ("cache_a_k", a["cache_a_k"][0].reshape(DEPTH, P, 512)),
        ("cache_a_v", a["cache_a_v"][0].reshape(DEPTH, P, 512)),
        ("cache_b_k", a["cache_b_k"][0].reshape(DEPTH, P, 512)),
        ("cache_b_v", a["cache_b_v"][0].reshape(DEPTH, P, 512)),
        ("state_f", a["state_c_fwd"][0]),
        ("state_b", a["state_c_bwd"][0]),
        ("w_mod", a["w_mod"]), ("b_mod", a["b_mod"]), ("norm_mix", a["norm_mix"]), ("norm_ffn", a["norm_ffn"]),
        ("w_in", a["w_in"]), ("diff_lambda", a["diff_lambda"]), ("diff_norm", a["diff_norm"]),
        ("rpb_rev", a["na_rpb"].transpose(0, 2, 1, 3)[..., ::-1]),
        ("ret_decay", a["ret_decay"]), ("ret_norm", a["ret_norm"]), ("w_pa", a["w_proj_a"]), ("w_pb", a["w_proj_b"]),
        ("w_pc", a["w_proj_c"]), ("w_out", a["w_out"]), ("w_router", a["w_router"]), ("w_gate", a["w_exp_gate"]),
        ("w_up", a["w_exp_up"]), ("w_down", a["w_exp_down"]), ("norm_final", a["norm_final"]),
        ("const", table), ("layer_const", per_layer),
    ]
    nc = _bacc.Bacc("TRN2", target_bir_lowering=False, num_devices=1)
    arrays, args = {}, []
    for name, value in feeds:
        value = _np.ascontiguousarray(value)
        arrays[f"in_{name}"] = value
        args.append(nc.dram_tensor(f"in_{name}", value.shape, _mybir.dt.from_np(value.dtype), kind="ExternalInput").ap())
    shapes = [("y", (T, D)), ("ak", (DEPTH, P, 512)), ("av", (DEPTH, P, 512)), ("bk", (DEPTH, P, 512)),
              ("bv", (DEPTH, P, 512)), ("sf", (DEPTH, HEADS_C, 64, P)), ("sb", (DEPTH, HEADS_C, 64, P))]
    for name, shape in shapes:
        args.append(nc.dram_tensor(f"out_{name}", shape, _mybir.dt.float32, kind="ExternalOutput").ap())
    build(nc, *args)
    r = _run(nc, [arrays], core_ids=[0]).results[0]
    y = r["out_y"]
    rest = [r[f"out_{name}"].reshape(shape) for (name, _), (_, shape) in zip(shapes[1:], _OUTS[2:])]
    return (y[0:P].reshape(_OUTS[0][1]), y[P:T].reshape(_OUTS[1][1]), *rest)
```

```python
import math
from contextlib import ExitStack

import numpy as np

import concourse.bass as bass
from concourse import mybir

F32 = mybir.dt.float32
ALU = mybir.AluOpType
ACT = mybir.ActivationFunctionType
AX_X = mybir.AxisListType.X

P = 128
D = 1024
KD = D // P
NBLK = 3
T = NBLK * P
CTX = slice(0, P)
LAT = slice(P, T)
DEPTH = 2
GRID_W = 64
HEADS_A = 4
HEADS_B = 8
HEADS_C = 4
RPB_ROWS, RPB_COLS = 15, 31
NE = 16
CAP_CTX = 2 * P // NE
CAP_LAT = 2 * (T - P) // NE
SLOTS = CAP_CTX + CAP_LAT
HALF = P // 2
EPS = 1e-6
SCALE = 64 ** -0.5
NEG = -1e30

SLAB = 512
RING = 4
DENSE_SLABS = 32
EXPERT_SLABS = 6

CONST_AT = {}
_at = 0
for _name, _width in (("ident", P), ("rot", P), ("ones", P), ("cos", 2 * P), ("sin", 2 * P),
                      ("below", P), ("above", P), ("is_below", P), ("is_above", P),
                      ("since", P), ("until", P), ("k_until", 1), ("k_since", 1), ("eps", 1), ("one", 1),
                      ("slot", HALF), ("window", GRID_W)):
    CONST_AT[_name] = (_at, _at + _width)
    _at += _width
CONST_COLS = _at


def shape_constants():
    t = np.zeros((P, CONST_COLS), np.float32)

    def put(name, value):
        a, b = CONST_AT[name]
        t[:, a:b] = value

    p = np.arange(P)[:, None].astype(np.float32)
    i = np.arange(P)[None, :].astype(np.float32)
    put("ident", np.eye(P))
    rot = np.zeros((P, P), np.float32)
    for m in range(P):
        if m % 32 < 16:
            rot[m + 16, m] = -1.0
        else:
            rot[m - 16, m] = 1.0
    put("rot", rot)
    put("ones", 1.0)
    quarter = 16
    freqs = (np.float32(10000.0) ** (-np.arange(quarter, dtype=np.float32) * np.float32(2.0) / np.float32(32))).astype(np.float32)
    tok = np.arange(2 * P)
    row = (tok // GRID_W).astype(np.float32)[:, None] * freqs
    col = (tok % GRID_W).astype(np.float32)[:, None] * freqs
    ang = np.concatenate([row, row, col, col], axis=-1).T
    ang = np.concatenate([ang, ang], axis=0)
    put("cos", np.cos(ang))
    put("sin", np.sin(ang))
    put("below", np.maximum(i - p, 0))
    put("above", np.maximum(p - i, 0))
    put("is_below", (i >= p).astype(np.float32))
    put("is_above", (p >= i).astype(np.float32))
    put("since", i + 1)
    put("until", P - i)
    put("k_until", P - 1 - p)
    put("k_since", p)
    put("eps", EPS)
    put("one", 1.0)
    put("slot", np.arange(1, HALF + 1)[None, :])
    qc = np.arange(P)[:, None] % GRID_W
    kc = GRID_W - 1 - np.arange(GRID_W)[None, :]
    start = np.clip(qc - 8, 0, GRID_W - 16)
    put("window", np.where((kc >= start) & (kc < start + 16), 0.0, NEG))
    layer = np.zeros((DEPTH, 2), np.float32)
    for l in range(DEPTH):
        lam_init = 0.8 - 0.6 * math.exp(-0.3 * l)
        layer[l] = lam_init, 1.0 - lam_init
    return t, layer


def build(nc, x_rows, cvec, cache_k, cache_v, state_f, state_b, w_mod, layer_vectors, layer_scalars,
          w_in, rpb_rev, w_pa, w_pb, w_pc, w_out, w_router, w_gate, w_up, w_down, norm_final, const_in,
          y_out, new_ak, new_av, new_bk, new_bv, new_sf, new_sb):
    ctx = ExitStack()
    sems = []

    def sb(name, shape):
        return ctx.enter_context(nc.sbuf_tensor(name, shape, F32))

    def sem(name):
        s = ctx.enter_context(nc.semaphore(name))
        sems.append(s)
        return s

    with ctx:
        ring = sb("ring", [P, RING, KD, SLAB])
        xT = sb("xT", [P, KD, T])
        hT = sb("hT", [P, KD, T])
        const = sb("const", [P, CONST_COLS])
        dense = sb("dense", [P, 13824])
        silu_c = sb("silu_c", [P, KD, 32])
        modT = sb("modT", [P, 48, 2])
        scale_mix = sb("scale_mix", [P, KD, 2])
        scale_ffn = sb("scale_ffn", [P, KD, 2])
        vec_rows = sb("vec_rows", [72, P])
        vecT = sb("vecT", [P, 72])
        square = sb("square", [P, 2, T])
        rs = sb("rs", [P, T])
        tmp = sb("tmp", [P, 2, T])
        merged = sb("merged", [P, KD, T])
        bias0 = sb("bias0", [P, HEADS_B * 4, GRID_W])
        probs = sb("probs", [P, 2, 2, T])
        probsT = sb("probsT", [P, 2, 2, T])
        akcT = sb("akcT", [P, 4, P])
        bkcT = sb("bkcT", [P, 4, P])
        small = sb("small", [P, 2, 8])
        layer_rows = sb("layer_rows", [P, 4 * 64 + 8 + 2])
        lam_rows = layer_rows[:, 0:256].rearrange("p (a d) -> p a d", a=4)
        decay = layer_rows[:, 256:264]
        layer_c = layer_rows[:, 264:266]
        lamb = sb("lamb", [P, 8])
        gain_a = sb("gain_a", [P, 4])
        decay_t = sb("decay_t", [P, 4, 8])
        in_decay = sb("in_decay", [P, 4, P])
        bwd_decay = sb("bwd_decay", [P, 4, P])
        q_decay = sb("q_decay", [P, 2, 2, P])
        k_decay = sb("k_decay", [P, 2, 4])
        chunk_decay = sb("chunk_decay", [P, 2, 2])
        state0 = sb("state0", [P, 2, 2, P])
        state1 = sb("state1", [P, 2, 2, P])
        w_r = sb("w_r", [P, KD, NE])
        keys_out = bwd_decay[:].rearrange("p h t -> p (h t)")

        def c_(name):
            a, b = CONST_AT[name]
            return const[:, a:b]

        ident = c_("ident")
        ones = c_("ones")

        zT = dense[:, 0:24 * T].rearrange("p (c t) -> p c t", t=T)
        AQ, AK, BQ, BK, CQ, CK, CG = 0, 4, 8, 12, 16, 18, 20
        v_rows = dense[:, 24 * T:24 * T + 9 * SLAB].rearrange("p (m b e) -> p m b e", m=3, b=NBLK)
        assert 24 * T + 9 * SLAB == 13824
        mod_rows = square[:].rearrange("p u t -> p (u t)")
        kc_rows = probs[:].rearrange("p a b t -> p (a b t)")[:, 0:2 * SLAB]
        vc_rows = merged[:].rearrange("p k t -> p (k t)")[:, 0:2 * SLAB]
        av_c = merged[:].rearrange("p k t -> p (k t)")[:, 0:SLAB]
        bv_c = merged[:].rearrange("p k t -> p (k t)")[:, SLAB:2 * SLAB]
        akc_rows = probs[:].rearrange("p a b t -> p (a b t)")[:, 0:SLAB]
        bkc_rows = probs[:].rearrange("p a b t -> p (a b t)")[:, SLAB:2 * SLAB]
        bias1 = merged[:].rearrange("p k t -> p (k t)")[:, 2 * SLAB:6 * SLAB].rearrange("p (r c) -> p r c", c=GRID_W)
        bias = [bias0, bias1]
        ctx_state = bias0[:].rearrange("p r c -> p (r c)")[:, 0:SLAB].rearrange("p (d c e) -> p d c e", d=2, c=2)
        q_dec = probs[:].rearrange("p a b t -> p (a b t)")[:, 0:1024].rearrange("p (d c t) -> p d c t", d=2, c=2)
        k_dec = probsT[:].rearrange("p a b t -> p (a b t)")[:, 0:1024].rearrange("p (n e) -> p n e", n=4)
        att = tmp
        gate_e = [x[:].rearrange("p a b t -> p (a b t)")[:, 1024:1024 + T] for x in (probs, probsT)]
        a_free = v_rows[:, 0].rearrange("p b e -> p (b e)")
        c_raw = a_free[:, 0:2 * T].rearrange("p (u t) -> p u t", u=2)
        c_rs = a_free[:, 2 * T:4 * T].rearrange("p (u t) -> p u t", u=2)
        cg_sig = v_rows[:, 1].rearrange("p b e -> p (b e)")[:, 0:4 * T]
        h_rows = dense[:, 0:3072].rearrange("p (b d) -> p b d", b=NBLK)
        acc = dense[:, 3072:6144].rearrange("p (k t) -> p k t", k=KD)
        at = 6144

        def carve(n):
            nonlocal at
            at += n
            return dense[:, at - n:at]

        pick = carve(2 * NBLK * HALF).rearrange("p (u b s) -> p u b s", u=2, b=NBLK)
        pick_g = carve(2 * NBLK * P).rearrange("p (u b s) -> p u b s", u=2, b=NBLK)
        pick_gT = carve(T)
        xg = carve(SLAB)
        xgT = carve(SLAB).rearrange("p (q h s) -> p q h s", q=4, h=2)
        act = carve(SLAB)
        hid = carve(SLAB)
        hidT = carve(SLAB).rearrange("p (q h s) -> p q h s", q=4, h=2)
        out_rows = carve(SLAB)
        aff = carve(NBLK * NE).rearrange("p (b e) -> p b e", b=NBLK)
        slot_of = carve(NBLK * NE).rearrange("p (b e) -> p b e", b=NBLK)
        affT = carve(T)
        left = carve(T)
        chosen = carve(T)
        place = carve(T)
        best = carve(8)
        assert at <= 13824

        psum = ctx.enter_context(nc.psum_tensor("psum", [P, 8, SLAB], F32))
        Z = [0, 1]
        S = [2, 3]
        TR = [4, 7]
        O = [5, 6]

        slab_in = [sem(f"slab_in{i}") for i in range(RING)]
        rows_in = sem("rows_in")
        small_in = sem("small_in")
        cache_in = sem("cache_in")
        state_in = sem("state_in")
        bias_in = sem("bias_in")
        stored = sem("stored")
        act_link = sem("act_link")
        dve_link = sem("dve_link")
        pool_link = sem("pool_link")
        x_tr = sem("x_tr")
        x_ev = sem("x_ev")
        c_ready = sem("c_ready")
        c_zero = sem("c_zero")
        vec_tr = sem("vec_tr")
        vec_ready = sem("vec_ready")
        lam_sum = sem("lam_sum")
        lam_exp = sem("lam_exp")
        lam_ready = sem("lam_ready")
        abs_ready = sem("abs_ready")
        ln_ready = sem("ln_ready")
        decay_ready = sem("decay_ready")
        decay_exp = sem("decay_exp")
        in_decay_ready = sem("in_decay_ready")
        chunk_ready = sem("chunk_ready")
        sq_ready = sem("sq_ready")
        sq_used = sem("sq_used")
        rs_ready = sem("rs_ready")
        mod1_ready = sem("mod1_ready")
        norm_mul = sem("norm_mul")
        h_ready = sem("h_ready")
        z_full = sem("z_full")
        z_read = sem("z_read")
        rot_full = sem("rot_full")
        rope_done = sem("rope_done")
        kc_tr = sem("kc_tr")
        kc_ev = sem("kc_ev")
        ko_tr = sem("ko_tr")
        ko_ev = sem("ko_ev")
        ko_st = sem("ko_st")
        bias_ready = sem("bias_ready")
        s_full = sem("s_full")
        s_max = sem("s_max")
        s_exp = sem("s_exp")
        p_ready = sem("p_ready")
        pT_full = sem("pT_full")
        pT_act = sem("pT_act")
        pT_dve = sem("pT_dve")
        o_full = sem("o_full")
        o_read = sem("o_read")
        nsum = sem("nsum")
        nrs = sem("nrs")
        a_done = sem("a_done")
        kr_tr = sem("kr_tr")
        kr_ev = sem("kr_ev")
        qd_ready = sem("qd_ready")
        st_full = sem("st_full")
        st_ev = sem("st_ev")
        st1_ready = sem("st1_ready")
        att_full = sem("att_full")
        att_ready = sem("att_ready")
        co_full = sem("co_full")
        co_read = sem("co_read")
        cmean_full = sem("cmean_full")
        ccen = sem("ccen")
        csq = sem("csq")
        cvar_full = sem("cvar_full")
        crs = sem("crs")
        cgate = sem("cgate")
        c_done = sem("c_done")
        gate_full = sem("gate_full")
        gate_exp = sem("gate_exp")
        br_full = sem("br_full")
        br_read = sem("br_read")
        mod2_ready = sem("mod2_ready")
        w_full = sem("w_full")
        w_read = sem("w_read")
        lg_full = sem("lg_full")
        lg_max = sem("lg_max")
        lg_exp = sem("lg_exp")
        aff_ready = sem("aff_ready")
        affT_full = sem("affT_full")
        slots_ready = sem("slots_ready")
        slots_tr = sem("slots_tr")
        slots_ev = sem("slots_ev")
        hr_tr = sem("hr_tr")
        hr_ev = sem("hr_ev")
        v_stored = sem("v_stored")
        acc_zero = sem("acc_zero")
        a_sq = sem("a_sq")
        crs_read = sem("crs_read")
        cg_exp = sem("cg_exp")
        pick_ready = sem("pick_ready")
        xg_full = sem("xg_full")
        xg_read = sem("xg_read")
        xt_full = sem("xt_full")
        xt_read = sem("xt_read")
        ht_full = sem("ht_full")
        ht_read = sem("ht_read")
        pgT_full = sem("pgT_full")
        pgT_read = sem("pgT_read")
        gate_h = sem("gate_h")
        up_h = sem("up_h")
        silu_ready = sem("silu_ready")
        hid_ready = sem("hid_ready")
        down_full = sem("down_full")
        down_read = sem("down_read")
        sc_full = sem("sc_full")
        sc_read = sem("sc_read")

        V, A_, G, M = nc.vector, nc.scalar, nc.gpsimd, nc.tensor

        def chain(eng, s):
            n = 0

            def then(ins):
                nonlocal n
                n += 1
                ins.then_inc(s, 1)
                eng.wait_ge(s, n)
            return then

        def clear_all():
            with nc.Block() as block:
                @block.sync
                def _(sp):
                    for s in sems:
                        sp.sem_clear(s)

        def transpose(out, in_):
            n = in_.shape[0]
            return M.matmul(out, in_, ident[0:n, 0:n], start=True, stop=True, is_transpose=True)

        x_in = hT[:].rearrange("p k t -> p (k t)").rearrange("p (b d) -> p b d", b=NBLK)
        with nc.Block() as block:
            @block.sync
            def _(sp):
                sp.dma_start(const[:], const_in).then_inc(rows_in, 16)
                sp.dma_start(x_in, x_rows.rearrange("(b p) d -> p b d", p=P)).then_inc(rows_in, 16)
                sp.dma_start(vec_rows[0:2 * KD, :], cvec.rearrange("g (k p) -> (g k) p", p=P)).then_inc(rows_in, 16)

            @block.tensor
            def _(pe):
                pe.wait_ge(rows_in, 48)
                for k in range(KD):
                    if k >= 4:
                        pe.wait_ge(x_ev, k - 3)
                    for b in range(NBLK):
                        last = transpose(psum[:, k % 4, b * P:(b + 1) * P], x_in[:, b, k * P:(k + 1) * P])
                    last.then_inc(x_tr, 1)
                transpose(psum[:, 4, 0:2 * KD], vec_rows[0:2 * KD, :]).then_inc(vec_tr, 1)

            @block.vector
            def _(dve):
                for k in range(KD):
                    dve.wait_ge(x_tr, k + 1)
                    V.tensor_copy(xT[:, k, :], psum[:, k % 4, 0:T]).then_inc(x_ev, 1)

            @block.gpsimd
            def _(pool):
                G.memset(silu_c[:], 0.0).then_inc(c_zero, 1)

            @block.scalar
            def _(sc):
                sc.wait_ge(vec_tr, 1)
                sc.wait_ge(c_zero, 1)
                A_.activation(silu_c[:, :, 0:2].rearrange("p k g -> p g k"),
                              psum[:, 4, 0:2 * KD].rearrange("p (g k) -> p g k", g=2), ACT.Silu).then_inc(c_ready, 1)
        clear_all()

        with nc.Fori(0, DEPTH) as layer:
            with nc.Block() as block:
                def f_of_z(g):
                    return 5 + g if g < 25 else (31 + 2 * (g - 25) if g < 29 else 38 + g - 29)

                def f_of_norm(t):
                    return 30 + 2 * t

                def f_of_mod(j):
                    return j if j < 4 else 42 + (j - 4) + (j - 4) // 4

                def f_of_modT(i):
                    return f_of_mod(4 * i + 3) + 1

                FILLERS = f_of_modT(2) + 1
                Z_GROUPS = ([(0, j, "T") for j in range(4)] + [(1, j, "T") for j in range(4)]
                            + [(2, j, "rows") for j in range(NBLK)]
                            + [(3, j, "T") for j in range(4)] + [(4, j, "T") for j in range(4)]
                            + [(5, j, "rows") for j in range(NBLK)]
                            + [(6, j, "T") for j in range(4)] + [(7, j, "rows") for j in range(NBLK)]
                            + [(8, j, "T") for j in range(4)])
                UNITS = 12
                A_STEPS = UNITS + 2

                def slab_source(n):
                    def cols(w, j):
                        return w[layer].rearrange("(k p) n -> p k n", p=P)[:, :, j * SLAB:(j + 1) * SLAB]
                    if n < 4:
                        return cols(w_mod, n)
                    if n < 13:
                        return cols(w_in, n - 4)
                    if n < 21:
                        return cols(w_mod, n - 9)
                    if n < 30:
                        branch, which = divmod(n - 21, 3)
                        if which == 1:
                            return [w_pa, w_pb, w_pc][branch][layer].rearrange("(k p) n -> p k n", p=P)
                        return cols(w_in, 9 + 2 * branch + which // 2)
                    return cols(w_out, n - 30)

                def slab_into(n):
                    if 21 <= n < 30 and (n - 21) % 3 == 1:
                        return ring[:, n % RING].rearrange("p k n -> p (k n)").rearrange("p (k n) -> p k n", k=4)
                    return ring[:, n % RING]

                def wait_slab_free(eng, n):
                    if n < 4:
                        eng.wait_ge(z_full, f_of_mod(n) + 1)
                    elif n < 13:
                        last_group = max(g for g, (slab, _, _) in enumerate(Z_GROUPS) if slab == n - 4)
                        eng.wait_ge(z_full, f_of_z(last_group) + 1)
                    elif n < 21:
                        eng.wait_ge(z_full, f_of_mod(n - 9) + 1)
                    elif n < 30:
                        branch, which = divmod(n - 21, 3)
                        if which == 1:
                            eng.wait_ge(br_full, KD * (branch + 1))
                        else:
                            eng.wait_ge(gate_full, KD * branch + (4 if which == 0 else 8))
                    else:
                        eng.wait_ge(w_full, 4 * (n - 29))

                @block.sync
                def _(sp):
                    for n in range(DENSE_SLABS):
                        if n >= RING:
                            wait_slab_free(sp, n - RING)
                        sp.dma_start(slab_into(n), slab_source(n)).then_inc(slab_in[n % RING], 16)

                    def load(pair, j):
                        e, s = divmod(j, EXPERT_SLABS)
                        w = (w_gate, w_up, w_down)[s // 2]
                        sp.dma_start(ring[:, j % RING],
                                     w[layer, pair * 2 + e].rearrange("(k p) n -> p k n", p=P)[:, :, (s % 2) * SLAB:(s % 2 + 1) * SLAB]
                                     ).then_inc(slab_in[j % RING], 16)

                    def wait_free(pair, j):
                        e, s = divmod(j, EXPERT_SLABS)
                        sp.wait_ge((gate_h, up_h, down_full)[s // 2], pair * 4 + (2 * e + s % 2 + 1))

                    for j in range(RING):
                        wait_slab_free(sp, DENSE_SLABS - RING + j)
                        load(0, j)
                    with sp.Fori(0, NE // 2 - 1) as pair:
                        for j in range(RING, 2 * EXPERT_SLABS + RING):
                            wait_free(pair, j - RING)
                            if j < 2 * EXPERT_SLABS:
                                load(pair, j)
                            else:
                                load(pair + 1, j - 2 * EXPERT_SLABS)
                    for j in range(RING, 2 * EXPERT_SLABS):
                        wait_free(NE // 2 - 1, j - RING)
                        load(NE // 2 - 1, j)

                @block.gpsimd
                def _(pool):
                    link = chain(pool, pool_link)
                    pool.wait_ge(decay_exp, 1)
                    four = [P, 4, P]
                    link(G.tensor_tensor(in_decay[:], in_decay[:], c_("is_below").unsqueeze(1).to_broadcast(four), ALU.mult))
                    link(G.tensor_tensor(bwd_decay[:], bwd_decay[:], c_("is_above").unsqueeze(1).to_broadcast(four), ALU.mult))
                    G.tensor_tensor(in_decay[:], in_decay[:], bwd_decay[:], ALU.add).then_inc(in_decay_ready, 1)
                    pool.wait_ge(bias_in, 64)
                    for b in bias:
                        v = b if b is bias1 else b[:]
                        G.tensor_tensor(v, v, c_("window").unsqueeze(1).to_broadcast([P, 32, GRID_W]), ALU.add).then_inc(bias_ready, 1)
                    pool.wait_ge(w_full, KD)
                    G.memset(acc, 0.0).then_inc(acc_zero, 1)

                @block.tensor
                def _(pe):
                    def slab_here(n):
                        pe.wait_ge(slab_in[n % RING], 16 * (n // RING + 1))

                    def bank_free(f):
                        if f >= 2:
                            pe.wait_ge(z_read, f - 1)
                        return Z[f % 2]

                    def norm_sum(bank, first):
                        for k in range(KD):
                            pe.wait_ge(sq_ready, first + k + 1)
                            M.matmul(psum[:, bank, 0:T], ones, square[:, k % 2, :], start=k == 0, stop=k == KD - 1).then_inc(sq_used, 1)

                    def mod_slab(j):
                        n = j if j < 4 else j + 9
                        f = f_of_mod(j)
                        slab_here(n)
                        bank = bank_free(f)
                        for k in range(KD):
                            for q in range(4):
                                last = M.matmul(psum[32 * q:32 * q + 32, bank, 0:P], silu_c[:, k, :],
                                                ring[:, n % RING, k, q * P:(q + 1) * P], start=k == 0, stop=k == KD - 1)
                        last.then_inc(z_full, 1)

                    def mod_transposed(i):
                        f = f_of_modT(i)
                        pe.wait_ge(z_read, f)
                        for j in range(4):
                            last = transpose(psum[:, Z[f % 2], j * P:(j + 1) * P], mod_rows[:, j * P:(j + 1) * P])
                        last.then_inc(z_full, 1)

                    def z_group(g):
                        slab, j, kind = Z_GROUPS[g]
                        n = 4 + slab
                        f = f_of_z(g)
                        if j == 0:
                            slab_here(n)
                        bank = bank_free(f)
                        cols = slice(j * P, (j + 1) * P)
                        for k in range(KD):
                            if kind == "T":
                                last = M.matmul(psum[:, bank, 0:T], ring[:, n % RING, k, cols], hT[:, k, :], start=k == 0, stop=k == KD - 1)
                            else:
                                last = M.matmul(psum[:, bank, :], hT[:, k, cols], ring[:, n % RING, k, :], start=k == 0, stop=k == KD - 1)
                        last.then_inc(z_full, 1)

                    norm_sum(S[0], 0)
                    pe.wait_ge(small_in, 16 * 3)
                    transpose(psum[:, TR[1], 0:72], vec_rows[:, :]).then_inc(vec_tr, 1)
                    pe.wait_ge(cache_in, 32)
                    for rows, bank in ((akc_rows, O[0]), (bkc_rows, O[1])):
                        for c in range(4):
                            last = transpose(psum[:, bank, c * P:(c + 1) * P], rows[:, c * P:(c + 1) * P])
                        last.then_inc(kc_tr, 1)
                    for j in range(4):
                        mod_slab(j)
                    mod_transposed(0)
                    pe.wait_ge(h_ready, KD)
                    for g in range(11):
                        z_group(g)

                    for c in range(8):
                        pe.wait_ge(z_read, f_of_z(c) + 1)
                        if c >= 2:
                            pe.wait_ge(rope_done, c - 1)
                        M.matmul(psum[:, S[c % 2], 0:2 * P], c_("rot"), zT[:, AQ + c, LAT], start=True, stop=True).then_inc(rot_full, 1)

                    def keys_in_rows(first, bank):
                        for c in range(4):
                            last = transpose(psum[:, bank, c * P:(c + 1) * P], zT[:, first + c, CTX])
                        last.then_inc(ko_tr, 1)

                    keys_in_rows(AK, TR[0])
                    pe.wait_ge(rope_done, 8)
                    pe.wait_ge(kc_ev, 2)

                    def scores(n):
                        mixer, u = divmod(n, UNITS)
                        c, b = divmod(u, NBLK)
                        q0, k0 = ((AQ, AK), (BQ, BK))[mixer]
                        kcT = (akcT, bkcT)[mixer]
                        if n >= 1:
                            pe.wait_ge(s_exp, n)
                        for i in range(2):
                            part = slice(64 * i, 64 * i + 64)
                            q = zT[part, q0 + c, b * P:(b + 1) * P]
                            if b == 0:
                                last = M.matmul(psum[:, S[i], 0:P], q, zT[part, k0 + c, CTX], start=True, stop=True)
                            else:
                                M.matmul(psum[:, S[i], 0:2 * P], q, zT[part, k0 + c, LAT], start=True, stop=True)
                                last = M.matmul(psum[:, S[i], 2 * P:T], q, kcT[part, c, :], start=True, stop=True)
                        last.then_inc(s_full, 1)

                    def probs_transposed(n):
                        mixer, u = divmod(n, UNITS)
                        tiles = 1 if u % NBLK == 0 else 3
                        pe.wait_ge(p_ready, n + 1)
                        if n == 0:
                            pe.wait_ge(ko_ev, 1)
                        else:
                            pe.wait_ge(pT_act, n)
                        if n > UNITS:
                            pe.wait_ge(pT_dve, n - UNITS)
                        for i in range(1 + mixer):
                            for m in range(tiles):
                                last = transpose(psum[:, TR[i], m * P:(m + 1) * P], probs[:, n % 2, i, m * P:(m + 1) * P])
                        last.then_inc(pT_full, 1)

                    def values(n):
                        mixer, u = divmod(n, UNITS)
                        c, b = divmod(u, NBLK)
                        head = 4 * mixer + c
                        pe.wait_ge(pT_act, n + 1)
                        if mixer:
                            pe.wait_ge(pT_dve, n + 1 - UNITS)
                        if b == 0 and head >= 2:
                            pe.wait_ge(o_read, head - 1)
                        elif n == 0:
                            pe.wait_ge(kc_ev, 2)
                        cached = (av_c, bv_c)[mixer]
                        tiles = [(v_rows[:, mixer, 0], 0)] if b == 0 else [
                            (v_rows[:, mixer, 1], 0), (v_rows[:, mixer, 2], 1), (cached, 2)]
                        out = psum[:, O[head % 2], b * P:(b + 1) * P]
                        for v, m in tiles:
                            keys = slice(m * P, (m + 1) * P)
                            if mixer == 0:
                                last = M.matmul(out, v[:, c * P:(c + 1) * P], probsT[:, n % 2, 0, keys], start=m == 0, stop=m == len(tiles) - 1)
                            else:
                                for i in range(2):
                                    last = M.matmul(out[64 * i:64 * i + 64], v[:, (2 * c + i) * 64:(2 * c + i + 1) * 64],
                                                    probsT[:, n % 2, i, keys], start=m == 0, stop=m == len(tiles) - 1)
                        last.then_inc(o_full, 1)

                    for t in range(A_STEPS):
                        if t < UNITS:
                            scores(t)
                        if 1 <= t <= UNITS:
                            probs_transposed(t - 1)
                        if t >= 2:
                            values(t - 2)
                        z_group(11 + t)
                    for t in range(A_STEPS):
                        if t < UNITS:
                            scores(UNITS + t)
                        if 1 <= t <= UNITS:
                            probs_transposed(UNITS + t - 1)
                        if t >= 2:
                            values(UNITS + t - 2)
                        if t < 4:
                            f = f_of_norm(t)
                            pe.wait_ge(a_sq, t + 1)
                            M.matmul(psum[:, bank_free(f), 0:T], ones, square[:, t % 2, :], start=True, stop=True).then_inc(z_full, 1)
                        if t < 8:
                            z_group(25 + t)
                        elif t < 12:
                            mod_slab(t - 4)
                        elif t == 12:
                            mod_transposed(1)
                        else:
                            mod_slab(8)
                    for j in range(9, 12):
                        mod_slab(j)
                    mod_transposed(2)

                    pe.wait_ge(pT_act, 2 * UNITS)
                    keys_in_rows(BK, TR[0])
                    for b in range(NBLK):
                        for c in range(2):
                            last = transpose(psum[:, S[b // 2], (b % 2) * 2 * P + c * P:(b % 2) * 2 * P + (c + 1) * P],
                                             zT[:, CK + c, b * P:(b + 1) * P])
                    last.then_inc(kr_tr, 1)
                    pe.wait_ge(ko_ev, 2)
                    pe.wait_ge(pT_dve, UNITS)
                    pe.wait_ge(kr_ev, 4)
                    for kind, b in ((0, 0), (1, 0), (2, 1), (3, 2)):
                        for h in range(HEADS_C):
                            c, i = divmod(h, 2)
                            last = M.matmul(psum[64 * i:64 * i + 64, TR[kind // 2], (kind % 2) * 2 * P + c * P:(kind % 2) * 2 * P + (c + 1) * P],
                                            k_dec[:, kind, h * 64:(h + 1) * 64], v_rows[:, 2, b, h * P:(h + 1) * P], start=True, stop=True)
                        if kind % 2:
                            last.then_inc(st_full, 1)

                    def c_att(h):
                        c, i = divmod(h, 2)
                        part = slice(64 * i, 64 * i + 64)
                        if h >= 2:
                            pe.wait_ge(att_ready, h - 1)
                        for b in range(NBLK):
                            blk = slice(b * P, (b + 1) * P)
                            last = M.matmul(psum[:, S[h % 2], blk], zT[part, CK + c, blk], zT[part, CQ + c, blk], start=True, stop=True)
                        last.then_inc(att_full, 1)

                    def c_out(h):
                        c, i = divmod(h, 2)
                        part = slice(64 * i, 64 * i + 64)
                        pe.wait_ge(att_ready, h + 1)
                        if h == 0:
                            pe.wait_ge(st1_ready, 4)
                            pe.wait_ge(qd_ready, 4)
                            pe.wait_ge(o_read, 8)
                        if h >= 2:
                            pe.wait_ge(co_read, h - 1)
                        for b in range(NBLK):
                            out = psum[:, O[h % 2], b * P:(b + 1) * P]
                            last = M.matmul(out, v_rows[:, 2, b, h * P:(h + 1) * P], att[:, h % 2, b * P:(b + 1) * P], start=True, stop=b == 0)
                            if b:
                                for d in range(2):
                                    state = state0 if (b == 1) == (d == 0) else state1
                                    last = M.matmul(out, state[part, d, c, :], q_dec[part, d, c, (b - 1) * P:b * P], start=False, stop=d == 1)
                        last.then_inc(co_full, 1)

                    def c_mean(h):
                        if h == 0:
                            pe.wait_ge(st_ev, 1)
                        pe.wait_ge(co_read, h + 1)
                        if h >= 1:
                            pe.wait_ge(ccen, h)
                        M.matmul(psum[:, TR[0], 0:T], ones, c_raw[:, h % 2, :], start=True, stop=True).then_inc(cmean_full, 1)

                    def c_var(h):
                        pe.wait_ge(csq, h + 1)
                        if h >= 1:
                            pe.wait_ge(crs, h)
                        M.matmul(psum[:, TR[1], 0:T], ones, square[:, h % 2, :], start=True, stop=True).then_inc(cvar_full, 1)

                    for m in range(3 * KD):
                        branch, j = divmod(m, KD)
                        if m < HEADS_C:
                            c_att(m)
                        if 1 <= m <= HEADS_C:
                            c_out(m - 1)
                        if 2 <= m <= HEADS_C + 1:
                            c_mean(m - 2)
                        if 3 <= m <= HEADS_C + 2:
                            c_var(m - 3)
                        n_gate = 21 + 3 * branch + (0 if j < 4 else 2)
                        n_proj = 22 + 3 * branch
                        if j % 4 == 0:
                            slab_here(n_gate)
                        if m == 0:
                            pe.wait_ge(z_read, FILLERS)
                        else:
                            pe.wait_ge(gate_exp, m)
                        bank = Z[1]
                        for k in range(KD):
                            last = M.matmul(psum[:, bank, 0:T], ring[:, n_gate % RING, k, (j % 4) * P:(j % 4 + 1) * P], hT[:, k, :],
                                            start=k == 0, stop=k == KD - 1)
                        last.then_inc(gate_full, 1)
                        if j == 0:
                            slab_here(n_proj)
                            if branch == 0:
                                pe.wait_ge(a_done, 4)
                            if branch == 2:
                                pe.wait_ge(c_done, 4)
                        if m >= 1:
                            pe.wait_ge(br_read, m)
                        w = slab_into(n_proj)
                        source = (AQ, BQ, CG)[branch]
                        for k in range(4):
                            last = M.matmul(psum[:, Z[0], 0:T], w[:, k, j * P:(j + 1) * P], zT[:, source + k, :], start=k == 0, stop=k == 3)
                        last.then_inc(br_full, 1)

                    for j in range(KD):
                        if j % 4 == 0:
                            slab_here(30 + j // 4)
                        if j == 0:
                            pe.wait_ge(br_read, 3 * KD)
                        if j >= 2:
                            pe.wait_ge(w_read, j - 1)
                        for k in range(KD):
                            last = M.matmul(psum[:, S[j % 2], 0:T], ring[:, (30 + j // 4) % RING, k, (j % 4) * P:(j % 4 + 1) * P], merged[:, k, :],
                                            start=k == 0, stop=k == KD - 1)
                        last.then_inc(w_full, 1)

                    norm_sum(TR[0], KD)
                    pe.wait_ge(h_ready, 2 * KD)
                    for b in range(NBLK):
                        for k in range(KD):
                            last = M.matmul(psum[:, TR[1], b * NE:(b + 1) * NE], hT[:, k, b * P:(b + 1) * P], w_r[:, k, :], start=k == 0, stop=k == KD - 1)
                    last.then_inc(lg_full, 1)
                    for n in range(2 * NBLK):
                        if n >= 2:
                            pe.wait_ge(hr_ev, n - 1)
                        for q in range(4):
                            last = transpose(psum[:, O[n % 2], q * P:(q + 1) * P], hT[:, (n % 2) * 4 + q, (n // 2) * P:(n // 2 + 1) * P])
                        last.then_inc(hr_tr, 1)
                    pe.wait_ge(aff_ready, 1)
                    for b in range(NBLK):
                        last = transpose(psum[0:NE, S[0], b * P:(b + 1) * P], aff[:, b, :])
                    last.then_inc(affT_full, 1)
                    pe.wait_ge(slots_ready, 1)
                    for b in range(NBLK):
                        last = transpose(psum[:, S[1], b * NE:(b + 1) * NE], place[0:NE, b * P:(b + 1) * P])
                    last.then_inc(slots_tr, 1)
                    pe.wait_ge(hr_ev, 2 * NBLK)

                    def gather(e, expert):
                        pe.wait_ge(pick_ready, expert + 1)
                        for b in range(NBLK):
                            for half in range(2):
                                last = M.matmul(psum[HALF * half:HALF * (half + 1), O[0], :], pick[:, e, b, :],
                                                h_rows[:, b, half * SLAB:(half + 1) * SLAB], start=b == 0, stop=b == NBLK - 1)
                        last.then_inc(xg_full, 1)
                        pe.wait_ge(xg_read, expert + 1)
                        for q in range(4):
                            last = transpose(psum[:, O[1], q * P:(q + 1) * P], xg[:, q * P:(q + 1) * P])
                        last.then_inc(xt_full, 1)

                    def expert_step(pair, e, last_expert):
                        def nth(per_expert, x):
                            return pair * (2 * per_expert) + (e * per_expert + x)

                        def product(s, bank, signal, lhs):
                            j = e * EXPERT_SLABS + s
                            pe.wait_ge(slab_in[j % RING], pair * (16 * 3) + 16 * (DENSE_SLABS // RING + j // RING + 1))
                            for k in range(KD):
                                for half in range(2):
                                    last = M.matmul(psum[HALF * half:HALF * (half + 1), bank, (s % 2) * 256:(s % 2 + 1) * 256], lhs(k),
                                                    ring[:, j % RING, k, half * 256:(half + 1) * 256], start=k == 0, stop=k == KD - 1)
                            last.then_inc(signal, 1)

                        pe.wait_ge(xt_read, nth(1, 1))
                        for s in range(4):
                            product(s, S[s // 2], (gate_h, up_h)[s // 2], lambda k: xgT[:, k % 4, k // 4, :])
                        if last_expert:
                            pe.wait_ge(sc_read, KD * (NE - 1))
                        else:
                            gather(1 - e, pair * 2 + (e + 1))
                        pe.wait_ge(hid_ready, nth(1, 1))
                        for q in range(4):
                            last = transpose(psum[:, TR[0], q * P:(q + 1) * P], hid[:, q * P:(q + 1) * P])
                        last.then_inc(ht_full, 1)
                        for b in range(NBLK):
                            last = transpose(psum[:, O[0], b * P:(b + 1) * P], pick_g[:, e, b, :])
                        last.then_inc(pgT_full, 1)
                        pe.wait_ge(ht_read, nth(1, 1))
                        for s in range(4, 6):
                            product(s, TR[1], down_full, lambda k: hidT[:, 2 * (k // 4) + k % 2, (k // 2) % 2, :])
                        pe.wait_ge(down_read, nth(1, 1))
                        pe.wait_ge(pgT_read, nth(1, 1))
                        if not last_expert:
                            pe.wait_ge(xt_read, nth(1, 2))
                        for q in range(4):
                            if q >= 2:
                                pe.wait_ge(sc_read, nth(KD, 2 * (q - 1)))
                            for half in range(2):
                                part = slice(HALF * half, HALF * (half + 1))
                                M.matmul(psum[:, (Z, O)[q % 2][half], 0:T], out_rows[part, q * P:(q + 1) * P], pick_gT[part, :],
                                         start=True, stop=True).then_inc(sc_full, 1)

                    gather(0, 0)
                    with pe.Fori(0, NE // 2 - 1) as pair:
                        for e in range(2):
                            expert_step(pair, e, False)
                    for e in range(2):
                        expert_step(NE // 2 - 1, e, e == 1)

                @block.scalar
                def _(sc):
                    for dst, src in ((vec_rows[:], layer_vectors[layer]),
                                     (layer_rows[:], bass.AP(layer_scalars.tensor, layer_scalars.offset + layer * 266, [[0, P], [1, 266]])),
                                     (w_r[:], w_router[layer].rearrange("(k p) e -> p k e", p=P))):
                        sc.dma_start(dst, src).then_inc(small_in, 16)
                    sc.dma_start(kc_rows, cache_k[layer]).then_inc(cache_in, 16)
                    sc.dma_start(vc_rows, cache_v[layer]).then_inc(cache_in, 16)
                    link = chain(sc, act_link)

                    def squares(first):
                        for k in range(KD):
                            if first + k >= 2:
                                sc.wait_ge(sq_used, first + k - 1)
                            if first:
                                sc.wait_ge(w_read, k + 1)
                            A_.activation(square[:, k % 2, :], xT[:, k, :], ACT.Square).then_inc(sq_ready, 1)

                    def inverse_rms(bank, n):
                        sc.wait_ge(sq_used, n)
                        link(A_.activation(rs[:], psum[:, bank, 0:T], ACT.Ln, scale=1.0 / D, bias=c_("eps")))
                        A_.activation(rs[:], rs[:], ACT.Exp, scale=-0.5).then_inc(rs_ready, 1)

                    def modulate(first, scale, shift):
                        for k in range(KD):
                            sc.wait_ge(norm_mul, first + k + 1)
                            for g, cols in enumerate((CTX, LAT)):
                                last = A_.activation(hT[:, k, cols], tmp[:, k % 2, cols], ACT.Identity,
                                                     bias=modT[:, shift + k, g:g + 1], scale=scale[:, k, g:g + 1])
                            last.then_inc(h_ready, 1)

                    A_.preload_act_table_set("natural_log_exp_and_others")
                    squares(0)
                    inverse_rms(S[0], KD)
                    for d, src in enumerate((state_f, state_b)):
                        sc.dma_start(state0[:, d], src[layer].rearrange("(c i) k e -> (i k) c e", c=2)).then_inc(state_in, 16)
                    for b in range(2):
                        for half in range(2):
                            q_row = 2 * b + half
                            skew = bass.AP(rpb_rev.tensor,
                                           rpb_rev.offset + layer * (HEADS_B * RPB_ROWS * RPB_COLS) + ((7 - q_row) * HEADS_B * RPB_COLS + 15 - (GRID_W - 1)),
                                           [[1, GRID_W], [RPB_COLS, 4 * HEADS_B], [1, GRID_W]])
                            dst = (bias[b] if b else bias[b][:])[GRID_W * half:GRID_W * (half + 1)]
                            sc.dma_start(dst, skew).then_inc(bias_in, 16)

                    sc.wait_ge(lam_sum, 1)
                    A_.activation(lamb[:, 2:4], lamb[:, 0:2], ACT.Exp).then_inc(lam_exp, 1)
                    sc.wait_ge(abs_ready, 1)
                    link(A_.activation(decay_t[:, 1], decay_t[:, 0], ACT.Exp, scale=-1.0))
                    A_.activation(decay_t[:, 2], decay_t[:, 1], ACT.Ln, bias=c_("one")).then_inc(ln_ready, 1)
                    sc.wait_ge(decay_ready, 1)
                    for h in range(HEADS_C):
                        A_.activation(in_decay[:, h], c_("below"), ACT.Exp, scale=decay[:, h:h + 1])
                        last = A_.activation(bwd_decay[:, h], c_("above"), ACT.Exp, scale=decay[:, 4 + h:5 + h])
                    last.then_inc(decay_exp, 1)
                    for d, (row, col) in enumerate((("since", "k_until"), ("until", "k_since"))):
                        for c in range(2):
                            for i in range(2):
                                part = slice(64 * i, 64 * i + 64)
                                h = 4 * d + 2 * c + i
                                A_.activation(q_decay[part, d, c, :], c_(row)[part], ACT.Exp, scale=decay[part, h:h + 1])
                        A_.activation(k_decay[:, d, :], decay[:, 4 * d:4 * d + 4], ACT.Exp, scale=c_(col))
                    for i in range(2):
                        part = slice(64 * i, 64 * i + 64)
                        last = A_.activation(chunk_decay[part], decay[part].rearrange("p (d c i) -> p d c i", d=2, c=2)[:, :, :, i],
                                             ACT.Exp, scale=float(P))
                    last.then_inc(chunk_ready, 1)
                    for n, (dst, bank) in enumerate(((akcT, O[0]), (bkcT, O[1]))):
                        sc.wait_ge(kc_tr, n + 1)
                        A_.activation(dst[:].rearrange("p c t -> p (c t)"), psum[:, bank, :], ACT.Copy).then_inc(kc_ev, 1)

                    def read_mod(j):
                        f = f_of_mod(j)
                        sc.wait_ge(z_full, f + 1)
                        at = (j % 4) * P
                        A_.activation(mod_rows[:, at:at + P], psum[:, Z[f % 2], 0:P], ACT.Copy).then_inc(z_read, 1)

                    def read_modT(i):
                        f = f_of_modT(i)
                        sc.wait_ge(z_full, f + 1)
                        A_.activation(modT[:, 16 * i:16 * (i + 1), :], psum[:, Z[f % 2], :].rearrange("p (c w) -> p c w", w=32)[:, :, 0:2],
                                      ACT.Copy).then_inc(z_read, 1)

                    def read_z(g):
                        slab, j, kind = Z_GROUPS[g]
                        f = f_of_z(g)
                        sc.wait_ge(z_full, f + 1)
                        if kind == "rows":
                            mixer = {2: 0, 5: 1, 7: 2}[slab]
                            A_.activation(v_rows[:, mixer, j, :], psum[:, Z[f % 2], :], ACT.Copy).then_inc(z_read, 1)
                        else:
                            chunk = {0: AQ, 1: AK, 3: BQ, 4: BK, 6: CQ, 8: CG}[slab] + j
                            s = SCALE if chunk in (CK, CK + 1) else 1.0
                            A_.activation(zT[:, chunk, :], psum[:, Z[f % 2], 0:T], ACT.Copy, scale=s).then_inc(z_read, 1)

                    for j in range(4):
                        read_mod(j)
                    read_modT(0)
                    sc.wait_ge(mod1_ready, 1)
                    modulate(0, scale_mix, 0)
                    for g in range(11):
                        read_z(g)
                    sc.wait_ge(z_read, f_of_z(10) + 1)
                    sc.dma_start(new_av[layer], v_rows[:, 0, 0, :]).then_inc(v_stored, 16)
                    sc.wait_ge(ko_tr, 1)
                    sc.wait_ge(in_decay_ready, 1)
                    A_.activation(keys_out, psum[:, TR[0], :], ACT.Copy).then_inc(ko_ev, 1)
                    sc.wait_ge(ko_ev, 1)
                    sc.dma_start(new_ak[layer], keys_out).then_inc(ko_st, 16)

                    def exps(n):
                        mixer, u = divmod(n, UNITS)
                        b = u % NBLK
                        keys = P if b == 0 else T
                        own = mixer == 0 or b == 0
                        sc.wait_ge(s_max, n + 1)
                        if own and n >= 2:
                            sc.wait_ge(pT_full, n - 1)
                        for i in range(2):
                            dst = probs[:, n % 2, i, 0:keys]
                            last = A_.activation(dst, psum[:, S[i], 0:keys] if own else dst, ACT.Exp,
                                                 bias=small[:, n % 2, i:i + 1], scale=SCALE if own else 1.0,
                                                 accum_out=small[:, n % 2, 2 + i:3 + i])
                        last.then_inc(s_exp, 1)

                    def read_pT(n):
                        keys = P if n % NBLK == 0 else T
                        sc.wait_ge(pT_full, n + 1)
                        if n >= 2:
                            sc.wait_ge(o_full, n - 1)
                        A_.activation(probsT[:, n % 2, 0, 0:keys], psum[:, TR[0], 0:keys], ACT.Copy).then_inc(pT_act, 1)

                    def read_o(n):
                        mixer, u = divmod(n, UNITS)
                        if u % NBLK == NBLK - 1:
                            c = u // NBLK
                            sc.wait_ge(o_full, n + 1)
                            A_.activation(zT[:, (AQ, BQ)[mixer] + c, :], psum[:, O[c % 2], 0:T], ACT.Copy).then_inc(o_read, 1)

                    for t in range(A_STEPS):
                        if t < UNITS:
                            exps(t)
                        if 1 <= t <= UNITS:
                            read_pT(t - 1)
                        if t >= 2:
                            read_o(t - 2)
                        read_z(11 + t)
                        if 11 + t == 21:
                            sc.wait_ge(z_read, f_of_z(21) + 1)
                            sc.dma_start(new_bv[layer], v_rows[:, 1, 0, :]).then_inc(v_stored, 16)
                    for t in range(A_STEPS):
                        if t < 4:
                            sc.wait_ge(o_read, t + 1)
                            A_.activation(square[:, t % 2, :], zT[:, AQ + t, :], ACT.Square).then_inc(a_sq, 1)
                        if t < UNITS:
                            exps(UNITS + t)
                        if 1 <= t <= UNITS:
                            read_pT(UNITS + t - 1)
                        if t >= 2:
                            read_o(UNITS + t - 2)
                        if t < 4:
                            f = f_of_norm(t)
                            sc.wait_ge(z_full, f + 1)
                            if t >= 2:
                                sc.wait_ge(a_done, t - 1)
                            A_.activation(tmp[:, t % 2, :], psum[:, Z[f % 2], 0:T], ACT.Ln, scale=1.0 / P, bias=c_("eps")).then_inc(z_read, 1)
                            sc.wait_ge(z_read, f + 1)
                            A_.activation(tmp[:, t % 2, :], tmp[:, t % 2, :], ACT.Exp, scale=-0.5).then_inc(nrs, 1)
                        if t < 8:
                            read_z(25 + t)
                        elif t < 12:
                            read_mod(t - 4)
                        elif t == 12:
                            read_modT(1)
                        else:
                            read_mod(8)
                    for j in range(9, 12):
                        read_mod(j)
                    read_modT(2)

                    sc.wait_ge(ko_tr, 2)
                    sc.wait_ge(ko_st, 16)
                    A_.activation(keys_out, psum[:, TR[0], :], ACT.Copy).then_inc(ko_ev, 1)
                    sc.wait_ge(ko_ev, 2)
                    sc.dma_start(new_bk[layer], keys_out).then_inc(ko_st, 16)
                    sc.wait_ge(v_stored, 32)
                    sc.wait_ge(o_full, 2 * UNITS)
                    sc.wait_ge(z_read, f_of_z(32) + 1)
                    A_.activation(cg_sig, zT[:, CG:CG + 4, :].rearrange("p c t -> p (c t)"), ACT.Exp, scale=-1.0).then_inc(cg_exp, 1)
                    sc.wait_ge(st_full, 1)
                    A_.activation(ctx_state.rearrange("p d c e -> p (d c e)"), psum[:, TR[0], :], ACT.Copy).then_inc(st_ev, 1)
                    sc.wait_ge(st_ev, 1)
                    for d, out in enumerate((new_sf, new_sb)):
                        sc.dma_start(out[layer].rearrange("(c i) k e -> (i k) c e", c=2), ctx_state[:, d]).then_inc(stored, 16)

                    for m in range(3 * KD):
                        if 2 <= m <= HEADS_C + 1:
                            h = m - 2
                            sc.wait_ge(ccen, h + 1)
                            A_.activation(square[:, h % 2, :], c_raw[:, h % 2, :], ACT.Square).then_inc(csq, 1)
                        if 3 <= m <= HEADS_C + 2:
                            h = m - 3
                            sc.wait_ge(cvar_full, h + 1)
                            if h >= 2:
                                sc.wait_ge(c_done, h - 1)
                            A_.activation(c_rs[:, h % 2, :], psum[:, TR[1], 0:T], ACT.Ln, scale=1.0 / P, bias=c_("eps")).then_inc(crs, 1)
                            sc.wait_ge(crs, h + 1)
                            A_.activation(c_rs[:, h % 2, :], c_rs[:, h % 2, :], ACT.Exp, scale=-0.5).then_inc(crs_read, 1)
                        if 1 <= m <= HEADS_C:
                            h = m - 1
                            sc.wait_ge(co_full, h + 1)
                            if h >= 2:
                                sc.wait_ge(c_done, h - 1)
                            A_.activation(c_raw[:, h % 2, :], psum[:, O[h % 2], 0:T], ACT.Copy).then_inc(co_read, 1)
                        sc.wait_ge(gate_full, m + 1)
                        if m >= 2:
                            sc.wait_ge(br_read, m - 1)
                        A_.activation(gate_e[m % 2], psum[:, Z[1], 0:T], ACT.Exp, scale=-1.0).then_inc(gate_exp, 1)

                    squares(KD)
                    inverse_rms(TR[0], 2 * KD)
                    modulate(KD, scale_ffn, 24)
                    sc.wait_ge(lg_max, 1)
                    A_.activation(aff, aff, ACT.Exp).then_inc(lg_exp, 1)
                    for n in range(2 * NBLK):
                        sc.wait_ge(hr_tr, n + 1)
                        A_.activation(h_rows[:, n // 2, (n % 2) * 512:(n % 2 + 1) * 512], psum[:, O[n % 2], :], ACT.Copy).then_inc(hr_ev, 1)

                    sc.wait_ge(ko_st, 32)
                    sc.wait_ge(stored, 32)
                    A_.preload_act_table(ACT.Silu)

                    def read_gathered(expert):
                        sc.wait_ge(xg_full, expert + 1)
                        A_.activation(xg, psum[:, O[0], :], ACT.Copy).then_inc(xg_read, 1)

                    def expert_step(pair, e, last_expert):
                        expert = pair * 2 + e
                        sc.wait_ge(gate_h, pair * 4 + (2 * e + 2))
                        A_.activation(act, psum[:, S[0], :], ACT.Silu).then_inc(silu_ready, 1)
                        if not last_expert:
                            read_gathered(pair * 2 + (e + 1))
                        sc.wait_ge(ht_full, expert + 1)
                        A_.activation(hidT.rearrange("p q h s -> p (q h s)"), psum[:, TR[0], :], ACT.Copy).then_inc(ht_read, 1)
                        sc.wait_ge(down_full, pair * 4 + (2 * e + 2))
                        A_.activation(out_rows, psum[:, TR[1], :], ACT.Copy).then_inc(down_read, 1)

                    read_gathered(0)
                    with sc.Fori(0, NE // 2 - 1) as pair:
                        for e in range(2):
                            expert_step(pair, e, False)
                    for e in range(2):
                        expert_step(NE // 2 - 1, e, e == 1)

                @block.vector
                def _(dve):
                    then = chain(dve, dve_link)

                    dve.wait_ge(vec_tr, 1)
                    V.tensor_copy(vecT[:], psum[:, TR[1], 0:72]).then_inc(vec_ready, 1)
                    dve.wait_ge(vec_ready, 1)
                    dve.wait_ge(small_in, 16 * 3)
                    pairs = lam_rows.rearrange("p (a i) d -> p a i d", i=2)
                    prod = gate_e[0][:, 0:P].rearrange("p (a d) -> p a d", a=2)
                    then(V.tensor_tensor(prod, pairs[:, :, 0, :], pairs[:, :, 1, :], ALU.mult))
                    V.reduce_sum(lamb[:, 0:2], prod, axis=AX_X).then_inc(lam_sum, 1)
                    then(V.tensor_scalar(decay_t[:, 3], decay, -1.0, None, ALU.mult))
                    V.tensor_tensor(decay_t[:, 0], decay, decay_t[:, 3], ALU.max).then_inc(abs_ready, 1)
                    dve.wait_ge(lam_exp, 1)
                    then(V.tensor_tensor(lamb[:, 4:5], lamb[:, 3:4], lamb[:, 2:3], ALU.subtract))
                    then(V.tensor_tensor(lamb[:, 5:6], lamb[:, 4:5], layer_c[:, 0:1], ALU.subtract))
                    then(V.tensor_scalar(gain_a[:], vecT[:, 64:68], layer_c[:, 1:2], None, ALU.mult))
                    dve.wait_ge(ln_ready, 1)
                    then(V.tensor_scalar(decay_t[:, 3], decay, 0.0, None, ALU.min))
                    V.tensor_tensor(decay, decay_t[:, 3], decay_t[:, 2], ALU.subtract).then_inc(decay_ready, 1)
                    dve.wait_ge(decay_ready, 1)

                    def normed(first):
                        dve.wait_ge(rs_ready, 1 + first // KD)
                        for k in range(KD):
                            if k >= 2:
                                dve.wait_ge(h_ready, first + k - 1)
                            V.tensor_tensor(tmp[:, k % 2, :], xT[:, k, :], rs[:], ALU.mult).then_inc(norm_mul, 1)

                    dve.wait_ge(z_read, f_of_modT(0) + 1)
                    then(V.tensor_tensor(modT[:, 0:16, :], modT[:, 0:16, :], vecT[:, 0:16].unsqueeze(2).to_broadcast([P, 16, 2]), ALU.add))
                    V.scalar_tensor_tensor(out=scale_mix[:], in0=modT[:, 8:16, :], scalar=1.0,
                                           in1=vecT[:, 48:56].unsqueeze(2).to_broadcast([P, KD, 2]), op0=ALU.add, op1=ALU.mult).then_inc(mod1_ready, 1)
                    normed(0)

                    for c in range(8):
                        dve.wait_ge(rot_full, c + 1)
                        if c >= 2:
                            dve.wait_ge(rope_done, c - 1)
                        else:
                            dve.wait_ge(h_ready, KD)
                        then(V.tensor_tensor(tmp[:, c % 2, 0:2 * P], psum[:, S[c % 2], 0:2 * P], c_("sin"), ALU.mult))
                        then(V.tensor_tensor(zT[:, AQ + c, LAT], zT[:, AQ + c, LAT], c_("cos"), ALU.mult))
                        V.tensor_tensor(zT[:, AQ + c, LAT], zT[:, AQ + c, LAT], tmp[:, c % 2, 0:2 * P], ALU.add).then_inc(rope_done, 1)

                    def row_max(n):
                        mixer, u = divmod(n, UNITS)
                        c, b = divmod(u, NBLK)
                        keys = P if b == 0 else T
                        dve.wait_ge(s_full, n + 1)
                        if mixer == 0 or b == 0:
                            for i in range(2):
                                then(V.reduce_max(small[:, n % 2, 4 + i:5 + i], psum[:, S[i], 0:keys], axis=AX_X))
                            V.tensor_scalar(small[:, n % 2, 0:2], small[:, n % 2, 4:6], -SCALE, None, ALU.mult).then_inc(s_max, 1)
                        else:
                            dve.wait_ge(pT_full, n - 1)
                            if n < UNITS + 3:
                                dve.wait_ge(bias_ready, 2)
                            for i in range(2):
                                h = 2 * c + i
                                own = probs[:, n % 2, i, 0:2 * P].rearrange("p (r c) -> p r c", r=4)
                                V.scalar_tensor_tensor(out=own, in0=psum[:, S[i], 0:2 * P].rearrange("p (r c) -> p r c", r=4), scalar=SCALE,
                                                       in1=bias[b - 1][:, h::HEADS_B, ::-1], op0=ALU.mult, op1=ALU.add)
                                then(V.tensor_scalar(probs[:, n % 2, i, 2 * P:T], psum[:, S[i], 2 * P:T], SCALE, None, ALU.mult))
                            then(V.reduce_max(small[:, n % 2, 4:6], probs[:, n % 2, :, :], axis=AX_X))
                            V.tensor_scalar(small[:, n % 2, 0:2], small[:, n % 2, 4:6], -1.0, None, ALU.mult).then_inc(s_max, 1)

                    def normalise(n):
                        mixer, u = divmod(n, UNITS)
                        keys = P if u % NBLK == 0 else T
                        dve.wait_ge(s_exp, n + 1)
                        then(V.reciprocal(small[:, n % 2, 4:6], small[:, n % 2, 2:4]))
                        p0, p1 = probs[:, n % 2, 0, 0:keys], probs[:, n % 2, 1, 0:keys]
                        if mixer == 0:
                            then(V.tensor_tensor(small[:, n % 2, 6:7], small[:, n % 2, 5:6], lamb[:, 5:6], ALU.mult))
                            then(V.tensor_scalar(p1, p1, small[:, n % 2, 6:7], None, ALU.mult))
                            V.scalar_tensor_tensor(out=p0, in0=p0, scalar=small[:, n % 2, 4:5], in1=p1, op0=ALU.mult, op1=ALU.add).then_inc(p_ready, 1)
                        else:
                            V.tensor_scalar(p0, p0, small[:, n % 2, 4:5], None, ALU.mult)
                            V.tensor_scalar(p1, p1, small[:, n % 2, 5:6], None, ALU.mult).then_inc(p_ready, 1)

                    for n in range(UNITS):
                        row_max(n)
                        normalise(n)
                    for t in range(A_STEPS):
                        if t < UNITS:
                            row_max(UNITS + t)
                            normalise(UNITS + t)
                        if 1 <= t <= UNITS:
                            n = UNITS + t - 1
                            keys = P if n % NBLK == 0 else T
                            dve.wait_ge(pT_full, n + 1)
                            dve.wait_ge(o_full, n - 1)
                            V.tensor_copy(probsT[:, n % 2, 1, 0:keys], psum[:, TR[1], 0:keys]).then_inc(pT_dve, 1)
                        if t < 4:
                            dve.wait_ge(nrs, t + 1)
                            V.scalar_tensor_tensor(out=zT[:, AQ + t, :], in0=zT[:, AQ + t, :], scalar=gain_a[:, t:t + 1],
                                                   in1=tmp[:, t % 2, :], op0=ALU.mult, op1=ALU.mult).then_inc(a_done, 1)

                    dve.wait_ge(o_full, 2 * UNITS)
                    dve.wait_ge(kr_tr, 1)
                    dve.wait_ge(chunk_ready, 1)
                    heads = [P, 4, 64]
                    for kind, (b, d) in enumerate(((0, 0), (0, 1), (1, 0), (2, 1))):
                        rows = psum[:, S[b // 2], (b % 2) * 2 * P:(b % 2 + 1) * 2 * P].rearrange("p (h e) -> p h e", h=4)
                        V.tensor_tensor(k_dec[:, kind, :].rearrange("p (h e) -> p h e", h=4), rows,
                                        k_decay[:, d, :].unsqueeze(2).to_broadcast(heads), ALU.mult).then_inc(kr_ev, 1)
                    for d in range(2):
                        for c in range(2):
                            V.tensor_tensor(q_dec[:, d, c, :].rearrange("p (b t) -> p b t", b=2),
                                            zT[:, CQ + c, LAT].rearrange("p (b t) -> p b t", b=2),
                                            q_decay[:, d, c, :].unsqueeze(1).to_broadcast([P, 2, P]), ALU.mult).then_inc(qd_ready, 1)
                    dve.wait_ge(st_full, 2)
                    dve.wait_ge(state_in, 32)
                    for d in range(2):
                        for c in range(2):
                            V.scalar_tensor_tensor(out=state1[:, d, c, :], in0=state0[:, d, c, :], scalar=chunk_decay[:, d, c:c + 1],
                                                   in1=psum[:, TR[1], d * 2 * P + c * P:d * 2 * P + (c + 1) * P],
                                                   op0=ALU.mult, op1=ALU.add).then_inc(st1_ready, 1)
                    dve.wait_ge(z_read, FILLERS)
                    then(V.tensor_tensor(modT[:, 16:48, :], modT[:, 16:48, :], vecT[:, 16:48].unsqueeze(2).to_broadcast([P, 32, 2]), ALU.add))
                    V.scalar_tensor_tensor(out=scale_ffn[:], in0=modT[:, 32:40, :], scalar=1.0,
                                           in1=vecT[:, 56:64].unsqueeze(2).to_broadcast([P, KD, 2]), op0=ALU.add, op1=ALU.mult).then_inc(mod2_ready, 1)
                    dve.wait_ge(mod2_ready, 1)
                    dve.wait_ge(in_decay_ready, 1)

                    for m in range(3 * KD):
                        branch, j = divmod(m, KD)
                        if m < HEADS_C:
                            dve.wait_ge(att_full, m + 1)
                            if m >= 2:
                                dve.wait_ge(co_full, m - 1)
                            blocks = [P, NBLK, P]
                            V.tensor_tensor(att[:, m % 2, :].rearrange("p (b t) -> p b t", b=NBLK),
                                            psum[:, S[m % 2], 0:T].rearrange("p (b t) -> p b t", b=NBLK),
                                            in_decay[:, m, :].unsqueeze(1).to_broadcast(blocks), ALU.mult).then_inc(att_ready, 1)
                        if m == 0:
                            cg = zT[:, CG:CG + 4, :].rearrange("p c t -> p (c t)")
                            dve.wait_ge(cg_exp, 1)
                            then(V.tensor_scalar(cg_sig, cg_sig, 1.0, None, ALU.add))
                            then(V.reciprocal(cg_sig, cg_sig))
                            then(V.tensor_tensor(cg, cg, cg_sig, ALU.mult))
                        if 2 <= m <= HEADS_C + 1:
                            h = m - 2
                            dve.wait_ge(cmean_full, h + 1)
                            V.scalar_tensor_tensor(out=c_raw[:, h % 2, :], in0=psum[:, TR[0], 0:T], scalar=-1.0 / P, in1=c_raw[:, h % 2, :],
                                                   op0=ALU.mult, op1=ALU.add).then_inc(ccen, 1)
                        if 3 <= m <= HEADS_C + 2:
                            h = m - 3
                            dve.wait_ge(crs_read, h + 1)
                            then(V.tensor_tensor(c_rs[:, h % 2, :], c_rs[:, h % 2, :], c_raw[:, h % 2, :], ALU.mult))
                            V.scalar_tensor_tensor(out=zT[:, CG + h, :], in0=c_rs[:, h % 2, :], scalar=vecT[:, 68 + h:69 + h],
                                                   in1=zT[:, CG + h, :], op0=ALU.mult, op1=ALU.mult).then_inc(c_done, 1)
                        g = gate_e[m % 2]
                        dve.wait_ge(gate_exp, m + 1)
                        then(V.tensor_scalar(g, g, 1.0, None, ALU.add))
                        then(V.reciprocal(g, g))
                        dve.wait_ge(br_full, m + 1)
                        if branch == 0:
                            V.tensor_tensor(merged[:, j, :], g, psum[:, Z[0], 0:T], ALU.mult).then_inc(br_read, 1)
                        else:
                            then(V.tensor_tensor(g, g, psum[:, Z[0], 0:T], ALU.mult))
                            V.tensor_tensor(merged[:, j, :], merged[:, j, :], g, ALU.add).then_inc(br_read, 1)

                    for j in range(KD):
                        dve.wait_ge(w_full, j + 1)
                        for g, cols in enumerate((CTX, LAT)):
                            last = V.scalar_tensor_tensor(out=xT[:, j, cols], in0=psum[:, S[j % 2], cols], scalar=modT[:, 16 + j, g:g + 1],
                                                          in1=xT[:, j, cols], op0=ALU.mult, op1=ALU.add)
                        last.then_inc(w_read, 1)
                    dve.wait_ge(w_read, KD)
                    normed(KD)

                    dve.wait_ge(lg_full, 1)
                    logits = psum[:, TR[1], 0:NBLK * NE].rearrange("p (b e) -> p b e", b=NBLK)
                    per_block = small[:].rearrange("p a b -> p (a b)")
                    wide = [P, NBLK, NE]
                    then(V.reduce_max(per_block[:, 0:3], logits, axis=AX_X))
                    V.tensor_tensor(aff, logits, per_block[:, 0:3].unsqueeze(2).to_broadcast(wide), ALU.subtract).then_inc(lg_max, 1)
                    dve.wait_ge(lg_exp, 1)
                    then(V.reduce_sum(per_block[:, 4:7], aff, axis=AX_X))
                    then(V.reciprocal(per_block[:, 8:11], per_block[:, 4:7]))
                    V.tensor_tensor(aff, aff, per_block[:, 8:11].unsqueeze(2).to_broadcast(wide), ALU.mult).then_inc(aff_ready, 1)
                    dve.wait_ge(affT_full, 1)
                    rows = slice(0, NE)
                    then(V.tensor_copy(left[rows], psum[rows, S[0], 0:T]))
                    for cols, cap, first in ((CTX, CAP_CTX, 0), (LAT, CAP_LAT, CAP_CTX)):
                        for _ in range(cap // 8):
                            then(V.max(best[rows], left[rows, cols]))
                            then(V.match_replace(left[rows, cols], best[rows], left[rows, cols], -1.0))
                        then(V.tensor_scalar(chosen[rows, cols], left[rows, cols], 0.0, None, ALU.is_lt))
                        then(V.tensor_tensor_scan(place[rows, cols], chosen[rows, cols], chosen[rows, cols], float(first), ALU.add, ALU.max))
                        last = V.tensor_tensor(place[rows, cols], place[rows, cols], chosen[rows, cols], ALU.mult)
                        if cols is CTX:
                            then(last)
                        else:
                            last.then_inc(slots_ready, 1)
                    dve.wait_ge(slots_tr, 1)
                    V.tensor_copy(slot_of, psum[:, S[1], 0:NBLK * NE].rearrange("p (b e) -> p b e", b=NBLK)).then_inc(slots_ev, 1)
                    dve.wait_ge(slots_ev, 1)
                    dve.wait_ge(acc_zero, 1)

                    def choose(e, expert):
                        column = bass.ds(expert, 1)
                        for b in range(NBLK):
                            V.tensor_scalar(pick[:, e, b, :], c_("slot"), slot_of[:, b, column], None, ALU.is_equal)
                            last = V.tensor_scalar(pick_g[:, e, b, :].rearrange("p (h s) -> p h s", h=2), c_("slot").unsqueeze(1).to_broadcast([P, 2, HALF]),
                                                   slot_of[:, b, column], aff[:, b, column], ALU.is_equal, ALU.mult)
                        last.then_inc(pick_ready, 1)

                    def read_gatheredT(expert):
                        dve.wait_ge(xt_full, expert + 1)
                        V.tensor_copy(xgT.rearrange("p q h s -> p (q h s)"), psum[:, O[1], :]).then_inc(xt_read, 1)

                    def expert_step(pair, e, last_expert):
                        expert = pair * 2 + e
                        if not last_expert:
                            choose(1 - e, pair * 2 + (e + 1))
                        dve.wait_ge(silu_ready, expert + 1)
                        dve.wait_ge(up_h, pair * 4 + (2 * e + 2))
                        V.tensor_tensor(hid, act, psum[:, S[1], :], ALU.mult).then_inc(hid_ready, 1)
                        if not last_expert:
                            read_gatheredT(pair * 2 + (e + 1))
                        dve.wait_ge(pgT_full, expert + 1)
                        V.tensor_copy(pick_gT, psum[:, O[0], 0:T]).then_inc(pgT_read, 1)
                        for q in range(4):
                            for half in range(2):
                                chunk = 4 * (q // 2) + 2 * half + q % 2
                                dve.wait_ge(sc_full, pair * (2 * KD) + (e * KD + 2 * q + half + 1))
                                V.tensor_tensor(acc[:, chunk, :], acc[:, chunk, :], psum[:, (Z, O)[q % 2][half], 0:T], ALU.add).then_inc(sc_read, 1)

                    choose(0, 0)
                    read_gatheredT(0)
                    with dve.Fori(0, NE // 2 - 1) as pair:
                        for e in range(2):
                            expert_step(pair, e, False)
                    for e in range(2):
                        expert_step(NE // 2 - 1, e, e == 1)

                    dve.wait_ge(sc_read, NE * KD)
                    for k in range(KD):
                        for g, cols in enumerate((CTX, LAT)):
                            V.scalar_tensor_tensor(out=xT[:, k, cols], in0=acc[:, k, cols], scalar=modT[:, 40 + k, g:g + 1],
                                                   in1=xT[:, k, cols], op0=ALU.mult, op1=ALU.add)
            clear_all()

        y_rows = hT[:].rearrange("p k t -> p (k t)").rearrange("p (b d) -> p b d", b=NBLK)
        with nc.Block() as block:
            @block.sync
            def _(sp):
                sp.dma_start(vec_rows[0:KD, :], norm_final.rearrange("(k p) -> k p", p=P)).then_inc(small_in, 16)
                for b in range(NBLK):
                    sp.wait_ge(hr_ev, 2 * (b + 1))
                    sp.dma_start(y_out[b * P:(b + 1) * P, :], y_rows[:, b, :]).then_inc(stored, 16)
                sp.wait_ge(stored, 48)

            @block.scalar
            def _(sc):
                for k in range(KD):
                    if k >= 2:
                        sc.wait_ge(sq_used, k - 1)
                    A_.activation(square[:, k % 2, :], xT[:, k, :], ACT.Square).then_inc(sq_ready, 1)
                sc.wait_ge(nsum, 1)
                link = chain(sc, act_link)
                link(A_.activation(rs[:], psum[:, S[0], 0:T], ACT.Ln, scale=1.0 / D, bias=c_("eps")))
                A_.activation(rs[:], rs[:], ACT.Exp, scale=-0.5).then_inc(rs_ready, 1)

            @block.vector
            def _(dve):
                dve.wait_ge(vec_tr, 1)
                V.tensor_copy(vecT[:, 0:KD], psum[:, TR[1], 0:KD]).then_inc(vec_ready, 1)
                dve.wait_ge(vec_ready, 1)
                dve.wait_ge(rs_ready, 1)
                for k in range(KD):
                    V.scalar_tensor_tensor(out=xT[:, k, :], in0=xT[:, k, :], scalar=vecT[:, k:k + 1], in1=rs[:],
                                           op0=ALU.mult, op1=ALU.mult).then_inc(h_ready, 1)
                for n in range(2 * NBLK):
                    dve.wait_ge(hr_tr, n + 1)
                    V.tensor_copy(y_rows[:, n // 2, (n % 2) * 512:(n % 2) * 512 + 512], psum[:, n % 2, :]).then_inc(hr_ev, 1)

            @block.tensor
            def _(pe):
                pe.wait_ge(small_in, 16)
                transpose(psum[:, TR[1], 0:KD], vec_rows[0:KD, :]).then_inc(vec_tr, 1)
                for k in range(KD):
                    pe.wait_ge(sq_ready, k + 1)
                    last = M.matmul(psum[:, S[0], 0:T], ones, square[:, k % 2, :], start=k == 0, stop=k == KD - 1)
                    last.then_inc(sq_used if k < KD - 1 else nsum, 1)
                pe.wait_ge(h_ready, KD)
                for n in range(2 * NBLK):
                    if n >= 2:
                        pe.wait_ge(hr_ev, n - 1)
                    for j in range(4):
                        k = (n % 2) * 4 + j
                        last = transpose(psum[:, n % 2, j * P:(j + 1) * P], xT[:, k, (n // 2) * P:(n // 2 + 1) * P])
                    last.then_inc(hr_tr, 1)


_OUTS = [("y_prompt", (1, P, D)), ("y_sample", (1, T - P, D)), ("new_a_k", (1, DEPTH, P, HEADS_A, 2, 64)),
         ("new_a_v", (1, DEPTH, P, HEADS_A, 128)), ("new_b_k", (1, DEPTH, P, HEADS_B, 64)),
         ("new_b_v", (1, DEPTH, P, HEADS_B, 64)), ("new_c_fwd", (1, DEPTH, HEADS_C, 64, 128)),
         ("new_c_bwd", (1, DEPTH, HEADS_C, 64, 128))]


def kernel(**inputs):
    import numpy as _np
    import concourse.bacc as _bacc
    from concourse import mybir as _mybir
    from concourse.bass_utils import run_bass_kernel_spmd as _run

    a = {k: _np.asarray(v) for k, v in inputs.items()}
    table, per_layer = shape_constants()
    feeds = [
        ("x", _np.concatenate([a["x_prompt"][0], a["x_sample"][0]], axis=0)),
        ("cvec", _np.stack([a["c_ctx"], a["c"][0]])),
        ("cache_k", _np.concatenate([a["cache_a_k"][0].reshape(DEPTH, P, 512), a["cache_b_k"][0].reshape(DEPTH, P, 512)], axis=2)),
        ("cache_v", _np.concatenate([a["cache_a_v"][0].reshape(DEPTH, P, 512), a["cache_b_v"][0].reshape(DEPTH, P, 512)], axis=2)),
        ("state_f", a["state_c_fwd"][0]),
        ("state_b", a["state_c_bwd"][0]),
        ("w_mod", a["w_mod"]),
        ("layer_vectors", _np.concatenate([a[n].reshape(DEPTH, -1, P) for n in
                                           ("b_mod", "norm_mix", "norm_ffn", "diff_norm", "ret_norm")], axis=1)),
        ("layer_scalars", _np.concatenate([a["diff_lambda"].reshape(DEPTH, 256), a["ret_decay"].reshape(DEPTH, 8), per_layer], axis=1)),
        ("w_in", a["w_in"]),
        ("rpb_rev", a["na_rpb"].transpose(0, 2, 1, 3)[..., ::-1]),
        ("w_pa", a["w_proj_a"]), ("w_pb", a["w_proj_b"]),
        ("w_pc", a["w_proj_c"]), ("w_out", a["w_out"]), ("w_router", a["w_router"]), ("w_gate", a["w_exp_gate"]),
        ("w_up", a["w_exp_up"]), ("w_down", a["w_exp_down"]), ("norm_final", a["norm_final"]),
        ("const", table),
    ]
    nc = _bacc.Bacc("TRN2", target_bir_lowering=False, num_devices=1)
    arrays, args = {}, []
    for name, value in feeds:
        value = _np.ascontiguousarray(value)
        arrays[f"in_{name}"] = value
        args.append(nc.dram_tensor(f"in_{name}", value.shape, _mybir.dt.from_np(value.dtype), kind="ExternalInput").ap())
    shapes = [("y", (T, D)), ("ak", (DEPTH, P, 512)), ("av", (DEPTH, P, 512)), ("bk", (DEPTH, P, 512)),
              ("bv", (DEPTH, P, 512)), ("sf", (DEPTH, HEADS_C, 64, P)), ("sb", (DEPTH, HEADS_C, 64, P))]
    for name, shape in shapes:
        args.append(nc.dram_tensor(f"out_{name}", shape, _mybir.dt.float32, kind="ExternalOutput").ap())
    build(nc, *args)
    r = _run(nc, [arrays], core_ids=[0]).results[0]
    y = r["out_y"]
    rest = [r[f"out_{name}"].reshape(shape) for (name, _), (_, shape) in zip(shapes[1:], _OUTS[2:])]
    return (y[0:P].reshape(_OUTS[0][1]), y[P:T].reshape(_OUTS[1][1]), *rest)
```

```python
import math
from contextlib import ExitStack

import numpy as np

import concourse.bass as bass
from concourse import mybir

F32 = mybir.dt.float32
ALU = mybir.AluOpType
ACT = mybir.ActivationFunctionType
AX_X = mybir.AxisListType.X

P = 128
D = 1024
KD = D // P
NBLK = 3
T = NBLK * P
CTX = slice(0, P)
LAT = slice(P, T)
DEPTH = 2
GRID_W = 64
HEADS_A = 4
HEADS_B = 8
HEADS_C = 4
RPB_ROWS, RPB_COLS = 15, 31
NE = 16
CAP_CTX = 2 * P // NE
CAP_LAT = 2 * (T - P) // NE
HALF = P // 2
EPS = 1e-6
SCALE = 64 ** -0.5
NEG = -1e30

SLAB = 512
RING = 4
DENSE_SLABS = 32
EXPERT_SLABS = 6
MOD_AHEAD = 4
DVE_MODULATES = ((0, 2, 3, 5, 6), (2, 4, 7))

CONST_AT = {}
_at = 0
for _name, _width in (("ident", P), ("rot", P), ("ones", P), ("cos", 2 * P), ("sin", 2 * P),
                      ("below", P), ("above", P), ("is_below", P), ("is_above", P),
                      ("since", P), ("until", P), ("k_until", 1), ("k_since", 1), ("eps", 1), ("one", 1),
                      ("slot", HALF), ("window", GRID_W), ("gather_experts", NE)):
    CONST_AT[_name] = (_at, _at + _width)
    _at += _width
CONST_COLS = _at


def shape_constants():
    t = np.zeros((P, CONST_COLS), np.float32)

    def put(name, value):
        a, b = CONST_AT[name]
        t[:, a:b] = value

    p = np.arange(P)[:, None].astype(np.float32)
    i = np.arange(P)[None, :].astype(np.float32)
    put("ident", np.eye(P))
    rot = np.zeros((P, P), np.float32)
    for m in range(P):
        if m % 32 < 16:
            rot[m + 16, m] = -1.0
        else:
            rot[m - 16, m] = 1.0
    put("rot", rot)
    put("ones", 1.0)
    quarter = 16
    freqs = (np.float32(10000.0) ** (-np.arange(quarter, dtype=np.float32) * np.float32(2.0) / np.float32(32))).astype(np.float32)
    tok = np.arange(2 * P)
    row = (tok // GRID_W).astype(np.float32)[:, None] * freqs
    col = (tok % GRID_W).astype(np.float32)[:, None] * freqs
    ang = np.concatenate([row, row, col, col], axis=-1).T
    ang = np.concatenate([ang, ang], axis=0)
    put("cos", np.cos(ang))
    put("sin", np.sin(ang))
    put("below", np.maximum(i - p, 0))
    put("above", np.maximum(p - i, 0))
    put("is_below", (i >= p).astype(np.float32))
    put("is_above", (p >= i).astype(np.float32))
    put("since", i + 1)
    put("until", P - i)
    put("k_until", P - 1 - p)
    put("k_since", p)
    put("eps", EPS)
    put("one", 1.0)
    put("gather_experts", np.tile(np.eye(32)[:, 0:NE], (4, 1)))
    put("slot", np.arange(1, HALF + 1)[None, :])
    qc = np.arange(P)[:, None] % GRID_W
    kc = GRID_W - 1 - np.arange(GRID_W)[None, :]
    start = np.clip(qc - 8, 0, GRID_W - 16)
    put("window", np.where((kc >= start) & (kc < start + 16), 0.0, NEG))
    layer = np.zeros((DEPTH, 2), np.float32)
    for l in range(DEPTH):
        lam_init = 0.8 - 0.6 * math.exp(-0.3 * l)
        layer[l] = lam_init, 1.0 - lam_init
    return t, layer


def build(nc, x_rows, cvec, cache_k, cache_v, state_f, state_b, w_mod, layer_vectors, layer_scalars,
          w_in, rpb_rev, w_pa, w_pb, w_pc, w_out, w_router, w_gate, w_up, w_down, norm_final, const_in,
          y_out, new_ak, new_av, new_bk, new_bv, new_sf, new_sb):
    ctx = ExitStack()
    sems = []

    def sb(name, shape):
        return ctx.enter_context(nc.sbuf_tensor(name, shape, F32))

    def sem(name):
        s = ctx.enter_context(nc.semaphore(name))
        sems.append(s)
        return s

    with ctx:
        ring = sb("ring", [P, RING, KD, SLAB])
        xT = sb("xT", [P, KD, T])
        hT = sb("hT", [P, KD, T])
        const = sb("const", [P, CONST_COLS])
        dense = sb("dense", [P, 13824])
        silu_c = sb("silu_c", [P, KD, 32])
        modT = sb("modT", [P, 48, 2])
        scale_mix = sb("scale_mix", [P, KD, 2])
        scale_ffn = sb("scale_ffn", [P, KD, 2])
        vec_rows = sb("vec_rows", [72, P])
        vecT = sb("vecT", [P, 72])
        final_gain = sb("final_gain", [P, KD])
        square = sb("square", [P, 2, T])
        rs = sb("rs", [P, T])
        tmp = sb("tmp", [P, 2, T])
        wide = sb("wide", [P, 2, KD, SLAB])
        wide_cols = wide[:].rearrange("p u k n -> p (u k n)")
        merged = wide_cols[:, 0:KD * T].rearrange("p (k t) -> p k t", k=KD)
        bias0 = wide_cols[:, KD * T:KD * T + 2048].rearrange("p (r c) -> p r c", c=GRID_W)
        probs = wide_cols[:, KD * T + 2048:KD * T + 2048 + 4 * T].rearrange("p (a b t) -> p a b t", a=2, b=2)
        probsT = wide_cols[:, KD * T + 2048 + 4 * T:KD * T + 2048 + 8 * T].rearrange("p (a b t) -> p a b t", a=2, b=2)
        assert KD * T + 2048 + 8 * T == 2 * KD * SLAB
        akcT = sb("akcT", [P, 4, P])
        bkcT = sb("bkcT", [P, 4, P])
        small = sb("small", [P, 2, 8])
        layer_rows = sb("layer_rows", [P, 4 * 64 + 8 + 2])
        lam_rows = layer_rows[:, 0:256].rearrange("p (a d) -> p a d", a=4)
        decay = layer_rows[:, 256:264]
        layer_c = layer_rows[:, 264:266]
        lamb = sb("lamb", [P, 8])
        gain_a = sb("gain_a", [P, 4])
        decay_t = sb("decay_t", [P, 4, 8])
        in_decay = sb("in_decay", [P, 4, P])
        bwd_decay = sb("bwd_decay", [P, 4, P])
        q_decay = sb("q_decay", [P, 2, 2, P])
        k_decay = sb("k_decay", [P, 2, 4])
        chunk_decay = sb("chunk_decay", [P, 2, 2])
        state0 = sb("state0", [P, 2, 2, P])
        state1 = sb("state1", [P, 2, 2, P])
        w_r = sb("w_r", [P, KD, 32])
        keys_out = bwd_decay[:].rearrange("p h t -> p (h t)")

        def c_(name):
            a, b = CONST_AT[name]
            return const[:, a:b]

        ident = c_("ident")
        ones = c_("ones")

        zT = dense[:, 0:24 * T].rearrange("p (c t) -> p c t", t=T)
        AQ, AK, BQ, BK, CQ, CK, CG = 0, 4, 8, 12, 16, 18, 20
        v_rows = dense[:, 24 * T:24 * T + 9 * SLAB].rearrange("p (m b e) -> p m b e", m=3, b=NBLK)
        assert 24 * T + 9 * SLAB == 13824
        kc_rows = probs.rearrange("p a b t -> p (a b t)")[:, 0:2 * SLAB]
        vc_rows = merged.rearrange("p k t -> p (k t)")[:, 0:2 * SLAB]
        av_c = merged.rearrange("p k t -> p (k t)")[:, 0:SLAB]
        bv_c = merged.rearrange("p k t -> p (k t)")[:, SLAB:2 * SLAB]
        akc_rows = probs.rearrange("p a b t -> p (a b t)")[:, 0:SLAB]
        bkc_rows = probs.rearrange("p a b t -> p (a b t)")[:, SLAB:2 * SLAB]
        bias1 = merged.rearrange("p k t -> p (k t)")[:, 2 * SLAB:6 * SLAB].rearrange("p (r c) -> p r c", c=GRID_W)
        bias = [bias0, bias1]
        ctx_state = bias0.rearrange("p r c -> p (r c)")[:, 0:SLAB].rearrange("p (d c e) -> p d c e", d=2, c=2)
        q_dec = probs.rearrange("p a b t -> p (a b t)")[:, 0:1024].rearrange("p (d c t) -> p d c t", d=2, c=2)
        k_dec = probsT.rearrange("p a b t -> p (a b t)")[:, 0:1024].rearrange("p (n e) -> p n e", n=4)
        att = tmp
        gate_e = [x.rearrange("p a b t -> p (a b t)")[:, 1024:1024 + T] for x in (probs, probsT)]
        a_free = v_rows[:, 0].rearrange("p b e -> p (b e)")
        c_raw = a_free[:, 0:2 * T].rearrange("p (u t) -> p u t", u=2)
        c_rs = a_free[:, 2 * T:4 * T].rearrange("p (u t) -> p u t", u=2)
        cg_sig = v_rows[:, 1].rearrange("p b e -> p (b e)")[:, 0:4 * T]
        sum_sq = tmp[:, 0, :]
        h_rows = dense[:, 0:3072].rearrange("p (b d) -> p b d", b=NBLK)
        acc = dense[:, 3072:6144].rearrange("p (k t) -> p k t", k=KD)
        odd_first = dense[:, 13824 - KD * SLAB:13824].rearrange("p (k n) -> p k n", k=KD)
        at = 6144

        def flat(x):
            v = x[:]
            return v.rearrange("p c t -> p (c t)") if len(v.shape) == 3 else v.rearrange("p d c t -> p (d c t)")

        def carve(n):
            nonlocal at
            at += n
            return dense[:, at - n:at]

        pick = carve(2 * NBLK * HALF).rearrange("p (u b s) -> p u b s", u=2, b=NBLK)
        pick_g = carve(2 * NBLK * P).rearrange("p (u b s) -> p u b s", u=2, b=NBLK)
        pick_gT = carve(T)
        xg = flat(akcT)
        xgT = flat(bkcT).rearrange("p (q h s) -> p q h s", q=4, h=2)
        act = flat(state0)
        hid = flat(state1)
        hidT = flat(in_decay).rearrange("p (q h s) -> p q h s", q=4, h=2)
        out_rows = flat(q_decay)
        aff = carve(NBLK * NE).rearrange("p (b e) -> p b e", b=NBLK)
        slot_of = carve(NBLK * NE).rearrange("p (b e) -> p b e", b=NBLK)
        left = carve(T)
        chosen = carve(T)
        place = carve(T)
        best = carve(16)
        assert at <= 13824 - KD * SLAB

        psum = ctx.enter_context(nc.psum_tensor("psum", [P, 8, SLAB], F32))
        Z = [0, 1]
        S = [2, 3]
        TR = [4, 7]
        O = [5, 6]

        slab_in = [sem(f"slab_in{i}") for i in range(EXPERT_SLABS + 1)]
        mod_in = [ctx.enter_context(nc.semaphore(f"mod_in{i}")) for i in range(MOD_AHEAD)]
        router_in = sem("router_in")
        rows_in = sem("rows_in")
        small_in = sem("small_in")
        keys_in = sem("keys_in")
        values_in = sem("values_in")
        state_in = sem("state_in")
        bias_in = sem("bias_in")
        stored = sem("stored")
        act_link = sem("act_link")
        dve_link = sem("dve_link")
        top_link = [sem("top_link_ctx"), sem("top_link_lat")]
        cg_one = sem("cg_one")
        pool_link = sem("pool_link")
        x_tr = sem("x_tr")
        x_ev = sem("x_ev")
        c_ready = sem("c_ready")
        c_zero = sem("c_zero")
        vec_tr = sem("vec_tr")
        vec_ready = sem("vec_ready")
        lam_sum = sem("lam_sum")
        lam_exp = sem("lam_exp")
        abs_ready = sem("abs_ready")
        ln_ready = sem("ln_ready")
        decay_ready = sem("decay_ready")
        decay_exp = sem("decay_exp")
        in_decay_ready = sem("in_decay_ready")
        chunk_ready = sem("chunk_ready")
        sq_ready = sem("sq_ready")
        sq_used = sem("sq_used")
        rs_ready = sem("rs_ready")
        mod1_ready = sem("mod1_ready")
        norm_mul = sem("norm_mul")
        h_act = sem("h_act")
        h_dve = sem("h_dve")
        h_ready = sem("h_ready")
        z_full = sem("z_full")
        z_read = sem("z_read")
        rot_full = sem("rot_full")
        rope_done = sem("rope_done")
        kc_tr = sem("kc_tr")
        kc_ev = sem("kc_ev")
        ko_tr = sem("ko_tr")
        ko_ev = sem("ko_ev")
        ko_st = sem("ko_st")
        bias_ready = sem("bias_ready")
        s_full = sem("s_full")
        s_max = sem("s_max")
        s_exp = sem("s_exp")
        p_ready = sem("p_ready")
        pT_full = sem("pT_full")
        pT_act = sem("pT_act")
        pT_dve = sem("pT_dve")
        o_full = sem("o_full")
        o_read = sem("o_read")
        nsum = sem("nsum")
        nrs = sem("nrs")
        a_done = sem("a_done")
        kr_tr = sem("kr_tr")
        kr_ev = sem("kr_ev")
        qd_ready = sem("qd_ready")
        st_full = sem("st_full")
        st_ev = sem("st_ev")
        st1_ready = sem("st1_ready")
        att_full = sem("att_full")
        att_ready = sem("att_ready")
        co_full = sem("co_full")
        co_read = sem("co_read")
        cmean_full = sem("cmean_full")
        ccen = sem("ccen")
        csq = sem("csq")
        cvar_full = sem("cvar_full")
        crs = sem("crs")
        c_done = sem("c_done")
        gate_full = sem("gate_full")
        gate_exp = sem("gate_exp")
        br_full = sem("br_full")
        br_read = sem("br_read")
        mod2_ready = sem("mod2_ready")
        w_full = sem("w_full")
        w_read = sem("w_read")
        lgT_full = sem("lgT_full")
        lgT_read = sem("lgT_read")
        lg_full = sem("lg_full")
        lg_max = sem("lg_max")
        lg_exp = sem("lg_exp")
        aff_ready = sem("aff_ready")
        affT_full = sem("affT_full")
        slots_ready = sem("slots_ready")
        slots_tr = sem("slots_tr")
        slots_ev = sem("slots_ev")
        hr_tr = sem("hr_tr")
        hr_ev = sem("hr_ev")
        v_stored = sem("v_stored")
        acc_zero = sem("acc_zero")
        a_sq = sem("a_sq")
        crs_read = sem("crs_read")
        cg_exp = sem("cg_exp")
        pick_ready = sem("pick_ready")
        pick_g_ready = sem("pick_g_ready")
        xg_full = sem("xg_full")
        xg_read = sem("xg_read")
        xt_full = sem("xt_full")
        xt_read = sem("xt_read")
        ht_full = sem("ht_full")
        ht_read = sem("ht_read")
        pgT_full = sem("pgT_full")
        pgT_read = sem("pgT_read")
        gate_h = sem("gate_h")
        up_h = sem("up_h")
        silu_ready = sem("silu_ready")
        hid_ready = sem("hid_ready")
        down_full = sem("down_full")
        down_read = sem("down_read")
        sc_full = sem("sc_full")
        sc_read = sem("sc_read")
        acc_added = sem("acc_added")
        rows_dve = sem("rows_dve")
        rows_act = sem("rows_act")

        V, A_, G, M = nc.vector, nc.scalar, nc.gpsimd, nc.tensor

        def chain(eng, s):
            n = 0

            def then(ins):
                nonlocal n
                n += 1
                ins.then_inc(s, 1)
                eng.wait_ge(s, n)
            return then

        def clear_all(used):
            with nc.Block() as block:
                @block.sync
                def _(sp):
                    for s in used[0::5]:
                        sp.sem_clear(s)

                @block.tensor
                def _(pe):
                    for s in used[1::5]:
                        pe.sem_clear(s)

                @block.vector
                def _(dve):
                    for s in used[2::5]:
                        dve.sem_clear(s)

                @block.scalar
                def _(sc):
                    for s in used[3::5]:
                        sc.sem_clear(s)

                @block.gpsimd
                def _(pool):
                    for s in used[4::5]:
                        pool.sem_clear(s)

        def mod_ahead(sp, of_layer, j):
            sp.dma_start(ring[:, j], w_mod[of_layer].rearrange("(k p) n -> p k n", p=P)[:, :, j * SLAB:(j + 1) * SLAB]
                         ).then_inc(mod_in[j], 16)

        def sum_squares(dve, first):
            dve.wait_ge(sq_ready, first + 2)
            V.tensor_tensor(sum_sq, square[:, 0, :], square[:, 1, :], ALU.add).then_inc(sq_used, 2)
            for k in range(2, KD):
                dve.wait_ge(sq_used, first + k)
                dve.wait_ge(sq_ready, first + k + 1)
                V.tensor_tensor(sum_sq, sum_sq, square[:, k % 2, :], ALU.add).then_inc(sq_used, 1)

        def transpose(out, in_):
            n = in_.shape[0]
            return M.matmul(out, in_, ident[0:n, 0:n], start=True, stop=True, is_transpose=True)

        x_in = hT[:].rearrange("p k t -> p (k t)").rearrange("p (b d) -> p b d", b=NBLK)
        with nc.Block() as block:
            @block.sync
            def _(sp):
                sp.dma_start(vec_rows[0:2 * KD, :], cvec.rearrange("g (k p) -> (g k) p", p=P)).then_inc(rows_in, 16)
                sp.dma_start(vec_rows[2 * KD:3 * KD, :], norm_final.rearrange("(k p) -> k p", p=P)).then_inc(rows_in, 16)
                sp.dma_start(const[:], const_in).then_inc(rows_in, 16)
                sp.dma_start(x_in, x_rows.rearrange("(b p) d -> p b d", p=P)).then_inc(rows_in, 16)
                for j in range(MOD_AHEAD):
                    mod_ahead(sp, 0, j)

            @block.tensor
            def _(pe):
                pe.wait_ge(rows_in, 64)
                for k in range(KD):
                    if k >= 4:
                        pe.wait_ge(x_ev, k - 3)
                    for b in range(NBLK):
                        last = transpose(psum[:, k % 4, b * P:(b + 1) * P], x_in[:, b, k * P:(k + 1) * P])
                    last.then_inc(x_tr, 1)
                transpose(psum[:, 4, 0:3 * KD], vec_rows[0:3 * KD, :]).then_inc(vec_tr, 1)

            @block.vector
            def _(dve):
                for k in range(KD):
                    dve.wait_ge(x_tr, k + 1)
                    V.tensor_copy(xT[:, k, :], psum[:, k % 4, 0:T]).then_inc(x_ev, 1)

            @block.gpsimd
            def _(pool):
                G.memset(silu_c[:], 0.0).then_inc(c_zero, 1)
                G.memset(w_r[:], 0.0)

            @block.scalar
            def _(sc):
                sc.wait_ge(vec_tr, 1)
                sc.wait_ge(c_zero, 1)
                A_.activation(silu_c[:, :, 0:2].rearrange("p k g -> p g k"),
                              psum[:, 4, 0:2 * KD].rearrange("p (g k) -> p g k", g=2), ACT.Silu).then_inc(c_ready, 1)
                A_.activation(final_gain[:], psum[:, 4, 2 * KD:3 * KD], ACT.Copy)
                A_.preload_act_table_set("natural_log_exp_and_others")
        clear_all([rows_in, x_tr, x_ev, vec_tr, c_zero, c_ready])

        with nc.Fori(0, DEPTH) as layer:
            with nc.Block() as block:
                START_FILL = [("mod", 0), ("mod", 1), ("modT", 0), ("mod", 2), ("modT", 1), ("mod", 3), ("modT", 2), ("modT", 3)]
                Z_FIRST = 11
                A_FILL = [[("z", Z_FIRST + t)] for t in range(14)]
                B_FILL = ([[("norm", t), ("z", 25 + t)] for t in range(4)] + [[("z", 25 + t)] for t in range(4, 8)]
                          + [[("mod", 4), ("mod", 5)], [("modT", 4), ("mod", 6), ("modT", 5)], [("mod", 7), ("modT", 6), ("mod", 8)],
                             [("modT", 7), ("mod", 9), ("modT", 8)], [("mod", 10), ("modT", 9), ("mod", 11)], [("modT", 10), ("modT", 11)]])
                FILL = START_FILL + [("z", g) for g in range(Z_FIRST)] + [x for step in A_FILL + B_FILL for x in step]
                FILLERS = len(FILL)

                def f_of(kind, i):
                    return FILL.index((kind, i))

                def mod_rows(j):
                    if j < 4:
                        return probsT.rearrange("p a b t -> p (a b t)")[:, (j % 2) * SLAB:(j % 2 + 1) * SLAB]
                    return (square, tmp)[j % 2][:].rearrange("p u t -> p (u t)")[:, 0:SLAB]

                parts_start = probsT.rearrange("p a b t -> p (a b t)")[:, 2 * SLAB:2 * SLAB + P]

                def mod_parts(j):
                    return parts_start[:, 32 * j:32 * j + 32] if j < 4 else rs[:, 32 * (j - 4):32 * (j - 3)]

                Z_GROUPS = ([(0, j, "T") for j in range(4)] + [(1, j, "T") for j in range(4)]
                            + [(2, j, "rows") for j in range(NBLK)]
                            + [(3, j, "T") for j in range(4)] + [(4, j, "T") for j in range(4)]
                            + [(5, j, "rows") for j in range(NBLK)]
                            + [(6, j, "T") for j in range(4)] + [(7, j, "rows") for j in range(NBLK)]
                            + [(8, j, "T") for j in range(4)])
                SCATTER_ORDER = [4 * (q // 2) + 2 * half + q % 2 for q in range(4) for half in range(2)]
                UNITS = 12
                A_STEPS = UNITS + 2

                SLABS = ([("mod", j) for j in range(MOD_AHEAD)] + [("w_in", j) for j in range(9)] + [("mod", j) for j in range(4, 12)]
                         + [x for b in range(3) for x in (("w_in", 9 + 2 * b), ("branch", b), ("w_in", 10 + 2 * b))] + [("w_out", 0), ("w_out", 1)])
                assert len(SLABS) == DENSE_SLABS

                def slab_source(n):
                    kind, j = SLABS[n]
                    w = [w_pa, w_pb, w_pc][j] if kind == "branch" else {"mod": w_mod, "w_in": w_in, "w_out": w_out}[kind]
                    rows = w[layer].rearrange("(k p) n -> p k n", p=P)
                    return rows if kind == "branch" else rows[:, :, j * SLAB:(j + 1) * SLAB]

                def slab_into(n):
                    if SLABS[n][0] == "branch":
                        return ring[:, n % RING].rearrange("p k n -> p (k n)").rearrange("p (k n) -> p k n", k=4)
                    return ring[:, n % RING]

                def expert_slab(odd, s):
                    if s == 0 and odd:
                        return odd_first, EXPERT_SLABS
                    return (ring[:, s] if s < RING else wide[:, s - RING]), s

                def chunk_ready_wait(eng, mixer, k):
                    by_dve = DVE_MODULATES[mixer]
                    if k in by_dve:
                        eng.wait_ge(h_dve, (len(DVE_MODULATES[0]) if mixer else 0) + by_dve.index(k) + 1)
                    else:
                        eng.wait_ge(h_act, (KD - len(DVE_MODULATES[0]) if mixer else 0) + sum(c not in by_dve for c in range(k)) + 1)

                def wait_slab_free(eng, n):
                    kind, j = SLABS[n]
                    if kind == "mod":
                        eng.wait_ge(z_full, f_of("mod", j) + 1)
                    elif kind == "w_in" and j < 9:
                        last_group = max(g for g, (slab, _, _) in enumerate(Z_GROUPS) if slab == j)
                        eng.wait_ge(z_full, f_of("z", last_group) + 1)
                    elif kind == "w_in":
                        eng.wait_ge(gate_full, 4 * (j - 8))
                    elif kind == "branch":
                        eng.wait_ge(br_full, KD * (j + 1))
                    else:
                        eng.wait_ge(w_full, 4 * (j + 1))

                @block.sync
                def _(sp):
                    sp.dma_start(vec_rows[:], layer_vectors[layer]).then_inc(small_in, 16)
                    sp.dma_start(layer_rows[:], bass.AP(layer_scalars.tensor, layer_scalars.offset + layer * 266, [[0, P], [1, 266]])).then_inc(small_in, 16)
                    sp.dma_start(kc_rows, cache_k[layer]).then_inc(keys_in, 16)
                    for n in range(MOD_AHEAD, DENSE_SLABS):
                        wait_slab_free(sp, n - RING)
                        sp.dma_start(slab_into(n), slab_source(n)).then_inc(slab_in[n % RING], 16)
                        if n == MOD_AHEAD + 2:
                            sp.dma_start(vc_rows, cache_v[layer]).then_inc(values_in, 16)
                            sp.dma_start(w_r[:, :, 0:NE], w_router[layer].rearrange("(k p) e -> p k e", p=P)).then_inc(router_in, 16)
                            for d, src in enumerate((state_f, state_b)):
                                sp.dma_start(state0[:, d], src[layer].rearrange("(c i) k e -> (i k) c e", c=2)).then_inc(state_in, 16)
                            for b in range(2):
                                for half in range(2):
                                    q_row = 2 * b + half
                                    skew = bass.AP(rpb_rev.tensor,
                                                   rpb_rev.offset + layer * (HEADS_B * RPB_ROWS * RPB_COLS) + ((7 - q_row) * HEADS_B * RPB_COLS + 15 - (GRID_W - 1)),
                                                   [[1, GRID_W], [RPB_COLS, 4 * HEADS_B], [1, GRID_W]])
                                    sp.dma_start(bias[b][GRID_W * half:GRID_W * (half + 1)], skew).then_inc(bias_in, 16)

                    def load(pair, e, s):
                        w = (w_gate, w_up, w_down)[s // 2]
                        place, number = expert_slab(e % 2, s)
                        sp.dma_start(place, w[layer, pair * 2 + e].rearrange("(k p) n -> p k n", p=P)[:, :, (s % 2) * SLAB:(s % 2 + 1) * SLAB]
                                     ).then_inc(slab_in[number], 16)

                    def wait_used(pair, e, s):
                        sp.wait_ge((gate_h, up_h, down_full)[s // 2], pair * 4 + (2 * e + s % 2 + 1))

                    for s in (0, 1, 5, 2, 3, 4):
                        if s < RING:
                            wait_slab_free(sp, DENSE_SLABS - RING + s)
                        elif s == 5:
                            sp.wait_ge(br_read, 3 * KD)
                        else:
                            sp.wait_ge(w_full, KD)
                            sp.wait_ge(stored, 32)
                        load(0, 0, s)
                    sp.wait_ge(c_done, HEADS_C)
                    load(0, 1, 0)
                    with sp.Fori(0, NE // 2 - 1) as pair:
                        for e in range(2):
                            for s in range(EXPERT_SLABS):
                                wait_used(pair, e, s)
                                if e == 1 or s == 0:
                                    load(pair + 1, e if s == 0 else 0, s)
                                elif s == 1:
                                    load(pair, 1, s)
                                else:
                                    load(pair + 1, -1, s)
                    last_pair = NE // 2 - 1
                    for s in range(1, EXPERT_SLABS):
                        wait_used(last_pair, 0, s)
                        load(last_pair, 1, s)
                    for j in range(MOD_AHEAD):
                        wait_used(last_pair, 1 if j else 0, j)
                        mod_ahead(sp, DEPTH - 1 - layer, j)

                @block.gpsimd
                def _(pool):
                    link = chain(pool, pool_link)
                    pool.wait_ge(decay_exp, 1)
                    four = [P, 4, P]
                    link(G.tensor_tensor(in_decay[:], in_decay[:], c_("is_below").unsqueeze(1).to_broadcast(four), ALU.mult))
                    link(G.tensor_tensor(bwd_decay[:], bwd_decay[:], c_("is_above").unsqueeze(1).to_broadcast(four), ALU.mult))
                    G.tensor_tensor(in_decay[:], in_decay[:], bwd_decay[:], ALU.add).then_inc(in_decay_ready, 1)
                    pool.wait_ge(bias_in, 64)
                    for b in bias:
                        G.tensor_tensor(b, b, c_("window").unsqueeze(1).to_broadcast([P, 32, GRID_W]), ALU.add).then_inc(bias_ready, 1)
                    pool.wait_ge(cg_exp, 1)
                    G.tensor_scalar(cg_sig, cg_sig, 1.0, None, ALU.add).then_inc(cg_one, 1)
                    pool.wait_ge(br_full, 3 * KD)
                    G.memset(acc, 0.0).then_inc(acc_zero, 1)

                @block.tensor
                def _(pe):
                    def slab_here(n):
                        pe.wait_ge(slab_in[n % RING], 16 * (n // RING))

                    def bank_free(f):
                        if f >= 2:
                            pe.wait_ge(z_read, f - 1)
                        return Z[f % 2]

                    def norm_sum(bank, n):
                        pe.wait_ge(sq_used, n)
                        M.matmul(psum[:, bank, 0:T], ones, sum_sq, start=True, stop=True).then_inc(nsum, 1)

                    def mod_slab(j):
                        n = SLABS.index(("mod", j))
                        f = f_of("mod", j)
                        if n < MOD_AHEAD:
                            pe.wait_ge(mod_in[n], layer * 16 + 16)
                        else:
                            slab_here(n)
                        bank = bank_free(f)
                        for half in range(2):
                            for q in range(4):
                                k = 4 * half + q
                                last = M.matmul(psum[32 * q:32 * q + 32, bank, :], silu_c[:, k, :], ring[:, n % RING, k, :],
                                                start=half == 0, stop=half == 1)
                        last.then_inc(z_full, 1)

                    def mod_transposed(j):
                        f = f_of("modT", j)
                        pe.wait_ge(z_read, max(f_of("mod", j) + 1, f - 1))
                        for c in range(4):
                            last = transpose(psum[:, Z[f % 2], c * P:(c + 1) * P], mod_rows(j)[:, c * P:(c + 1) * P])
                        last.then_inc(z_full, 1)

                    def z_group(g):
                        slab, j, kind = Z_GROUPS[g]
                        n = SLABS.index(("w_in", slab))
                        f = f_of("z", g)
                        if j == 0:
                            slab_here(n)
                        bank = bank_free(f)
                        cols = slice(j * P, (j + 1) * P)
                        for k in range(KD):
                            if g == 0:
                                chunk_ready_wait(pe, 0, k)
                            if kind == "T":
                                last = M.matmul(psum[:, bank, 0:T], ring[:, n % RING, k, cols], hT[:, k, :], start=k == 0, stop=k == KD - 1)
                            else:
                                last = M.matmul(psum[:, bank, :], hT[:, k, cols], ring[:, n % RING, k, :], start=k == 0, stop=k == KD - 1)
                        last.then_inc(z_full, 1)

                    def a_norm(t):
                        f = f_of("norm", t)
                        pe.wait_ge(a_sq, t + 1)
                        M.matmul(psum[:, bank_free(f), 0:T], ones, square[:, t % 2, :], start=True, stop=True).then_inc(z_full, 1)

                    def rotated(c):
                        pe.wait_ge(z_read, f_of("z", c) + 1)
                        if c == 0:
                            pe.wait_ge(rs_ready, 1)
                        if c >= 2:
                            pe.wait_ge(rope_done, c - 1)
                        M.matmul(psum[:, S[c % 2], 0:2 * P], c_("rot"), zT[:, AQ + c, LAT], start=True, stop=True).then_inc(rot_full, 1)

                    def fill(step):
                        for kind, i in step:
                            {"mod": mod_slab, "modT": mod_transposed, "z": z_group, "norm": a_norm}[kind](i)

                    fill(START_FILL[:3])
                    norm_sum(S[0], KD)
                    fill(START_FILL[3:6])
                    pe.wait_ge(small_in, 16 * 2)
                    transpose(psum[:, TR[1], 0:72], vec_rows[:, :]).then_inc(vec_tr, 1)
                    fill(START_FILL[6:])
                    for g in range(Z_FIRST):
                        z_group(g)
                        if g >= 2 and g - 2 < 8:
                            rotated(g - 2)
                    pe.wait_ge(keys_in, 16)
                    for rows, bank in ((akc_rows, O[0]), (bkc_rows, O[1])):
                        for c in range(4):
                            last = transpose(psum[:, bank, c * P:(c + 1) * P], rows[:, c * P:(c + 1) * P])
                        last.then_inc(kc_tr, 1)

                    def keys_in_rows(first, bank):
                        for c in range(4):
                            last = transpose(psum[:, bank, c * P:(c + 1) * P], zT[:, first + c, CTX])
                        last.then_inc(ko_tr, 1)

                    keys_in_rows(AK, TR[0])
                    pe.wait_ge(rope_done, 8)
                    pe.wait_ge(kc_ev, 2)
                    pe.wait_ge(values_in, 16)

                    def scores(n):
                        mixer, u = divmod(n, UNITS)
                        c, b = divmod(u, NBLK)
                        q0, k0 = ((AQ, AK), (BQ, BK))[mixer]
                        kcT = (akcT, bkcT)[mixer]
                        if n >= 1:
                            pe.wait_ge(s_exp, n)
                        halves = [(i, slice(64 * i, 64 * i + 64)) for i in range(2)]
                        for i, part in halves:
                            cols, keys = (slice(0, P), CTX) if b == 0 else (slice(0, 2 * P), LAT)
                            last = M.matmul(psum[:, S[i], cols], zT[part, q0 + c, b * P:(b + 1) * P], zT[part, k0 + c, keys], start=True, stop=True)
                        if b:
                            for i, part in halves:
                                last = M.matmul(psum[:, S[i], 2 * P:T], zT[part, q0 + c, b * P:(b + 1) * P], kcT[part, c, :], start=True, stop=True)
                        last.then_inc(s_full, 1)

                    def probs_transposed(n):
                        mixer, u = divmod(n, UNITS)
                        tiles = 1 if u % NBLK == 0 else 3
                        pe.wait_ge(p_ready, n + 1)
                        if n == 0:
                            pe.wait_ge(ko_ev, 1)
                        else:
                            pe.wait_ge(pT_act, n)
                        if n > UNITS:
                            pe.wait_ge(pT_dve, n - UNITS)
                        for i in range(1 + mixer):
                            for m in range(tiles):
                                last = transpose(psum[:, TR[i], m * P:(m + 1) * P], probs[:, n % 2, i, m * P:(m + 1) * P])
                        last.then_inc(pT_full, 1)

                    def values(n):
                        mixer, u = divmod(n, UNITS)
                        c, b = divmod(u, NBLK)
                        head = 4 * mixer + c
                        pe.wait_ge(pT_act, n + 1)
                        if mixer:
                            pe.wait_ge(pT_dve, n + 1 - UNITS)
                        if b == 0 and head >= 2:
                            pe.wait_ge(o_read, head - 1)
                        elif n == 0:
                            pe.wait_ge(kc_ev, 2)
                        cached = (av_c, bv_c)[mixer]
                        tiles = [(v_rows[:, mixer, 0], 0)] if b == 0 else [
                            (v_rows[:, mixer, 1], 0), (v_rows[:, mixer, 2], 1), (cached, 2)]
                        out = psum[:, O[head % 2], b * P:(b + 1) * P]
                        for v, m in tiles:
                            keys = slice(m * P, (m + 1) * P)
                            if mixer == 0:
                                last = M.matmul(out, v[:, c * P:(c + 1) * P], probsT[:, n % 2, 0, keys], start=m == 0, stop=m == len(tiles) - 1)
                            else:
                                for i in range(2):
                                    last = M.matmul(out[64 * i:64 * i + 64], v[:, (2 * c + i) * 64:(2 * c + i + 1) * 64],
                                                    probsT[:, n % 2, i, keys], start=m == 0, stop=m == len(tiles) - 1)
                        last.then_inc(o_full, 1)

                    for t in range(A_STEPS):
                        if t < UNITS:
                            scores(t)
                        if 1 <= t <= UNITS:
                            probs_transposed(t - 1)
                        if t >= 2:
                            values(t - 2)
                        fill(A_FILL[t])
                    for t in range(A_STEPS):
                        if t < UNITS:
                            scores(UNITS + t)
                        if 1 <= t <= UNITS:
                            probs_transposed(UNITS + t - 1)
                        if t >= 2:
                            values(UNITS + t - 2)
                        fill(B_FILL[t])

                    pe.wait_ge(pT_act, 2 * UNITS)
                    keys_in_rows(BK, TR[0])
                    for b in range(NBLK):
                        for c in range(2):
                            last = transpose(psum[:, S[b // 2], (b % 2) * 2 * P + c * P:(b % 2) * 2 * P + (c + 1) * P],
                                             zT[:, CK + c, b * P:(b + 1) * P])
                    last.then_inc(kr_tr, 1)

                    def gate(m):
                        branch, j = divmod(m, KD)
                        n_gate = 21 + 3 * branch + (0 if j < 4 else 2)
                        if j % 4 == 0:
                            slab_here(n_gate)
                        if m == 0:
                            pe.wait_ge(z_read, FILLERS)
                        else:
                            pe.wait_ge(gate_exp, m)
                        for k in range(KD):
                            last = M.matmul(psum[:, Z[1], 0:T], ring[:, n_gate % RING, k, (j % 4) * P:(j % 4 + 1) * P], hT[:, k, :],
                                            start=k == 0, stop=k == KD - 1)
                        last.then_inc(gate_full, 1)

                    gate(0)
                    pe.wait_ge(ko_ev, 2)
                    pe.wait_ge(pT_dve, UNITS)
                    pe.wait_ge(kr_ev, 4)
                    for kind, b in ((0, 0), (1, 0), (2, 1), (3, 2)):
                        for h in range(HEADS_C):
                            c, i = divmod(h, 2)
                            last = M.matmul(psum[64 * i:64 * i + 64, TR[kind // 2], (kind % 2) * 2 * P + c * P:(kind % 2) * 2 * P + (c + 1) * P],
                                            k_dec[:, kind, h * 64:(h + 1) * 64], v_rows[:, 2, b, h * P:(h + 1) * P], start=True, stop=True)
                        if kind % 2:
                            last.then_inc(st_full, 1)

                    def c_att(h):
                        c, i = divmod(h, 2)
                        part = slice(64 * i, 64 * i + 64)
                        if h >= 2:
                            pe.wait_ge(att_ready, h - 1)
                        for b in range(NBLK):
                            blk = slice(b * P, (b + 1) * P)
                            last = M.matmul(psum[:, S[h % 2], blk], zT[part, CK + c, blk], zT[part, CQ + c, blk], start=True, stop=True)
                        last.then_inc(att_full, 1)

                    def c_out(h):
                        c, i = divmod(h, 2)
                        part = slice(64 * i, 64 * i + 64)
                        pe.wait_ge(att_ready, h + 1)
                        if h == 0:
                            pe.wait_ge(st1_ready, 4)
                            pe.wait_ge(qd_ready, 4)
                            pe.wait_ge(o_read, 8)
                        if h >= 2:
                            pe.wait_ge(co_read, h - 1)
                        for b in range(NBLK):
                            out = psum[:, O[h % 2], b * P:(b + 1) * P]
                            last = M.matmul(out, v_rows[:, 2, b, h * P:(h + 1) * P], att[:, h % 2, b * P:(b + 1) * P], start=True, stop=b == 0)
                            if b:
                                for d in range(2):
                                    state = state0 if (b == 1) == (d == 0) else state1
                                    last = M.matmul(out, state[part, d, c, :], q_dec[part, d, c, (b - 1) * P:b * P], start=False, stop=d == 1)
                        last.then_inc(co_full, 1)

                    def c_mean(h):
                        if h == 0:
                            pe.wait_ge(st_ev, 1)
                        pe.wait_ge(co_read, h + 1)
                        if h >= 1:
                            pe.wait_ge(ccen, h)
                        M.matmul(psum[:, TR[0], 0:T], ones, c_raw[:, h % 2, :], start=True, stop=True).then_inc(cmean_full, 1)

                    def c_var(h):
                        pe.wait_ge(csq, h + 1)
                        if h >= 1:
                            pe.wait_ge(crs, h)
                        M.matmul(psum[:, TR[1], 0:T], ones, square[:, h % 2, :], start=True, stop=True).then_inc(cvar_full, 1)

                    for m in range(3 * KD):
                        branch, j = divmod(m, KD)
                        if m < HEADS_C:
                            c_att(m)
                        if 1 <= m <= HEADS_C:
                            c_out(m - 1)
                        if 2 <= m <= HEADS_C + 1:
                            c_mean(m - 2)
                        if 3 <= m <= HEADS_C + 2:
                            c_var(m - 3)
                        n_proj = 22 + 3 * branch
                        if m >= 1:
                            gate(m)
                        if j == 0:
                            slab_here(n_proj)
                            if branch == 0:
                                pe.wait_ge(a_done, 4)
                            if branch == 2:
                                pe.wait_ge(c_done, 4)
                        if m >= 1:
                            pe.wait_ge(br_read, m)
                        w = slab_into(n_proj)
                        source = (AQ, BQ, CG)[branch]
                        for k in range(4):
                            last = M.matmul(psum[:, Z[0], 0:T], w[:, k, j * P:(j + 1) * P], zT[:, source + k, :], start=k == 0, stop=k == 3)
                        last.then_inc(br_full, 1)

                    for j in range(KD):
                        if j % 4 == 0:
                            slab_here(30 + j // 4)
                        if j >= 2:
                            pe.wait_ge(w_read, j - 1)
                        for k in range(KD):
                            if j == 0:
                                pe.wait_ge(br_read, 2 * KD + k + 1)
                            last = M.matmul(psum[:, S[j % 2], 0:T], ring[:, (30 + j // 4) % RING, k, (j % 4) * P:(j % 4 + 1) * P], merged[:, k, :],
                                            start=k == 0, stop=k == KD - 1)
                        last.then_inc(w_full, 1)

                    norm_sum(TR[0], 2 * KD)
                    pe.wait_ge(router_in, 16)
                    for k in range(KD):
                        chunk_ready_wait(pe, 1, k)
                        q = k % 4
                        last = M.matmul(psum[32 * q:32 * q + 32, TR[1], 0:T], w_r[:, k, :], hT[:, k, :], start=k < 4, stop=k >= 4)
                    last.then_inc(lgT_full, 1)
                    pe.wait_ge(lgT_read, 1)
                    for b in range(NBLK):
                        last = M.matmul(psum[:, TR[0], b * NE:(b + 1) * NE], tmp[:, 1, b * P:(b + 1) * P], c_("gather_experts"), start=True, stop=True)
                    last.then_inc(lg_full, 1)
                    for n in range(2 * NBLK):
                        if n == 2:
                            pe.wait_ge(aff_ready, 1)
                            for b in range(NBLK):
                                last = transpose(psum[0:NE, S[0], b * P:(b + 1) * P], aff[:, b, :])
                            last.then_inc(affT_full, 1)
                        if n >= 2:
                            pe.wait_ge(hr_ev, n - 1)
                        for q in range(4):
                            last = transpose(psum[:, O[n % 2], q * P:(q + 1) * P], hT[:, (n % 2) * 4 + q, (n // 2) * P:(n // 2 + 1) * P])
                        last.then_inc(hr_tr, 1)
                    pe.wait_ge(slots_ready, 2)
                    for b in range(NBLK):
                        last = transpose(psum[:, S[1], b * NE:(b + 1) * NE], place[0:NE, b * P:(b + 1) * P])
                    last.then_inc(slots_tr, 1)
                    pe.wait_ge(hr_ev, 2 * NBLK)

                    def gather(e, blocks):
                        for b in blocks:
                            for half in range(2):
                                last = M.matmul(psum[HALF * half:HALF * (half + 1), O[0], :], pick[:, e, b, :],
                                                h_rows[:, b, half * SLAB:(half + 1) * SLAB], start=b == 0, stop=b == NBLK - 1)
                            if b == NBLK - 1:
                                last.then_inc(xg_full, 1)

                    def gathered_transposed(expert):
                        pe.wait_ge(xg_read, expert + 1)
                        for q in range(4):
                            last = transpose(psum[:, O[1], q * P:(q + 1) * P], xg[:, q * P:(q + 1) * P])
                        last.then_inc(xt_full, 1)

                    def expert_step(pair, e, last_expert):
                        def nth(per_expert, x):
                            return pair * (2 * per_expert) + (e * per_expert + x)

                        def product(s, bank, signal, lhs):
                            w, number = expert_slab(e, s)
                            before = DENSE_SLABS // RING - 1 if number < RING else 0
                            if s == 0:
                                pe.wait_ge(slab_in[number], pair * 16 + 16 * (before + 1))
                            else:
                                pe.wait_ge(slab_in[number], pair * (16 * 2) + 16 * (before + e + 1))
                            for k in range(KD):
                                for half in range(2):
                                    last = M.matmul(psum[HALF * half:HALF * (half + 1), bank, (s % 2) * 256:(s % 2 + 1) * 256], lhs(k),
                                                    w[:, k, half * 256:(half + 1) * 256], start=k == 0, stop=k == KD - 1)
                            last.then_inc(signal, 1)

                        def xg_half(k):
                            return xgT[:, k % 4, k // 4, :]

                        pe.wait_ge(xt_read, nth(1, 1))
                        for s in range(2):
                            product(s, S[0], gate_h, xg_half)
                        if last_expert:
                            pe.wait_ge(sc_read, KD * (NE - 1))
                        else:
                            pe.wait_ge(pick_ready, nth(1, 2))
                        pe.wait_ge(pick_g_ready, nth(1, 1))
                        for b in range(NBLK):
                            last = transpose(psum[:, O[0], b * P:(b + 1) * P], pick_g[:, e, b, :])
                        last.then_inc(pgT_full, 1)
                        for s in range(2, 4):
                            product(s, S[1], up_h, xg_half)
                        pe.wait_ge(pgT_read, nth(1, 1))
                        if not last_expert:
                            gather(1 - e, (0, 1))
                        pe.wait_ge(hid_ready, nth(1, 1))
                        for q in range(4):
                            last = transpose(psum[:, TR[0], q * P:(q + 1) * P], hid[:, q * P:(q + 1) * P])
                        last.then_inc(ht_full, 1)
                        if not last_expert:
                            gather(1 - e, (2,))
                        pe.wait_ge(ht_read, nth(1, 1))
                        for s in range(4, 6):
                            product(s, TR[1], down_full, lambda k: hidT[:, 2 * (k // 4) + k % 2, (k // 2) % 2, :])
                        if not last_expert:
                            gathered_transposed(pair * 2 + (e + 1))
                        pe.wait_ge(down_read, nth(1, 1))
                        for q in range(4):
                            if q >= 2:
                                pe.wait_ge(sc_read, nth(KD, 2 * (q - 1)))
                            elif q == 1 and not last_expert:
                                pe.wait_ge(xt_read, nth(1, 2))
                            for half in range(2):
                                part = slice(HALF * half, HALF * (half + 1))
                                M.matmul(psum[:, (Z, O)[q % 2][half], 0:T], out_rows[part, q * P:(q + 1) * P], pick_gT[part, :],
                                         start=True, stop=True).then_inc(sc_full, 1)

                    pe.wait_ge(pick_ready, 1)
                    gather(0, range(NBLK))
                    gathered_transposed(0)
                    with pe.Fori(0, NE // 2 - 1) as pair:
                        for e in range(2):
                            expert_step(pair, e, False)
                    for e in range(2):
                        expert_step(NE // 2 - 1, e, e == 1)

                @block.scalar
                def _(sc):
                    link = chain(sc, act_link)

                    def squares(first):
                        for k in range(KD):
                            if first + k >= 2:
                                sc.wait_ge(sq_used, first + k - 1)
                            if first:
                                sc.wait_ge(w_read, k + 1)
                            A_.activation(square[:, k % 2, :], xT[:, k, :], ACT.Square).then_inc(sq_ready, 1)

                    def inverse_rms(bank, n):
                        sc.wait_ge(nsum, n)
                        link(A_.activation(rs[:], psum[:, bank, 0:T], ACT.Ln, scale=1.0 / D, bias=c_("eps")))
                        A_.activation(rs[:], rs[:], ACT.Exp, scale=-0.5).then_inc(rs_ready, 1)

                    def modulate(mixer, scale, shift):
                        for k in range(KD):
                            if k not in DVE_MODULATES[mixer]:
                                sc.wait_ge(norm_mul, mixer * KD + k + 1)
                                for g, cols in enumerate((CTX, LAT)):
                                    last = A_.activation(hT[:, k, cols], hT[:, k, cols], ACT.Identity,
                                                         bias=modT[:, shift + k, g:g + 1], scale=scale[:, k, g:g + 1])
                                last.then_inc(h_act, 1)

                    squares(0)
                    def read_mod(j):
                        f = f_of("mod", j)
                        sc.wait_ge(z_full, f + 1)
                        if j == 4:
                            sc.wait_ge(a_done, 4)
                        A_.activation(mod_rows(j), psum[:, Z[f % 2], :], ACT.Copy).then_inc(z_read, 1)

                    def read_modT(j):
                        f = f_of("modT", j)
                        sc.wait_ge(z_full, f + 1)
                        A_.activation(mod_parts(j).rearrange("p (c q g) -> p c q g", c=4, q=4),
                                      psum[:, Z[f % 2], :].rearrange("p (c q w) -> p c q w", c=4, q=4)[:, :, :, 0:2],
                                      ACT.Copy).then_inc(z_read, 1)

                    def read_z(g):
                        slab, j, kind = Z_GROUPS[g]
                        f = f_of("z", g)
                        sc.wait_ge(z_full, f + 1)
                        if kind == "rows":
                            mixer = {2: 0, 5: 1, 7: 2}[slab]
                            A_.activation(v_rows[:, mixer, j, :], psum[:, Z[f % 2], :], ACT.Copy).then_inc(z_read, 1)
                        else:
                            chunk = {0: AQ, 1: AK, 3: BQ, 4: BK, 6: CQ, 8: CG}[slab] + j
                            s = SCALE if chunk in (CK, CK + 1) else 1.0
                            A_.activation(zT[:, chunk, :], psum[:, Z[f % 2], 0:T], ACT.Copy, scale=s).then_inc(z_read, 1)

                    def read_norm(t):
                        f = f_of("norm", t)
                        sc.wait_ge(z_full, f + 1)
                        if t >= 2:
                            sc.wait_ge(a_done, t - 1)
                        A_.activation(tmp[:, t % 2, :], psum[:, Z[f % 2], 0:T], ACT.Ln, scale=1.0 / P, bias=c_("eps")).then_inc(z_read, 1)
                        sc.wait_ge(z_read, f + 1)
                        A_.activation(tmp[:, t % 2, :], tmp[:, t % 2, :], ACT.Exp, scale=-0.5).then_inc(nrs, 1)

                    def read(step):
                        for kind, i in step:
                            {"mod": read_mod, "modT": read_modT, "z": read_z, "norm": read_norm}[kind](i)

                    read(START_FILL[:3])
                    inverse_rms(S[0], 1)
                    read(START_FILL[3:])
                    sc.wait_ge(mod1_ready, 1)
                    modulate(0, scale_mix, 0)
                    sc.wait_ge(lam_sum, 1)
                    A_.activation(lamb[:, 2:4], lamb[:, 0:2], ACT.Exp).then_inc(lam_exp, 1)
                    sc.wait_ge(abs_ready, 1)
                    link(A_.activation(decay_t[:, 1], decay_t[:, 0], ACT.Exp, scale=-1.0))
                    A_.activation(decay_t[:, 2], decay_t[:, 1], ACT.Ln, bias=c_("one")).then_inc(ln_ready, 1)
                    sc.wait_ge(decay_ready, 1)
                    for h in range(HEADS_C):
                        A_.activation(in_decay[:, h], c_("below"), ACT.Exp, scale=decay[:, h:h + 1])
                        last = A_.activation(bwd_decay[:, h], c_("above"), ACT.Exp, scale=decay[:, 4 + h:5 + h])
                    last.then_inc(decay_exp, 1)
                    for d, (row, col) in enumerate((("since", "k_until"), ("until", "k_since"))):
                        for c in range(2):
                            for i in range(2):
                                part = slice(64 * i, 64 * i + 64)
                                h = 4 * d + 2 * c + i
                                A_.activation(q_decay[part, d, c, :], c_(row)[part], ACT.Exp, scale=decay[part, h:h + 1])
                        A_.activation(k_decay[:, d, :], decay[:, 4 * d:4 * d + 4], ACT.Exp, scale=c_(col))
                    for i in range(2):
                        part = slice(64 * i, 64 * i + 64)
                        last = A_.activation(chunk_decay[part], decay[part].rearrange("p (d c i) -> p d c i", d=2, c=2)[:, :, :, i],
                                             ACT.Exp, scale=float(P))
                    last.then_inc(chunk_ready, 1)
                    for g in range(11):
                        read_z(g)
                    for n, (dst, bank) in enumerate(((akcT, O[0]), (bkcT, O[1]))):
                        sc.wait_ge(kc_tr, n + 1)
                        A_.activation(dst[:].rearrange("p c t -> p (c t)"), psum[:, bank, :], ACT.Copy).then_inc(kc_ev, 1)
                    sc.wait_ge(z_read, f_of("z", 10) + 1)
                    sc.dma_start(new_av[layer], v_rows[:, 0, 0, :]).then_inc(v_stored, 16)
                    sc.wait_ge(ko_tr, 1)
                    sc.wait_ge(in_decay_ready, 1)
                    A_.activation(keys_out, psum[:, TR[0], :], ACT.Copy).then_inc(ko_ev, 1)
                    sc.wait_ge(ko_ev, 1)
                    sc.dma_start(new_ak[layer], keys_out).then_inc(ko_st, 16)

                    def exps(n):
                        mixer, u = divmod(n, UNITS)
                        b = u % NBLK
                        keys = P if b == 0 else T
                        own = mixer == 0 or b == 0
                        sc.wait_ge(s_max, n + 1)
                        if own and n >= 2:
                            sc.wait_ge(pT_full, n - 1)
                        for i in range(2):
                            dst = probs[:, n % 2, i, 0:keys]
                            last = A_.activation(dst, psum[:, S[i], 0:keys] if own else dst, ACT.Exp,
                                                 bias=small[:, n % 2, i:i + 1], scale=SCALE if own else 1.0,
                                                 accum_out=small[:, n % 2, 2 + i:3 + i])
                        last.then_inc(s_exp, 1)

                    def read_pT(n):
                        keys = P if n % NBLK == 0 else T
                        sc.wait_ge(pT_full, n + 1)
                        if n >= 2:
                            sc.wait_ge(o_full, n - 1)
                        A_.activation(probsT[:, n % 2, 0, 0:keys], psum[:, TR[0], 0:keys], ACT.Copy).then_inc(pT_act, 1)

                    def read_o(n):
                        mixer, u = divmod(n, UNITS)
                        if u % NBLK == NBLK - 1:
                            c = u // NBLK
                            sc.wait_ge(o_full, n + 1)
                            A_.activation(zT[:, (AQ, BQ)[mixer] + c, :], psum[:, O[c % 2], 0:T], ACT.Copy).then_inc(o_read, 1)

                    for t in range(A_STEPS):
                        if t < UNITS:
                            exps(t)
                        if 1 <= t <= UNITS:
                            read_pT(t - 1)
                        if t >= 2:
                            read_o(t - 2)
                        read(A_FILL[t])
                        if t == 10:
                            sc.wait_ge(z_read, f_of("z", 21) + 1)
                            sc.dma_start(new_bv[layer], v_rows[:, 1, 0, :]).then_inc(v_stored, 16)
                    for t in range(A_STEPS):
                        if t < 4:
                            sc.wait_ge(o_read, t + 1)
                            A_.activation(square[:, t % 2, :], zT[:, AQ + t, :], ACT.Square).then_inc(a_sq, 1)
                        if t < UNITS:
                            exps(UNITS + t)
                        if 1 <= t <= UNITS:
                            read_pT(UNITS + t - 1)
                        if t >= 2:
                            read_o(UNITS + t - 2)
                        read(B_FILL[t])

                    sc.wait_ge(ko_tr, 2)
                    sc.wait_ge(ko_st, 16)
                    A_.activation(keys_out, psum[:, TR[0], :], ACT.Copy).then_inc(ko_ev, 1)
                    sc.wait_ge(ko_ev, 2)
                    sc.dma_start(new_bk[layer], keys_out).then_inc(ko_st, 16)
                    sc.wait_ge(v_stored, 32)
                    sc.wait_ge(o_full, 2 * UNITS)
                    sc.wait_ge(z_read, f_of("z", 32) + 1)
                    A_.activation(cg_sig, zT[:, CG:CG + 4, :].rearrange("p c t -> p (c t)"), ACT.Exp, scale=-1.0).then_inc(cg_exp, 1)
                    sc.wait_ge(st_full, 1)
                    A_.activation(ctx_state.rearrange("p d c e -> p (d c e)"), psum[:, TR[0], :], ACT.Copy).then_inc(st_ev, 1)
                    sc.wait_ge(st_ev, 1)
                    for d, out in enumerate((new_sf, new_sb)):
                        sc.dma_start(out[layer].rearrange("(c i) k e -> (i k) c e", c=2), ctx_state[:, d]).then_inc(stored, 16)

                    for m in range(3 * KD):
                        if 2 <= m <= HEADS_C + 1:
                            h = m - 2
                            sc.wait_ge(ccen, h + 1)
                            A_.activation(square[:, h % 2, :], c_raw[:, h % 2, :], ACT.Square).then_inc(csq, 1)
                        if 3 <= m <= HEADS_C + 2:
                            h = m - 3
                            sc.wait_ge(cvar_full, h + 1)
                            if h >= 2:
                                sc.wait_ge(c_done, h - 1)
                            A_.activation(c_rs[:, h % 2, :], psum[:, TR[1], 0:T], ACT.Ln, scale=1.0 / P, bias=c_("eps")).then_inc(crs, 1)
                            sc.wait_ge(crs, h + 1)
                            A_.activation(c_rs[:, h % 2, :], c_rs[:, h % 2, :], ACT.Exp, scale=-0.5).then_inc(crs_read, 1)
                        if 1 <= m <= HEADS_C:
                            h = m - 1
                            sc.wait_ge(co_full, h + 1)
                            if h >= 2:
                                sc.wait_ge(c_done, h - 1)
                            A_.activation(c_raw[:, h % 2, :], psum[:, O[h % 2], 0:T], ACT.Copy).then_inc(co_read, 1)
                        sc.wait_ge(gate_full, m + 1)
                        if m >= 2:
                            sc.wait_ge(br_read, m - 1)
                        A_.activation(gate_e[m % 2], psum[:, Z[1], 0:T], ACT.Exp, scale=-1.0).then_inc(gate_exp, 1)

                    squares(KD)
                    inverse_rms(TR[0], 2)
                    modulate(1, scale_ffn, 24)
                    sc.wait_ge(lg_max, 1)
                    A_.activation(aff, aff, ACT.Exp).then_inc(lg_exp, 1)
                    for n in range(2 * NBLK):
                        sc.wait_ge(hr_tr, n + 1)
                        A_.activation(h_rows[:, n // 2, (n % 2) * 512:(n % 2 + 1) * 512], psum[:, O[n % 2], :], ACT.Copy).then_inc(hr_ev, 1)

                    sc.wait_ge(ko_st, 32)
                    sc.wait_ge(stored, 32)
                    A_.preload_act_table(ACT.Silu)

                    def read_gathered(expert):
                        sc.wait_ge(xg_full, expert + 1)
                        A_.activation(xg, psum[:, O[0], :], ACT.Copy).then_inc(xg_read, 1)

                    def expert_step(pair, e, last_expert):
                        expert = pair * 2 + e
                        sc.wait_ge(gate_h, pair * 4 + (2 * e + 2))
                        A_.activation(act, psum[:, S[0], :], ACT.Silu).then_inc(silu_ready, 1)
                        sc.wait_ge(ht_full, expert + 1)
                        A_.activation(hidT.rearrange("p q h s -> p (q h s)"), psum[:, TR[0], :], ACT.Copy).then_inc(ht_read, 1)
                        if not last_expert:
                            read_gathered(pair * 2 + (e + 1))
                        sc.wait_ge(down_full, pair * 4 + (2 * e + 2))
                        A_.activation(out_rows, psum[:, TR[1], :], ACT.Copy).then_inc(down_read, 1)

                    read_gathered(0)
                    with sc.Fori(0, NE // 2 - 1) as pair:
                        for e in range(2):
                            expert_step(pair, e, False)
                    for e in range(2):
                        expert_step(NE // 2 - 1, e, e == 1)
                    A_.preload_act_table_set("natural_log_exp_and_others")

                @block.vector
                def _(dve):
                    then = chain(dve, dve_link)

                    def normed(mixer, is_modulated, scale, shift):
                        dve.wait_ge(rs_ready, 1 + mixer)
                        for k in range(KD):
                            V.tensor_tensor(hT[:, k, :], xT[:, k, :], rs[:], ALU.mult).then_inc(norm_mul, 1)
                        is_modulated()
                        for k in DVE_MODULATES[mixer]:
                            dve.wait_ge(norm_mul, mixer * KD + k + 1)
                            for g, cols in enumerate((CTX, LAT)):
                                last = V.tensor_scalar(hT[:, k, cols], hT[:, k, cols], scale[:, k, g:g + 1], modT[:, shift + k, g:g + 1],
                                                       ALU.mult, ALU.add)
                            last.then_inc(h_dve, 1)

                    def first_modulation():
                        dve.wait_ge(vec_tr, 1)
                        V.tensor_copy(vecT[:], psum[:, TR[1], 0:72]).then_inc(vec_ready, 1)
                        dve.wait_ge(vec_ready, 1)
                        dve.wait_ge(z_read, f_of("modT", 3) + 1)
                        then(V.reduce_sum(modT[:, 0:16, :], parts_start.rearrange("p (c q g) -> p c g q", q=4, g=2), axis=AX_X))
                        then(V.tensor_tensor(modT[:, 0:16, :], modT[:, 0:16, :], vecT[:, 0:16].unsqueeze(2).to_broadcast([P, 16, 2]), ALU.add))
                        V.scalar_tensor_tensor(out=scale_mix[:], in0=modT[:, 8:16, :], scalar=1.0,
                                               in1=vecT[:, 48:56].unsqueeze(2).to_broadcast([P, KD, 2]), op0=ALU.add, op1=ALU.mult).then_inc(mod1_ready, 1)
                        dve.wait_ge(mod1_ready, 1)

                    sum_squares(dve, 0)
                    normed(0, first_modulation, scale_mix, 0)

                    dve.wait_ge(small_in, 16 * 2)
                    pairs = lam_rows.rearrange("p (a i) d -> p a i d", i=2)
                    prod = gate_e[0][:, 0:P].rearrange("p (a d) -> p a d", a=2)
                    then(V.tensor_tensor(prod, pairs[:, :, 0, :], pairs[:, :, 1, :], ALU.mult))
                    V.reduce_sum(lamb[:, 0:2], prod, axis=AX_X).then_inc(lam_sum, 1)
                    then(V.tensor_scalar(decay_t[:, 3], decay, -1.0, None, ALU.mult))
                    V.tensor_tensor(decay_t[:, 0], decay, decay_t[:, 3], ALU.max).then_inc(abs_ready, 1)
                    dve.wait_ge(lam_exp, 1)
                    then(V.tensor_tensor(lamb[:, 4:5], lamb[:, 3:4], lamb[:, 2:3], ALU.subtract))
                    then(V.tensor_tensor(lamb[:, 5:6], lamb[:, 4:5], layer_c[:, 0:1], ALU.subtract))
                    then(V.tensor_scalar(gain_a[:], vecT[:, 64:68], layer_c[:, 1:2], None, ALU.mult))
                    dve.wait_ge(ln_ready, 1)
                    then(V.tensor_scalar(decay_t[:, 3], decay, 0.0, None, ALU.min))
                    V.tensor_tensor(decay, decay_t[:, 3], decay_t[:, 2], ALU.subtract).then_inc(decay_ready, 1)
                    dve.wait_ge(decay_ready, 1)

                    for c in range(8):
                        dve.wait_ge(rot_full, c + 1)
                        if c >= 2:
                            dve.wait_ge(rope_done, c - 1)
                        then(V.tensor_tensor(tmp[:, c % 2, 0:2 * P], psum[:, S[c % 2], 0:2 * P], c_("sin"), ALU.mult))
                        then(V.tensor_tensor(zT[:, AQ + c, LAT], zT[:, AQ + c, LAT], c_("cos"), ALU.mult))
                        V.tensor_tensor(zT[:, AQ + c, LAT], zT[:, AQ + c, LAT], tmp[:, c % 2, 0:2 * P], ALU.add).then_inc(rope_done, 1)

                    def row_max(n):
                        mixer, u = divmod(n, UNITS)
                        c, b = divmod(u, NBLK)
                        keys = P if b == 0 else T
                        dve.wait_ge(s_full, n + 1)
                        if mixer == 0 or b == 0:
                            for i in range(2):
                                then(V.reduce_max(small[:, n % 2, 4 + i:5 + i], psum[:, S[i], 0:keys], axis=AX_X))
                            V.tensor_scalar(small[:, n % 2, 0:2], small[:, n % 2, 4:6], -SCALE, None, ALU.mult).then_inc(s_max, 1)
                        else:
                            dve.wait_ge(pT_full, n - 1)
                            if n < UNITS + 3:
                                dve.wait_ge(bias_ready, 2)
                            for i in range(2):
                                h = 2 * c + i
                                own = probs[:, n % 2, i, 0:2 * P].rearrange("p (r c) -> p r c", r=4)
                                V.scalar_tensor_tensor(out=own, in0=psum[:, S[i], 0:2 * P].rearrange("p (r c) -> p r c", r=4), scalar=SCALE,
                                                       in1=bias[b - 1][:, h::HEADS_B, ::-1], op0=ALU.mult, op1=ALU.add)
                                then(V.tensor_scalar(probs[:, n % 2, i, 2 * P:T], psum[:, S[i], 2 * P:T], SCALE, None, ALU.mult))
                            then(V.reduce_max(small[:, n % 2, 4:6], probs[:, n % 2, :, :], axis=AX_X))
                            V.tensor_scalar(small[:, n % 2, 0:2], small[:, n % 2, 4:6], -1.0, None, ALU.mult).then_inc(s_max, 1)

                    def normalise(n):
                        mixer, u = divmod(n, UNITS)
                        keys = P if u % NBLK == 0 else T
                        dve.wait_ge(s_exp, n + 1)
                        then(V.reciprocal(small[:, n % 2, 4:6], small[:, n % 2, 2:4]))
                        p0, p1 = probs[:, n % 2, 0, 0:keys], probs[:, n % 2, 1, 0:keys]
                        if mixer == 0:
                            then(V.tensor_tensor(small[:, n % 2, 6:7], small[:, n % 2, 5:6], lamb[:, 5:6], ALU.mult))
                            then(V.tensor_scalar(p1, p1, small[:, n % 2, 6:7], None, ALU.mult))
                            V.scalar_tensor_tensor(out=p0, in0=p0, scalar=small[:, n % 2, 4:5], in1=p1, op0=ALU.mult, op1=ALU.add).then_inc(p_ready, 1)
                        else:
                            V.tensor_scalar(p0, p0, small[:, n % 2, 4:5], None, ALU.mult)
                            V.tensor_scalar(p1, p1, small[:, n % 2, 5:6], None, ALU.mult).then_inc(p_ready, 1)

                    for n in range(UNITS):
                        row_max(n)
                        normalise(n)
                    for t in range(A_STEPS):
                        if t < UNITS:
                            row_max(UNITS + t)
                            normalise(UNITS + t)
                        if 1 <= t <= UNITS:
                            n = UNITS + t - 1
                            keys = P if n % NBLK == 0 else T
                            dve.wait_ge(pT_full, n + 1)
                            dve.wait_ge(o_full, n - 1)
                            V.tensor_copy(probsT[:, n % 2, 1, 0:keys], psum[:, TR[1], 0:keys]).then_inc(pT_dve, 1)
                        if t < 4:
                            dve.wait_ge(nrs, t + 1)
                            V.scalar_tensor_tensor(out=zT[:, AQ + t, :], in0=zT[:, AQ + t, :], scalar=gain_a[:, t:t + 1],
                                                   in1=tmp[:, t % 2, :], op0=ALU.mult, op1=ALU.mult).then_inc(a_done, 1)

                    dve.wait_ge(o_full, 2 * UNITS)
                    dve.wait_ge(kr_tr, 1)
                    dve.wait_ge(chunk_ready, 1)
                    heads = [P, 4, 64]
                    for kind, (b, d) in enumerate(((0, 0), (0, 1), (1, 0), (2, 1))):
                        rows = psum[:, S[b // 2], (b % 2) * 2 * P:(b % 2 + 1) * 2 * P].rearrange("p (h e) -> p h e", h=4)
                        V.tensor_tensor(k_dec[:, kind, :].rearrange("p (h e) -> p h e", h=4), rows,
                                        k_decay[:, d, :].unsqueeze(2).to_broadcast(heads), ALU.mult).then_inc(kr_ev, 1)
                    for d in range(2):
                        for c in range(2):
                            V.tensor_tensor(q_dec[:, d, c, :].rearrange("p (b t) -> p b t", b=2),
                                            zT[:, CQ + c, LAT].rearrange("p (b t) -> p b t", b=2),
                                            q_decay[:, d, c, :].unsqueeze(1).to_broadcast([P, 2, P]), ALU.mult).then_inc(qd_ready, 1)
                    dve.wait_ge(st_full, 2)
                    dve.wait_ge(state_in, 32)
                    for d in range(2):
                        for c in range(2):
                            V.scalar_tensor_tensor(out=state1[:, d, c, :], in0=state0[:, d, c, :], scalar=chunk_decay[:, d, c:c + 1],
                                                   in1=psum[:, TR[1], d * 2 * P + c * P:d * 2 * P + (c + 1) * P],
                                                   op0=ALU.mult, op1=ALU.add).then_inc(st1_ready, 1)
                    dve.wait_ge(z_read, FILLERS)
                    then(V.reduce_sum(modT[:, 16:48, :], rs[:, 0:2 * P].rearrange("p (c q g) -> p c g q", q=4, g=2), axis=AX_X))
                    then(V.tensor_tensor(modT[:, 16:48, :], modT[:, 16:48, :], vecT[:, 16:48].unsqueeze(2).to_broadcast([P, 32, 2]), ALU.add))
                    V.scalar_tensor_tensor(out=scale_ffn[:], in0=modT[:, 32:40, :], scalar=1.0,
                                           in1=vecT[:, 56:64].unsqueeze(2).to_broadcast([P, KD, 2]), op0=ALU.add, op1=ALU.mult).then_inc(mod2_ready, 1)
                    dve.wait_ge(mod2_ready, 1)
                    dve.wait_ge(in_decay_ready, 1)

                    for m in range(3 * KD):
                        branch, j = divmod(m, KD)
                        if m < HEADS_C:
                            dve.wait_ge(att_full, m + 1)
                            if m >= 2:
                                dve.wait_ge(co_full, m - 1)
                            blocks = [P, NBLK, P]
                            V.tensor_tensor(att[:, m % 2, :].rearrange("p (b t) -> p b t", b=NBLK),
                                            psum[:, S[m % 2], 0:T].rearrange("p (b t) -> p b t", b=NBLK),
                                            in_decay[:, m, :].unsqueeze(1).to_broadcast(blocks), ALU.mult).then_inc(att_ready, 1)
                        if m < HEADS_C:
                            cg, sig = zT[:, CG + m, :], cg_sig[:, m * T:(m + 1) * T]
                            dve.wait_ge(cg_one, 1)
                            then(V.reciprocal(sig, sig))
                            then(V.tensor_tensor(cg, cg, sig, ALU.mult))
                        if 2 <= m <= HEADS_C + 1:
                            h = m - 2
                            dve.wait_ge(cmean_full, h + 1)
                            V.scalar_tensor_tensor(out=c_raw[:, h % 2, :], in0=psum[:, TR[0], 0:T], scalar=-1.0 / P, in1=c_raw[:, h % 2, :],
                                                   op0=ALU.mult, op1=ALU.add).then_inc(ccen, 1)
                        if 3 <= m <= HEADS_C + 2:
                            h = m - 3
                            dve.wait_ge(crs_read, h + 1)
                            then(V.tensor_tensor(c_rs[:, h % 2, :], c_rs[:, h % 2, :], c_raw[:, h % 2, :], ALU.mult))
                            V.scalar_tensor_tensor(out=zT[:, CG + h, :], in0=c_rs[:, h % 2, :], scalar=vecT[:, 68 + h:69 + h],
                                                   in1=zT[:, CG + h, :], op0=ALU.mult, op1=ALU.mult).then_inc(c_done, 1)
                        g = gate_e[m % 2]
                        dve.wait_ge(gate_exp, m + 1)
                        then(V.tensor_scalar(g, g, 1.0, None, ALU.add))
                        then(V.reciprocal(g, g))
                        dve.wait_ge(br_full, m + 1)
                        if branch == 0:
                            V.tensor_tensor(merged[:, j, :], g, psum[:, Z[0], 0:T], ALU.mult).then_inc(br_read, 1)
                        else:
                            then(V.tensor_tensor(g, g, psum[:, Z[0], 0:T], ALU.mult))
                            V.tensor_tensor(merged[:, j, :], merged[:, j, :], g, ALU.add).then_inc(br_read, 1)

                    def add_square(k):
                        dve.wait_ge(sq_ready, KD + k + 1)
                        if k:
                            dve.wait_ge(sq_used, KD + k)
                            V.tensor_tensor(sum_sq, sum_sq, square[:, k % 2, :], ALU.add).then_inc(sq_used, 1)
                        else:
                            V.tensor_copy(sum_sq, square[:, 0, :]).then_inc(sq_used, 1)

                    for j in range(KD):
                        dve.wait_ge(w_full, j + 1)
                        for g, cols in enumerate((CTX, LAT)):
                            last = V.scalar_tensor_tensor(out=xT[:, j, cols], in0=psum[:, S[j % 2], cols], scalar=modT[:, 16 + j, g:g + 1],
                                                          in1=xT[:, j, cols], op0=ALU.mult, op1=ALU.add)
                        last.then_inc(w_read, 1)
                        if j >= 2:
                            add_square(j - 2)
                    add_square(KD - 2)
                    add_square(KD - 1)
                    dve.wait_ge(w_read, KD)
                    normed(1, lambda: None, scale_ffn, 24)

                    dve.wait_ge(lgT_full, 1)
                    V.tensor_copy(tmp[:, 1, :], psum[:, TR[1], 0:T]).then_inc(lgT_read, 1)
                    dve.wait_ge(lg_full, 1)
                    logits = psum[:, TR[0], 0:NBLK * NE].rearrange("p (b e) -> p b e", b=NBLK)
                    per_block = small[:].rearrange("p a b -> p (a b)")
                    wide = [P, NBLK, NE]
                    then(V.reduce_max(per_block[:, 0:3], logits, axis=AX_X))
                    V.tensor_tensor(aff, logits, per_block[:, 0:3].unsqueeze(2).to_broadcast(wide), ALU.subtract).then_inc(lg_max, 1)
                    dve.wait_ge(lg_exp, 1)
                    then(V.reduce_sum(per_block[:, 4:7], aff, axis=AX_X))
                    then(V.reciprocal(per_block[:, 8:11], per_block[:, 4:7]))
                    V.tensor_tensor(aff, aff, per_block[:, 8:11].unsqueeze(2).to_broadcast(wide), ALU.mult).then_inc(aff_ready, 1)
                    dve.wait_ge(affT_full, 1)
                    rows = slice(0, NE)
                    then(V.tensor_copy(left[rows], psum[rows, S[0], 0:T]))
                    parts = ((CTX, CAP_CTX, 0), (LAT, CAP_LAT, CAP_CTX))
                    steps = [0, 0]

                    def then_of(part, ins):
                        steps[part] += 1
                        ins.then_inc(top_link[part], 1)

                    def wait_for(part):
                        if steps[part]:
                            dve.wait_ge(top_link[part], steps[part])

                    for r in range(CAP_LAT // 8):
                        for part, (cols, cap, first) in enumerate(parts):
                            if r < cap // 8:
                                wait_for(part)
                                then_of(part, V.max(best[rows, 8 * part:8 * part + 8], left[rows, cols]))
                        for part, (cols, cap, first) in enumerate(parts):
                            if r < cap // 8:
                                wait_for(part)
                                then_of(part, V.match_replace(left[rows, cols], best[rows, 8 * part:8 * part + 8], left[rows, cols], -1.0))
                    for part, (cols, cap, first) in enumerate(parts):
                        wait_for(part)
                        then_of(part, V.tensor_scalar(chosen[rows, cols], left[rows, cols], 0.0, None, ALU.is_lt))
                    for part, (cols, cap, first) in enumerate(parts):
                        wait_for(part)
                        then_of(part, V.tensor_tensor_scan(place[rows, cols], chosen[rows, cols], chosen[rows, cols], float(first), ALU.add, ALU.max))
                    for part, (cols, cap, first) in enumerate(parts):
                        wait_for(part)
                        V.tensor_tensor(place[rows, cols], place[rows, cols], chosen[rows, cols], ALU.mult).then_inc(slots_ready, 1)
                    dve.wait_ge(slots_tr, 1)
                    V.tensor_copy(slot_of, psum[:, S[1], 0:NBLK * NE].rearrange("p (b e) -> p b e", b=NBLK)).then_inc(slots_ev, 1)
                    dve.wait_ge(slots_ev, 1)
                    dve.wait_ge(acc_zero, 1)

                    def choose(e, expert):
                        column = bass.ds(expert, 1)
                        for b in range(NBLK):
                            last = V.tensor_scalar(pick[:, e, b, :], c_("slot"), slot_of[:, b, column], None, ALU.is_equal)
                        last.then_inc(pick_ready, 1)
                        for b in range(NBLK):
                            last = V.tensor_scalar(pick_g[:, e, b, :].rearrange("p (h s) -> p h s", h=2), c_("slot").unsqueeze(1).to_broadcast([P, 2, HALF]),
                                                   slot_of[:, b, column], aff[:, b, column], ALU.is_equal, ALU.mult)
                        last.then_inc(pick_g_ready, 1)

                    def read_gatheredT(expert):
                        dve.wait_ge(xt_full, expert + 1)
                        V.tensor_copy(xgT.rearrange("p q h s -> p (q h s)"), psum[:, O[1], :]).then_inc(xt_read, 1)

                    def residual(k, experts_sum):
                        for g, cols in enumerate((CTX, LAT)):
                            last = V.scalar_tensor_tensor(out=xT[:, k, cols], in0=experts_sum[:, cols], scalar=modT[:, 40 + k, g:g + 1],
                                                          in1=xT[:, k, cols], op0=ALU.mult, op1=ALU.add)
                        return last

                    def expert_step(pair, e, last_expert):
                        expert = pair * 2 + e
                        if not last_expert:
                            choose(1 - e, pair * 2 + (e + 1))
                        dve.wait_ge(pgT_full, expert + 1)
                        V.tensor_copy(pick_gT, psum[:, O[0], 0:T]).then_inc(pgT_read, 1)
                        dve.wait_ge(silu_ready, expert + 1)
                        dve.wait_ge(up_h, pair * 4 + (2 * e + 2))
                        V.tensor_tensor(hid, act, psum[:, S[1], :], ALU.mult).then_inc(hid_ready, 1)
                        if not last_expert:
                            read_gatheredT(pair * 2 + (e + 1))
                        if last_expert:
                            dve.wait_ge(sc_read, (NE - 1) * KD)
                            for chunk in SCATTER_ORDER:
                                residual(chunk, acc[:, chunk, :]).then_inc(acc_added, 1)
                        for q in range(4):
                            for half in range(2):
                                n = 2 * q + half
                                chunk = SCATTER_ORDER[n]
                                tokens = psum[:, (Z, O)[q % 2][half], 0:T]
                                dve.wait_ge(sc_full, pair * (2 * KD) + (e * KD + n + 1))
                                if last_expert:
                                    dve.wait_ge(acc_added, n + 1)
                                    residual(chunk, tokens).then_inc(sc_read, 1)
                                else:
                                    V.tensor_tensor(acc[:, chunk, :], acc[:, chunk, :], tokens, ALU.add).then_inc(sc_read, 1)

                    choose(0, 0)
                    read_gatheredT(0)
                    with dve.Fori(0, NE // 2 - 1) as pair:
                        for e in range(2):
                            expert_step(pair, e, False)
                    for e in range(2):
                        expert_step(NE // 2 - 1, e, e == 1)

            clear_all(sems)

        BY_DVE = (3, 5)

        def wait_copied(eng, n):
            if n in BY_DVE:
                eng.wait_ge(rows_dve, BY_DVE.index(n) + 1)
            else:
                eng.wait_ge(rows_act, sum(i not in BY_DVE for i in range(n)) + 1)

        y_rows = hT[:].rearrange("p k t -> p (k t)").rearrange("p (b d) -> p b d", b=NBLK)
        with nc.Block() as block:
            @block.sync
            def _(sp):
                for n in range(2 * NBLK):
                    half, b = divmod(n, NBLK)
                    wait_copied(sp, n)
                    cols = slice(half * SLAB, (half + 1) * SLAB)
                    sp.dma_start(y_out[b * P:(b + 1) * P, cols], y_rows[:, b, cols]).then_inc(stored, 16)
                sp.wait_ge(stored, 16 * 2 * NBLK)
                for s in mod_in:
                    sp.wait_ge(s, 16 * (DEPTH + 1))

            @block.scalar
            def _(sc):
                for k in range(KD):
                    if k >= 2:
                        sc.wait_ge(sq_used, k - 1)
                    A_.activation(square[:, k % 2, :], xT[:, k, :], ACT.Square).then_inc(sq_ready, 1)
                sc.wait_ge(nsum, 1)
                link = chain(sc, act_link)
                link(A_.activation(rs[:], psum[:, S[0], 0:T], ACT.Ln, scale=1.0 / D, bias=c_("eps")))
                A_.activation(rs[:], rs[:], ACT.Exp, scale=-0.5).then_inc(rs_ready, 1)
                for n in range(2 * NBLK):
                    if n not in BY_DVE:
                        sc.wait_ge(hr_tr, n + 1)
                        A_.activation(y_rows[:, n % NBLK, (n // NBLK) * SLAB:(n // NBLK + 1) * SLAB], psum[:, n % 4, :], ACT.Copy).then_inc(rows_act, 1)

            @block.vector
            def _(dve):
                sum_squares(dve, 0)
                dve.wait_ge(rs_ready, 1)
                for k in range(KD):
                    V.scalar_tensor_tensor(out=xT[:, k, :], in0=xT[:, k, :], scalar=final_gain[:, k:k + 1], in1=rs[:],
                                           op0=ALU.mult, op1=ALU.mult).then_inc(h_ready, 1)
                for n in BY_DVE:
                    dve.wait_ge(hr_tr, n + 1)
                    V.tensor_copy(y_rows[:, n % NBLK, (n // NBLK) * SLAB:(n // NBLK + 1) * SLAB], psum[:, n % 4, :]).then_inc(rows_dve, 1)

            @block.tensor
            def _(pe):
                pe.wait_ge(sq_used, KD)
                M.matmul(psum[:, S[0], 0:T], ones, sum_sq, start=True, stop=True).then_inc(nsum, 1)
                for n in range(2 * NBLK):
                    half, b = divmod(n, NBLK)
                    if b == 0:
                        pe.wait_ge(h_ready, 4 * (half + 1))
                    if n == 0:
                        pe.wait_ge(rs_ready, 1)
                    if n >= 4:
                        wait_copied(pe, n - 4)
                    for j in range(4):
                        last = transpose(psum[:, n % 4, j * P:(j + 1) * P], xT[:, half * 4 + j, b * P:(b + 1) * P])
                    last.then_inc(hr_tr, 1)


_OUTS = [("y_prompt", (1, P, D)), ("y_sample", (1, T - P, D)), ("new_a_k", (1, DEPTH, P, HEADS_A, 2, 64)),
         ("new_a_v", (1, DEPTH, P, HEADS_A, 128)), ("new_b_k", (1, DEPTH, P, HEADS_B, 64)),
         ("new_b_v", (1, DEPTH, P, HEADS_B, 64)), ("new_c_fwd", (1, DEPTH, HEADS_C, 64, 128)),
         ("new_c_bwd", (1, DEPTH, HEADS_C, 64, 128))]


def kernel(**inputs):
    import numpy as _np
    import concourse.bacc as _bacc
    from concourse import mybir as _mybir
    from concourse.bass_utils import run_bass_kernel_spmd as _run

    a = {k: _np.asarray(v) for k, v in inputs.items()}
    table, per_layer = shape_constants()
    feeds = [
        ("x", _np.concatenate([a["x_prompt"][0], a["x_sample"][0]], axis=0)),
        ("cvec", _np.stack([a["c_ctx"], a["c"][0]])),
        ("cache_k", _np.concatenate([a["cache_a_k"][0].reshape(DEPTH, P, 512), a["cache_b_k"][0].reshape(DEPTH, P, 512)], axis=2)),
        ("cache_v", _np.concatenate([a["cache_a_v"][0].reshape(DEPTH, P, 512), a["cache_b_v"][0].reshape(DEPTH, P, 512)], axis=2)),
        ("state_f", a["state_c_fwd"][0]),
        ("state_b", a["state_c_bwd"][0]),
        ("w_mod", a["w_mod"]),
        ("layer_vectors", _np.concatenate([a[n].reshape(DEPTH, -1, P) for n in
                                           ("b_mod", "norm_mix", "norm_ffn", "diff_norm", "ret_norm")], axis=1)),
        ("layer_scalars", _np.concatenate([a["diff_lambda"].reshape(DEPTH, 256), a["ret_decay"].reshape(DEPTH, 8), per_layer], axis=1)),
        ("w_in", a["w_in"]),
        ("rpb_rev", a["na_rpb"].transpose(0, 2, 1, 3)[..., ::-1]),
        ("w_pa", a["w_proj_a"]), ("w_pb", a["w_proj_b"]),
        ("w_pc", a["w_proj_c"]), ("w_out", a["w_out"]), ("w_router", a["w_router"]), ("w_gate", a["w_exp_gate"]),
        ("w_up", a["w_exp_up"]), ("w_down", a["w_exp_down"]), ("norm_final", a["norm_final"]),
        ("const", table),
    ]
    nc = _bacc.Bacc("TRN2", target_bir_lowering=False, num_devices=1)
    arrays, args = {}, []
    for name, value in feeds:
        value = _np.ascontiguousarray(value)
        arrays[f"in_{name}"] = value
        args.append(nc.dram_tensor(f"in_{name}", value.shape, _mybir.dt.from_np(value.dtype), kind="ExternalInput").ap())
    shapes = [("y", (T, D)), ("ak", (DEPTH, P, 512)), ("av", (DEPTH, P, 512)), ("bk", (DEPTH, P, 512)),
              ("bv", (DEPTH, P, 512)), ("sf", (DEPTH, HEADS_C, 64, P)), ("sb", (DEPTH, HEADS_C, 64, P))]
    for name, shape in shapes:
        args.append(nc.dram_tensor(f"out_{name}", shape, _mybir.dt.float32, kind="ExternalOutput").ap())
    build(nc, *args)
    r = _run(nc, [arrays], core_ids=[0]).results[0]
    y = r["out_y"]
    rest = [r[f"out_{name}"].reshape(shape) for (name, _), (_, shape) in zip(shapes[1:], _OUTS[2:])]
    return (y[0:P].reshape(_OUTS[0][1]), y[P:T].reshape(_OUTS[1][1]), *rest)
```
